# Optimizing a Trainium2 kernel written in Bass

```python
import math
import jax, jax.numpy as jnp
from jax import lax
import numpy as np

D_MODEL = 1024
BATCH = 1
SEQ = 1024
DEPTH = 1

CTX_LEN = 256
GRID_W = 64
CHUNK = 128
RET_HEADS = 4
RET_QK_DIM = 128
RET_V_DIM = 128
RET_WIDTH = RET_HEADS * RET_V_DIM
GMLP_GROUPS = 4
GMLP_GROUP_DIM = 128
GMLP_WIDTH = GMLP_GROUPS * GMLP_GROUP_DIM
MIX_WIDTH = RET_WIDTH + GMLP_WIDTH
IN_COLS = 4 * RET_WIDTH + 2 * GMLP_WIDTH
D_FF = 2816
N_MOD = 9
ROPE_BASE = 10000.0
EPS = 1e-6

kernel_name = "hybrid_retention_gmlp_macaron_dit"

def rmsnorm(x, g):
    xf = x.astype(jnp.float32)
    y = xf * lax.rsqrt(jnp.mean(xf * xf, axis=-1, keepdims=True) + EPS)
    return (y * g.astype(jnp.float32)).astype(x.dtype)

def modulate(h, shift, scale):
    return h * (1 + scale) + shift

def swiglu(h, w1, w2):
    gate, up = jnp.split(h @ w1, 2, axis=-1)
    return (jax.nn.silu(gate) * up) @ w2

def to_heads(t, n_heads):
    b, n, _ = t.shape
    return t.reshape(b, n, n_heads, -1).transpose(0, 2, 1, 3)

def rope_2d(t, row, col):
    half = t.shape[-1] // 2
    n_freq = half // 2
    freqs = ROPE_BASE ** (-jnp.arange(n_freq, dtype=jnp.float32) / n_freq)
    ang = jnp.concatenate([row[:, None] * freqs, col[:, None] * freqs], axis=-1)
    cos, sin = jnp.cos(ang), jnp.sin(ang)
    t1, t2 = t[..., :half], t[..., half:]
    return jnp.concatenate([t1 * cos - t2 * sin, t1 * sin + t2 * cos], axis=-1)

def retention_scan(q, k, v, log_gamma, s0):
    b, h, n, dk = q.shape
    dv = v.shape[-1]
    nc = n // CHUNK
    idx = jnp.arange(CHUNK, dtype=jnp.float32)
    diff = idx[:, None] - idx[None, :]
    lower = diff >= 0
    dmask = jnp.where(lower[None], jnp.exp(jnp.where(lower, diff, 0.0)[None] * log_gamma[:, None, None]), 0.0)
    xi = jnp.exp((idx + 1.0)[None] * log_gamma[:, None])
    zeta = jnp.exp((CHUNK - 1.0 - idx)[None] * log_gamma[:, None])
    chunk_decay = jnp.exp(CHUNK * log_gamma)

    def to_chunks(t):
        return t.reshape(b, h, nc, CHUNK, -1).transpose(2, 0, 1, 3, 4)

    def step(s, qkv):
        qc, kc, vc = qkv
        scores = jnp.einsum('bhid,bhjd->bhij', qc, kc) * dmask
        o = (jnp.einsum('bhij,bhjv->bhiv', scores, vc)
             + jnp.einsum('bhid,bhdv->bhiv', qc * xi[:, :, None], s))
        s_new = chunk_decay[:, None, None] * s + jnp.einsum('bhjd,bhjv->bhdv', kc * zeta[:, :, None], vc)
        return s_new, o

    s_fin, o = lax.scan(step, s0, (to_chunks(q), to_chunks(k), to_chunks(v)))
    o = o.transpose(1, 2, 0, 3, 4).reshape(b, h, n, dv)
    return o, s_fin

def bidir_retention(q, k, v, lg_fwd, lg_bwd, s0_fwd, s0_bwd):
    flip = lambda t: t[:, :, ::-1]
    o_f, s_f = retention_scan(q, k, v, lg_fwd, s0_fwd)
    o_b, s_b = retention_scan(flip(q), flip(k), flip(v), lg_bwd, s0_bwd)
    return o_f + flip(o_b), s_f, s_b

def retention_readout(y, gate):
    y = y * lax.rsqrt(jnp.mean(y * y, axis=-1, keepdims=True) + EPS)
    b, h, n, dv = y.shape
    y = y.transpose(0, 2, 1, 3).reshape(b, n, h * dv).astype(gate.dtype)
    return y * jax.nn.silu(gate)

def chunk_gmlp(u, v, w_s, b_s):
    b, n, _ = u.shape
    nc = n // CHUNK
    vg = v.reshape(b, nc, CHUNK, GMLP_GROUPS, GMLP_GROUP_DIM).astype(jnp.float32)
    mu = jnp.mean(vg, axis=-1, keepdims=True)
    var = jnp.mean(jnp.square(vg - mu), axis=-1, keepdims=True)
    vn = ((vg - mu) * lax.rsqrt(var + EPS)).astype(u.dtype)
    mixed = jnp.einsum('gpq,bcqgd->bcpgd', w_s, vn) + b_s.T[None, None, :, :, None]
    ug = u.reshape(b, nc, CHUNK, GMLP_GROUPS, GMLP_GROUP_DIM)
    return (ug * mixed).reshape(b, n, GMLP_WIDTH)

def split_proj(p):
    r, g = RET_WIDTH, GMLP_WIDTH
    return jnp.split(p, [r, 2 * r, 3 * r, 4 * r, 4 * r + g], axis=-1)

def setup_inputs(seed: int = 0) -> dict:
    key = jax.random.key(seed)
    ks = jax.random.split(key, 20)
    f32 = jnp.float32
    nrm = lambda k, s, sc: jax.random.normal(k, s, f32) * sc
    base_rate = np.log(-np.log(1.0 - 2.0 ** (-5.0 - np.arange(RET_HEADS)))).astype(np.float32)
    ret_decay = jnp.asarray(base_rate)[None, None, :] + nrm(ks[12], (DEPTH, 2, RET_HEADS), 0.05)
    return {
        "x": nrm(ks[0], (BATCH, SEQ, D_MODEL), 1.0),
        "c": nrm(ks[1], (BATCH, D_MODEL), 1.0),
        "ctx": nrm(ks[2], (BATCH, CTX_LEN, D_MODEL), 1.0),
        "c_ctx": nrm(ks[3], (D_MODEL,), 1.0),
        "w_ada": nrm(ks[4], (DEPTH, D_MODEL, N_MOD * D_MODEL), 0.02),
        "b_ada": nrm(ks[5], (DEPTH, N_MOD * D_MODEL), 0.02),
        "norm_g": 1.0 + nrm(ks[6], (DEPTH, 3, D_MODEL), 0.02),
        "ffn1_w1": nrm(ks[7], (DEPTH, D_MODEL, 2 * D_FF), D_MODEL ** -0.5),
        "ffn1_w2": nrm(ks[8], (DEPTH, D_FF, D_MODEL), D_FF ** -0.5),
        "w_in": nrm(ks[9], (DEPTH, D_MODEL, IN_COLS), D_MODEL ** -0.5),
        "ret_decay": ret_decay,
        "gmlp_ws": nrm(ks[10], (DEPTH, GMLP_GROUPS, CHUNK, CHUNK), 0.5 * CHUNK ** -0.5),
        "gmlp_bs": 1.0 + nrm(ks[11], (DEPTH, GMLP_GROUPS, CHUNK), 0.02),
        "w_out": nrm(ks[13], (DEPTH, MIX_WIDTH, D_MODEL), MIX_WIDTH ** -0.5),
        "ffn2_w1": nrm(ks[14], (DEPTH, D_MODEL, 2 * D_FF), D_MODEL ** -0.5),
        "ffn2_w2": nrm(ks[15], (DEPTH, D_FF, D_MODEL), D_FF ** -0.5),
        "final_g": 1.0 + nrm(ks[16], (D_MODEL,), 0.02),
    }

def reference(x, c, ctx, c_ctx, w_ada, b_ada, norm_g, ffn1_w1, ffn1_w2, w_in, ret_decay,
              gmlp_ws, gmlp_bs, w_out, ffn2_w1, ffn2_w2, final_g):
    b, n, _ = x.shape
    rows = n // GRID_W
    row = jnp.repeat(jnp.arange(rows, dtype=jnp.float32), GRID_W)
    col = jnp.tile(jnp.arange(GRID_W, dtype=jnp.float32), rows)
    k_scale = RET_QK_DIM ** -0.5

    for l in range(DEPTH):
        last = l == DEPTH - 1
        m_x = [t[:, None, :] for t in jnp.split(jax.nn.silu(c) @ w_ada[l] + b_ada[l], N_MOD, axis=-1)]
        m_c = [t[None, None, :] for t in jnp.split(jax.nn.silu(c_ctx) @ w_ada[l] + b_ada[l], N_MOD, axis=-1)]

        x = x + 0.5 * m_x[2] * swiglu(modulate(rmsnorm(x, norm_g[l, 0]), m_x[0], m_x[1]), ffn1_w1[l], ffn1_w2[l])
        ctx = ctx + 0.5 * m_c[2] * swiglu(modulate(rmsnorm(ctx, norm_g[l, 0]), m_c[0], m_c[1]), ffn1_w1[l], ffn1_w2[l])

        px = modulate(rmsnorm(x, norm_g[l, 1]), m_x[3], m_x[4]) @ w_in[l]
        pc = modulate(rmsnorm(ctx, norm_g[l, 1]), m_c[3], m_c[4]) @ w_in[l]
        qx, kx, vx, gx, ux, vgx = split_proj(px)
        qc, kc, vc, gc, uc, vgc = split_proj(pc)

        lg_fwd = -jnp.exp(ret_decay[l, 0].astype(jnp.float32))
        lg_bwd = -jnp.exp(ret_decay[l, 1].astype(jnp.float32))

        qch = to_heads(qc, RET_HEADS).astype(jnp.float32)
        kch = to_heads(kc, RET_HEADS).astype(jnp.float32) * k_scale
        vch = to_heads(vc, RET_HEADS).astype(jnp.float32)
        s_zero = jnp.zeros((b, RET_HEADS, RET_QK_DIM, RET_V_DIM), jnp.float32)
        yc, s_fwd_c, s_bwd_c = bidir_retention(qch, kch, vch, lg_fwd, lg_bwd, s_zero, s_zero)

        qxh = rope_2d(to_heads(qx, RET_HEADS).astype(jnp.float32), row, col)
        kxh = rope_2d(to_heads(kx, RET_HEADS).astype(jnp.float32), row, col) * k_scale
        vxh = to_heads(vx, RET_HEADS).astype(jnp.float32)
        yx, _, _ = bidir_retention(qxh, kxh, vxh, lg_fwd, lg_bwd, s_fwd_c, s_bwd_c)
        ret_x = retention_readout(yx, gx)

        gm_x = chunk_gmlp(jax.nn.gelu(ux), jax.nn.gelu(vgx), gmlp_ws[l], gmlp_bs[l])

        x = x + m_x[5] * (jnp.concatenate([ret_x, gm_x], axis=-1) @ w_out[l])
        if not last:
            ret_c = retention_readout(yc, gc)
            gm_c = chunk_gmlp(jax.nn.gelu(uc), jax.nn.gelu(vgc), gmlp_ws[l], gmlp_bs[l])
            ctx = ctx + m_c[5] * (jnp.concatenate([ret_c, gm_c], axis=-1) @ w_out[l])

        x = x + 0.5 * m_x[8] * swiglu(modulate(rmsnorm(x, norm_g[l, 2]), m_x[6], m_x[7]), ffn2_w1[l], ffn2_w2[l])
        if not last:
            ctx = ctx + 0.5 * m_c[8] * swiglu(modulate(rmsnorm(ctx, norm_g[l, 2]), m_c[6], m_c[7]), ffn2_w1[l], ffn2_w2[l])

    return rmsnorm(x, final_g)


_drawn_inputs = setup_inputs


def setup_inputs(seed=0):
    import zlib

    import numpy as np

    out = dict(_drawn_inputs(seed))
    spreads = {}
    factors = {}
    for name, (base, spread) in spreads.items():
        noise = np.random.default_rng([zlib.crc32(name.encode()), seed]).standard_normal(out[name].shape)
        drawn = base * np.exp(spread * noise) if base else spread * noise
        out[name] = __import__('jax').numpy.asarray(drawn.astype(out[name].dtype))
    for name, factor in factors.items():
        out[name] = (out[name] * factor).astype(out[name].dtype)
    return out
```

```python
from contextlib import ExitStack

import numpy as np

import concourse.bass as bass
from concourse import mybir

ALU = mybir.AluOpType
ACT = mybir.ActivationFunctionType
F32 = mybir.dt.float32
F32R = mybir.dt.float32r

P = 128
D = 1024
KT = D // P
SEQ, CTX = 1024, 256
FF = 2816
NF = FF // P
HEADS, GROUPS = 4, 4
CHUNK = 128
NCH = SEQ // CHUNK
NMOD = 9
TB = 512
EPS = 1e-6
K_SCALE = float(P) ** -0.5
GRID_W = 64

UC = 256
N_ADA = NMOD * D // UC
ADA_FIRST = 14
NIT = NF // 2
U_FFN1 = ADA_FIRST
U_MIX = U_FFN1 + 4 * NIT
WIN = {"q": 0, "k": 2, "v": 4, "g": 6, "u": 8, "vg": 10}
MIX_UNITS = ([("ctx", "k", 0), ("ctx", "k", 1), ("ctx", "v", 0), ("ctx", "v", 1)]
             + [("lat", a, p) for p in range(2) for a in ("k", "q", "v")]
             + [("lat", "g", 0), ("lat", "g", 1)]
             + [("lat", a, p) for p in range(2) for a in ("vg", "u")]
             + [("out", tb, p) for tb in range(2) for p in range(4)])
U_FFN2 = U_MIX + len(MIX_UNITS)
N_UNITS = U_FFN2 + 2 * NIT

C_ABS, C_LOW, C_UP, C_XIF, C_XIB, C_IDX, C_END = 0, 128, 256, 384, 512, 640, 648

BLOCKS = [(1, 0, CTX), (0, 0, TB), (0, TB, TB)]
NRING = 6


def mixer_fills():
    fills = []
    for i, (kind, a, p) in enumerate(MIX_UNITS):
        if kind == "ctx":
            fills.append((i, "c" + a, p, 0, 0))
            if i == 3:
                fills += [(i, "state0", d, 0, 0) for d in range(2)]
        elif kind == "out":
            fills += [(i, "out", a, 2 * p + t, 0) for t in range(2)]
        elif a in ("k", "q", "g", "u"):
            for t in range(2):
                for tb in range(2):
                    if a == "u":
                        fills.append((i, "mixed", 2 * p + t, tb, 0))
                    fills.append((i, a, 2 * p + t, tb, 0))
        else:
            fills += [(i, a, p, j, 0) for j in range(4)]
            if a == "v":
                for h in (2 * p, 2 * p + 1):
                    for name in ("kt", "score", "uf", "ub", "o"):
                        fills += [(i, name, h, j, 0) for j in range(2)]
                    fills.append((i, "ysum", h, 0, 0))
                    fills += [(i, "yscale", h, j, 0) for j in range(2)]
    return fills


FILLS = mixer_fills()
FILL = {(name, a, b): n for n, (_, name, a, b, _) in enumerate(FILLS)}
LAST_FILL = {i: max(n for n, f in enumerate(FILLS) if f[0] == i and f[1] in (MIX_UNITS[i][1], "c" + str(MIX_UNITS[i][1]), "out"))
             for i in range(len(MIX_UNITS))}


def layer(nc, x, ctx, c2, w_units, w2_units, b_ada, norm_g, final_g, decay, ws, bs, cosine, sine, consts, ident, sel, out):
    stack = ExitStack()
    with stack:
        def at(name, shape, dt, offset):
            return nc.alloc_sbuf_tensor_at(name, shape, dt, offset=offset)

        top = [192]

        def keep(name, shape, dt):
            n = 4 * int(np.prod(shape[1:]))
            n += -n % 32
            top[0] += n
            return at(name, shape, dt, top[0] - n)

        X = keep("X", [P, KT, SEQ], F32)
        HH = keep("HH", [P, KT, SEQ], F32R)
        HL = keep("HL", [P, KT, SEQ], F32R)
        WR = keep("WR", [P, 2, KT, UC], F32)
        WH = keep("WH", [P, 2, KT, UC], F32R)
        WL = keep("WL", [P, 2, KT, UC], F32R)
        MODS = keep("MODS", [P, NMOD * KT, 2], F32)
        BA = keep("BA", [P, NMOD * KT, 2], F32)
        GAIN = keep("GAIN", [P, 3, KT, 2], F32)
        GATE = keep("GATE", [P, 3, KT, 2], F32)
        NG = keep("NG", [P, 3, KT], F32)
        FG = keep("FG", [P, KT], F32)
        ID = keep("ID", [P, P], F32)
        ONES = keep("ONES", [P, P], F32)
        SEL = keep("SEL", [4, 2], F32)
        MS = keep("MS", [P, 32], F32)
        RS = keep("RS", [P, 32], F32)
        NEGH = keep("NEGH", [P, 32], F32)
        LG = keep("LG", [P, 8], F32)
        DEC = keep("DEC", [P, 8], F32)
        ZL = keep("ZL", [P, 8], F32)
        ZC = keep("ZC", [P, 2, 8], F32)
        R = top[0]

        XC = at("XC", [P, KT, CTX], F32, R)
        HCH = at("HCH", [P, KT, CTX], F32R, R + 8192)
        HCL = at("HCL", [P, KT, CTX], F32R, R + 16384)
        NTOK = SEQ + CTX
        PH1 = at("PH1", [P, 2, NTOK], F32R, R + 24576)
        PL1 = at("PL1", [P, 2, NTOK], F32R, R + 34816)
        W2R1 = at("W2R1", [P, D], F32, R + 45056)
        W2H1 = at("W2H1", [P, 2, D], F32R, R + 49152)
        W2L1 = at("W2L1", [P, 2, D], F32R, R + 57344)
        SG = at("SG", [P, 2, TB], F32, R + 65536)
        PR = at("PR", [P, 2, TB], F32, R + 69632)
        A4 = at("A4", [4, 2, UC], F32, R + 73728)
        CV = at("CV", [P, 160], F32R, R + 75776)
        CIN = at("CIN", [P, KT, 2], F32, R + 76416)
        CS = at("CS", [P, KT, 2], F32, R + 76480)
        SQ = at("SQ", [P, 2, TB], F32, R + 24576)
        ACC = at("ACC", [P, TB], F32, R + 28672)
        HF = at("HF", [P, 2, TB], F32, R + 30720)
        DG = at("DG", [P, 4, P], F32, R + 34816)
        KF = at("KF", [P, 2, SEQ], F32, R)
        QF = at("QF", [P, 2, SEQ], F32, R + 8192)
        V = at("V", [P, NCH, UC], F32, R + 16384)
        KZ = [at(f"KZ{d}", [P, NCH, P], F32, R + 24576 + 4096 * d) for d in range(2)]
        PM = at("PM", [P, NCH, P], F32, R + 32768)
        XI = at("XI", [P, 8, P], F32, R + 36864)
        RET = at("RET", [P, HEADS, SEQ], F32, R + 40960)
        KC = at("KC", [P, 2, 2, HEADS, P], F32, R + 40960)
        VC = at("VC", [P, 2, HEADS * P], F32, R + 49152)
        CST = at("CST", [P, C_END], F32, R + 53248)
        DT = at("DT", [P, 2, P], F32, R + 55872)
        COS = at("COS", [P, SEQ], F32, R + 57344)
        SIN = at("SIN", [P, SEQ], F32, R + 61440)
        DM = at("DM", [P, HEADS, P], F32, R + 65536)
        TMP = at("TMP", [P, 2, TB], F32, R + 69632)
        S0 = at("S0", [P, 2, HEADS, P], F32, R + 73728)
        GM = at("GM", [P, GROUPS, SEQ], F32, R)
        MIXD = at("MIXD", [P, 2, TB], F32, R + 24576)
        GU = at("GU", [P, 2, TB], F32, R + 28672)
        WST = at("WST", [P, GROUPS, P], F32, R + 32768)
        BB = at("BB", [P, GROUPS, P], F32, R + 34816)
        BST = at("BST", [P, 16, 6], F32, R + 67584)
        MV = at("MV", [P, 16, 2], F32, R + 67584 + 384)
        PH2 = at("PH2", [P, 2, SEQ], F32R, R)
        PL2 = at("PL2", [P, 2, SEQ], F32R, R + 8192)
        W2R2 = at("W2R2", [P, D], F32, R + 40960)
        W2H2 = at("W2H2", [P, 2, D], F32R, R + 45056)
        W2L2 = at("W2L2", [P, 2, D], F32R, R + 53248)
        OUT = [at(f"OUT{b}", [P, KT, TB], F32, o) for b, o in enumerate((R, R + 40960))]

        PS = [stack.enter_context(nc.psum_tensor(f"PS{b}", [P, 512], F32)) for b in range(8)]
        ST_BANK, RB_BANK = PS[6], PS[7]

        sem = lambda name: stack.enter_context(nc.semaphore(name))
        s_const = sem("const_loaded")
        s_cst = sem("decay_consts_loaded")
        s_rope = sem("rope_loaded")
        s_gw = sem("gmlp_weights_loaded")
        s_x = [sem(f"x_loaded{b}") for b in range(3)]
        s_raw = [sem(f"unit_loaded{s}") for s in range(2)]
        s_hi = sem("unit_high_done")
        s_lo = [sem(f"unit_low_done{s}") for s in range(2)]
        s_w2raw = sem("w2_loaded")
        s_w2hi = sem("w2_high_done")
        s_w2lo = sem("w2_low_done")
        s_set = sem("constants_set")
        s_cv = sem("silu_c_ready")
        s_ada = sem("ada_product_ready")
        s_a4 = sem("ada_rows_copied")
        s_col = sem("ada_columns_ready")
        s_mods = sem("mods_done")
        s_coef = sem("coefficients_ready")
        s_lg = sem("log_decay_ready")
        s_sq = sem("squares_done")
        s_acc = sem("squares_added")
        s_st = sem("norm_sum_ready")
        s_ms = sem("norm_mean_ready")
        s_rs = sem("norm_rsqrt_ready")
        s_dg = sem("norm_diagonal_ready")
        s_rb = sem("norm_scale_ready")
        s_hf = sem("modulated_done")
        s_hh = sem("modulated_high_done")
        s_hl = sem("modulated_low_done")
        s_gu = sem("gate_up_ready")
        s_silu = sem("silu_done")
        s_prod = sem("product_done")
        s_ph = sem("product_high_done")
        s_pl = sem("product_low_done")
        s_y = sem("down_ready")
        s_yd = sem("down_added")
        s_fill = sem("fill_ready")
        s_free = [sem(f"bank_free{b}") for b in range(NRING)]
        s_exp = sem("exp_done")
        s_dec = sem("decay_tables_ready")
        s_rope_done = sem("rope_done")
        s_kz = sem("decayed_keys_ready")
        s_state = sem("states_ready")
        s_q = sem("decayed_queries_ready")
        s_oc = sem("retention_copied")
        s_ym = sem("retention_mean_ready")
        s_yr = sem("retention_rsqrt_ready")
        s_yg = sem("retention_diagonal_ready")
        s_lv = sem("gmlp_variance_ready")
        s_lr = sem("gmlp_rsqrt_ready")
        s_vn = sem("gmlp_v_normed")
        s_mx = sem("gmlp_mixed_added")
        s_cat = sem("mixer_input_ready")
        s_cath = sem("mixer_high_done")
        s_catl = sem("mixer_low_done")
        s_chain = sem("vector_chain")
        s_out = sem("stored")

        def release(n):
            _, name, a, b, _ = FILLS[n]
            if name == "uf":
                return s_state, 14 * a + (7 if b == 0 else 13)
            if name == "ub":
                return s_state, 14 * a + (8 if b == 1 else 14)
            if name == "ysum":
                return s_ym, a + 1
            if name == "mixed":
                return s_mx, 2 * a + b + 1
            return s_free[n % NRING], sum(FILLS[m][1] not in ("uf", "ub", "ysum", "mixed")
                                          for m in range(n % NRING, n + 1, NRING))

        NORMS = [(0, b) for b in range(3)] + [(1, b) for b in range(3)] + [(2, 1), (2, 2), (3, 1), (3, 2)]
        J = {key: j for j, key in enumerate(NORMS)}
        FFN = [dict(T=3, blocks=BLOCKS, step=0, y=0, v=0, unit=U_FFN1, per=4),
               dict(T=2, blocks=BLOCKS[1:], step=6 * NIT, y=24 * NIT, v=2 * NIT, unit=U_FFN2, per=2)]
        y_all = [24 * NIT + 2, 40 * NIT + 2]

        def tokens(t, b):
            _, t0, n = BLOCKS[b]
            return lambda k: t[:, k, t0:t0 + n]

        def streams(b):
            return (XC, HCH, HCL) if b == 0 else (X, HH, HL)

        block = stack.enter_context(nc.Block())

        @block.sync
        def _(sp):
            for dst, src in ((CIN[:, :, :], c2), (BA[:, :, :], b_ada), (NG[:, :, :], norm_g),
                             (FG[:, :], final_g), (ID[:, :], ident), (SEL[:, :], sel), (LG[:, :], decay)):
                sp.dma_start(dst, src).then_inc(s_const, 16)

            def unit(u, slot):
                sp.dma_start(WR[:, slot], w_units[u]).then_inc(s_raw[slot], 16)

            unit(0, 0)
            sp.dma_start(XC[:, :, :], ctx.rearrange("(k p) t -> p k t", p=P)).then_inc(s_x[0], 16)
            unit(1, 1)
            for b in (1, 2):
                _, t0, n = BLOCKS[b]
                sp.dma_start(X[:, :, t0:t0 + n],
                             x.rearrange("(k p) t -> p k t", p=P)[:, :, t0:t0 + n]).then_inc(s_x[b], 16)
            for u in range(2, U_FFN1 + 2):
                sp.wait_ge(s_lo[u % 2], u // 2)
                unit(u, u % 2)

            def ffn(f, it, w2r, prefetch):
                for j in range(2):
                    sp.wait_ge(s_w2lo, f["v"] + 2 * it + j + 1)
                    sp.dma_start(w2r[:, :], w2_units[f["v"] + 2 * it + j]).then_inc(s_w2raw, 16)
                for j in range(f["per"] if prefetch else 0):
                    u = f["unit"] + f["per"] * it + 2 + j
                    sp.wait_ge(s_lo[j % 2], (f["unit"] + j - j % 2) // 2 + (f["per"] // 2) * it + 1)
                    unit(u, j % 2)

            with sp.Fori(0, NIT) as it:
                ffn(FFN[0], it, W2R1, True)
            sp.wait_ge(s_yd, y_all[0])
            sp.dma_start(CST[:, :], consts).then_inc(s_cst, 16)
            sp.dma_start(COS[:, :], cosine).then_inc(s_rope, 16)
            sp.dma_start(SIN[:, :], sine).then_inc(s_rope, 16)
            for u in range(U_MIX + 2, U_FFN2 + 2):
                sp.wait_ge(s_lo[u % 2], u // 2)
                unit(u, u % 2)
                if u - U_MIX == 12:
                    sp.wait_ge(s_fill, FILL["yscale", HEADS - 1, 1] + 1)
                    sp.dma_start(WST[:, :, :], ws).then_inc(s_gw, 16)
                    sp.dma_start(BB[:, :, :], bs).then_inc(s_gw, 16)
            sp.wait_ge(s_catl, 16)
            with sp.Fori(0, NIT - 1) as it:
                ffn(FFN[1], it, W2R2, True)
            ffn(FFN[1], NIT - 1, W2R2, False)
            for b in range(2):
                for k in range(0, KT, 2):
                    sp.wait_ge(s_hf, 8 * J[3, b + 1] + k + 2)
                    sp.dma_start(out.rearrange("(k p) t -> p k t", p=P)[:, k:k + 2, b * TB:(b + 1) * TB],
                                 OUT[b][:, k:k + 2, :]).then_inc(s_out, 16)
            sp.wait_ge(s_out, 16 * KT)

        @block.gpsimd
        def _(pool):
            pool.memset(NEGH[:, :], -0.5).then_inc(s_w2lo, 1)

            def low(slot, count):
                pool.wait_ge(s_hi, count)
                pool.tensor_tensor(WL[:, slot], WR[:, slot], WH[:, slot].bitcast(F32),
                                   ALU.subtract).then_inc(s_lo[slot], 1)

            def power(dst, src, ready, count, done):
                pool.wait_ge(ready, count)
                n = src.shape[-1]
                pool.tensor_tensor(dst, src, NEGH[:, 0:n], ALU.pow).then_inc(done, 1)

            def norm_rsqrt(j, n):
                power(RS[:, 0:n // P], MS[:, 0:n // P], s_ms, j + 1, s_rs)

            def norm_low(place, b):
                n, (_, hh, hl) = BLOCKS[b][2], streams(b)
                j = J[place, b]
                for k in range(KT):
                    pool.wait_ge(s_hh, 8 * j + k + 1)
                    pool.tensor_tensor(tokens(hl, b)(k), HF[:, k % 2, 0:n], tokens(hh, b)(k).bitcast(F32),
                                       ALU.subtract).then_inc(s_hl, 1)

            pool.wait_ge(s_w2lo, 1)
            for b in range(2):
                norm_rsqrt(J[0, b], BLOCKS[b][2])
                low(0, 2 * b + 1)
            low(0, 5)
            low(0, 7)
            norm_low(0, 0)
            norm_rsqrt(J[0, 2], BLOCKS[2][2])
            low(0, 9)
            norm_low(0, 1)
            low(0, 11)
            norm_low(0, 2)
            low(0, 13)
            low(0, U_FFN1 + 1)
            low(1, U_FFN1 + 2)

            def ffn(f, it, w2r, w2h, w2l, prefetch):
                for j in range(2):
                    pool.wait_ge(s_w2hi, f["v"] + 2 * it + j + 1)
                    pool.tensor_tensor(w2l[:, j], w2r[:, :], w2h[:, j].bitcast(F32),
                                       ALU.subtract).then_inc(s_w2lo, 1)
                for j in range(f["per"] if prefetch else 0):
                    low(j % 2, f["unit"] + f["per"] * it + 3 + j)

            with pool.Fori(0, NIT) as it:
                ffn(FFN[0], it, W2R1, W2H1, W2L1, True)
            for b in range(3):
                norm_rsqrt(J[1, b], BLOCKS[b][2])
                if b:
                    low((b + 1) % 2, U_MIX + b + 2)
                norm_low(1, b)
            for i, (kind, a, p) in enumerate(MIX_UNITS):
                if i >= 3:
                    low((i + 1) % 2, U_MIX + i + 2)
                if kind == "lat" and a == "v":
                    for hh in range(2):
                        h = 2 * p + hh
                        pool.wait_ge(s_fill, FILL["score", h, 1] + 1)
                        pool.wait_ge(s_exp, 9)
                        for d in (0, 1):
                            q = QF[:, hh, :].rearrange("p (c t) -> p c t", c=NCH)
                            dst = RET[:, h, :].rearrange("p (c t) -> p c t", c=NCH) if d == 0 else q
                            if d == 1:
                                pool.wait_ge(s_q, 2 * h + 1)
                            pool.tensor_tensor(dst, q, XI[:, 4 * d + h, :].unsqueeze(1).to_broadcast([P, NCH, P]),
                                               ALU.mult).then_inc(s_q, 1)
                        power(RS[:, 8:16], MS[:, 8:16], s_ym, h + 1, s_yr)
                if kind == "lat" and a == "vg":
                    power(RS[:, 16:32], MS[:, 16:32], s_lv, p + 1, s_lr)
                if kind == "lat" and a == "u" and p == 1:
                    for n in range(16):
                        k, tb = n % 8, n // 8
                        pool.wait_ge(s_cath, n + 1)
                        t0 = tb * TB
                        src = RET[:, k, t0:t0 + TB] if k < 4 else GM[:, k - 4, t0:t0 + TB]
                        pool.tensor_tensor(HL[:, k, t0:t0 + TB], src, HH[:, k, t0:t0 + TB].bitcast(F32),
                                           ALU.subtract).then_inc(s_catl, 1)
                if (kind, a, p) == ("out", 1, 0):
                    norm_rsqrt(J[2, 1], TB)
                if (kind, a, p) == ("out", 1, 1):
                    norm_low(2, 1)
            low(1, U_FFN2 + 2)
            norm_rsqrt(J[2, 2], TB)
            norm_low(2, 2)
            with pool.Fori(0, NIT - 1) as it:
                ffn(FFN[1], it, W2R2, W2H2, W2L2, True)
            ffn(FFN[1], NIT - 1, W2R2, W2H2, W2L2, False)
            for b in (1, 2):
                norm_rsqrt(J[3, b], TB)

        @block.scalar
        def _(act):
            def high(slot, raw_count):
                act.wait_ge(s_raw[slot], raw_count)
                act.activation(WH[:, slot], WR[:, slot], ACT.Copy).then_inc(s_hi, 1)

            def squares(place, b):
                n, (xs, _, _) = BLOCKS[b][2], streams(b)
                j = J[place, b]
                for k in range(KT):
                    if 8 * j + k >= 2:
                        act.wait_ge(s_acc, 8 * j + k - 1)
                    act.activation(SQ[:, k % 2, 0:n], tokens(xs, b)(k), ACT.Square).then_inc(s_sq, 1)

            def norm_high(place, b):
                n, (_, hh, _) = BLOCKS[b][2], streams(b)
                j = J[place, b]
                for k in range(KT):
                    act.wait_ge(s_hf, 8 * j + k + 1)
                    act.activation(tokens(hh, b)(k), HF[:, k % 2, 0:n], ACT.Copy).then_inc(s_hh, 1)

            act.wait_ge(s_const, 16 * 7)
            act.activation(CS[:, :, :], CIN[:, :, :], ACT.Silu).then_inc(s_cv, 1)
            act.wait_ge(s_set, 1)
            act.wait_ge(s_cv, 1)
            act.activation(CV[:, 0:4 * KT].rearrange("p (k c) -> p k c", c=4)[:, :, 0:2], CS[:, :, :],
                           ACT.Copy).then_inc(s_cv, 1)
            def high_start(u):
                if u >= 2:
                    act.wait_ge(s_ada, u - 1)
                high(u % 2, 16 * (u // 2 + 1))

            for b in range(3):
                act.wait_ge(s_x[b], 16)
                squares(0, b)
                high_start(2 * b)
                high_start(2 * b + 1)
            high_start(6)
            high_start(7)
            for b in range(3):
                norm_high(0, b)
                high_start(8 + 2 * b)
                high_start(9 + 2 * b)
            high_start(U_FFN1)
            high_start(U_FFN1 + 1)

            def ffn(f, it, ph, w2r, w2h, prefetch):
                nsteps = 2 * f["T"]
                for i in range(nsteps):
                    n = f["step"] + nsteps * it + i
                    ft, (_, t0, nt) = i // f["T"], f["blocks"][i % f["T"]]
                    act.wait_ge(s_gu, n + 1)
                    act.activation(SG[:, i % 2, 0:nt], PS[2 * (i % 2)][:, 0:nt], ACT.Silu).then_inc(s_silu, 1)
                    act.wait_ge(s_prod, n + 3)
                    act.activation(ph[:, ft, off(f, i):off(f, i) + nt], PR[:, i % 2, 0:nt],
                                   ACT.Copy).then_inc(s_ph, 1)
                    if i < 2:
                        if i == 0:
                            act.wait_ge(s_yd, f["y"] + 8 * f["T"] * it + 2)
                        act.wait_ge(s_w2raw, 32 * it + 16 * (f["v"] + i + 1))
                        act.activation(w2h[:, i], w2r[:, :], ACT.Copy).then_inc(s_w2hi, 1)
                    if i == f["T"] - 1 and prefetch:
                        high(0, 8 * (f["unit"] + 2) + 16 + 8 * f["per"] * it)
                if prefetch:
                    high(1, 8 * (f["unit"] + 2) + 16 + 8 * f["per"] * it)
                if prefetch and f["per"] == 4:
                    for j in range(2):
                        act.wait_ge(s_ada, ADA_FIRST + 2 * it + j + 1)
                        high(j, 8 * (f["unit"] + 4) + 16 + 32 * it)

            def off(f, i):
                s, t0, _ = f["blocks"][i % f["T"]]
                return SEQ if s else t0

            with act.Fori(0, NIT) as it:
                ffn(FFN[0], it, PH1, W2R1, W2H1, True)

            act.wait_ge(s_yd, y_all[0])
            for b in range(3):
                squares(1, b)
                if b:
                    act.wait_ge(s_fill, LAST_FILL[b - 1] + 1)
                    high((b + 1) % 2, 16 * ((U_MIX + b + 1) // 2 + 1))
                norm_high(1, b)

            act.wait_ge(s_cst, 16)
            act.activation(LG[:, :], LG[:, :], ACT.Exp).then_inc(s_exp, 1)
            act.wait_ge(s_lg, 1)
            for d in range(2):
                for h in range(HEADS):
                    dh = 4 * d + h
                    lg = LG[:, dh:dh + 1]
                    act.activation(ZL[:, dh:dh + 1], CST[:, C_IDX + d:C_IDX + d + 1], ACT.Exp, scale=lg)
                    for tb in range(2):
                        col = C_IDX + (2 + tb if d == 0 else 4 + tb)
                        act.activation(ZC[:, tb, dh:dh + 1], CST[:, col:col + 1], ACT.Exp, scale=lg)
                    act.activation(DEC[:, dh:dh + 1], CST[:, C_IDX + 6:C_IDX + 7], ACT.Exp, scale=lg)
                    c0 = C_XIF if d == 0 else C_XIB
                    act.activation(XI[:, dh, :], CST[:, c0:c0 + P], ACT.Exp, scale=lg).then_inc(s_exp, 1)
            for h in range(HEADS):
                for d in range(2):
                    if h:
                        act.wait_ge(s_dec, h)
                    act.activation(DT[:, d, :], CST[:, C_ABS:C_ABS + P], ACT.Exp,
                                   scale=LG[:, 4 * d + h:4 * d + h + 1]).then_inc(s_exp, 1)

            def evac(key):
                n = FILL[key]
                act.wait_ge(s_fill, n + 1)
                return PS[n % NRING], s_free[n % NRING]

            for i, (kind, a, p) in enumerate(MIX_UNITS):
                if i >= 3:
                    act.wait_ge(s_fill, LAST_FILL[i - 1] + 1)
                    high((i + 1) % 2, 16 * ((U_MIX + i + 1) // 2 + 1))
                if kind == "ctx" and a == "v":
                    ps, free = evac(("cv", p, 0))
                    act.activation(VC[:, :, p * UC:(p + 1) * UC], ps[:, :].rearrange("p (b c) -> p b c", b=2),
                                   ACT.Copy).then_inc(free, 1)
                    if p == 1:
                        for d in range(2):
                            ps, free = evac(("state0", d, 0))
                            act.activation(S0[:, d, :, :], ps[:, :].rearrange("p (h v) -> p h v", h=HEADS),
                                           ACT.Copy).then_inc(free, 1)
                if kind == "lat" and a == "v":
                    for j in range(4):
                        ps, free = evac(("v", p, j))
                        act.activation(V[:, 2 * j:2 * j + 2, :], ps[:, :].rearrange("p (b c) -> p b c", b=2),
                                       ACT.Copy).then_inc(free, 1)
                    for hh in range(2):
                        h = 2 * p + hh
                        for j in range(2):
                            ps, free = evac(("kt", h, j))
                            for d in range(2):
                                ins = act.activation(KZ[d][:, 4 * j:4 * j + 4, :],
                                                     ps[:, :].rearrange("p (c d) -> p c d", c=4),
                                                     ACT.Copy, scale=ZL[:, 4 * d + h:4 * d + h + 1])
                                ins.then_inc(free if d else s_kz, 1)
                        for j in range(2):
                            ps, free = evac(("o", h, j))
                            act.activation(RET[:, h, j * TB:(j + 1) * TB], ps[:, :], ACT.Copy).then_inc(s_oc, 1)
                            act.activation(PM[:, 4 * j:4 * j + 4, :], ps[:, :].rearrange("p (c t) -> p c t", c=4),
                                           ACT.Square).then_inc(free, 1)
                if kind == "lat" and a == "g":
                    for t in range(2):
                        for tb in range(2):
                            n = 4 * p + 2 * t + tb
                            if n >= 2:
                                act.wait_ge(s_cat, n - 1)
                            ps, free = evac(("g", 2 * p + t, tb))
                            act.activation(GU[:, tb, :], ps[:, :], ACT.Silu).then_inc(free, 1)
                if kind == "lat" and a == "vg":
                    for j in range(4):
                        ps, free = evac(("vg", p, j))
                        act.activation(V[:, 2 * j:2 * j + 2, :], ps[:, :].rearrange("p (b c) -> p b c", b=2),
                                       ACT.Gelu_apprx_tanh).then_inc(free, 1)
                if kind == "lat" and a == "u":
                    for t in range(2):
                        for tb in range(2):
                            n = 8 + 4 * p + 2 * t + tb
                            act.wait_ge(s_cat, n - 1)
                            ps, free = evac(("u", 2 * p + t, tb))
                            act.activation(GU[:, tb, :], ps[:, :], ACT.Gelu_apprx_tanh).then_inc(free, 1)
                    if p == 1:
                        for n in range(16):
                            k, t0 = n % 8, n // 8 * TB
                            act.wait_ge(s_cat, 16)
                            src = RET[:, k, t0:t0 + TB] if k < 4 else GM[:, k - 4, t0:t0 + TB]
                            act.activation(HH[:, k, t0:t0 + TB], src, ACT.Copy).then_inc(s_cath, 1)
                if kind == "out" and a == 1:
                    if p == 0:
                        act.wait_ge(*release(FILL["out", 0, 7]))
                        squares(2, 1)
                    if p == 1:
                        norm_high(2, 1)
            act.wait_ge(s_fill, LAST_FILL[len(MIX_UNITS) - 1] + 1)
            high(1, 16 * ((U_FFN2 + 1) // 2 + 1))
            act.wait_ge(*release(FILL["out", 1, 7]))
            squares(2, 2)
            norm_high(2, 2)
            with act.Fori(0, NIT - 1) as it:
                ffn(FFN[1], it, PH2, W2R2, W2H2, True)
            ffn(FFN[1], NIT - 1, PH2, W2R2, W2H2, False)
            act.wait_ge(s_yd, y_all[1])
            for b in (1, 2):
                squares(3, b)

        @block.vector
        def _(dve):
            chain = [0]

            def link(ins):
                chain[0] += 1
                ins.then_inc(s_chain, 1)
                dve.wait_ge(s_chain, chain[0])

            link(dve.memset(ONES[:, :], 1.0))
            dve.memset(CV[:, :].bitcast(F32), 0.0).then_inc(s_set, 1)
            dve.memset(MS[:, :], 0.0).then_inc(s_prod, 2)
            dve.memset(RS[:, :], 0.0).then_inc(s_pl, 2)
            dve.memset(DEC[:, :], 0.0).then_inc(s_yd, 2)
            dve.wait_ge(s_cv, 2)
            dve.tensor_tensor(CV[:, 0:4 * KT].rearrange("p (k c) -> p k c", c=4)[:, :, 2:4], CS[:, :, :],
                              CV[:, 0:4 * KT].rearrange("p (k c) -> p k c", c=4)[:, :, 0:2].bitcast(F32),
                              ALU.subtract).then_inc(s_cv, 1)

            def add_squares(place, b):
                n, j = BLOCKS[b][2], J[place, b]
                for k in range(KT):
                    dve.wait_ge(s_sq, 8 * j + k + 1)
                    if k == 0:
                        if j:
                            dve.wait_ge(s_st, j)
                        ins = dve.tensor_copy(ACC[:, 0:n], SQ[:, 0, 0:n])
                    else:
                        dve.wait_ge(s_acc, 8 * j + k)
                        ins = dve.tensor_tensor(ACC[:, 0:n], ACC[:, 0:n], SQ[:, k % 2, 0:n], ALU.add)
                    ins.then_inc(s_acc, 1)

            def norm_mean(place, b):
                nb, j = BLOCKS[b][2] // P, J[place, b]
                dve.wait_ge(s_st, j + 1)
                dve.tensor_scalar(MS[:, 0:nb], ST_BANK[:, 0:nb], 1.0 / D, EPS, ALU.mult, ALU.add).then_inc(s_ms, 1)

            def diagonal(nb, rs, dst):
                return dve.tensor_tensor(dst, ID[:, :].unsqueeze(1).to_broadcast([P, nb, P]),
                                         rs.unsqueeze(2).to_broadcast([P, nb, P]), ALU.mult)

            def norm_diagonal(place, b):
                nb, j = BLOCKS[b][2] // P, J[place, b]
                dve.wait_ge(s_rs, j + 1)
                if j:
                    dve.wait_ge(s_rb, j)
                diagonal(nb, RS[:, 0:nb], DG[:, 0:nb, :]).then_inc(s_dg, 1)

            def norm_apply(place, b):
                s, _, n = BLOCKS[b]
                xs, j = streams(b)[0], J[place, b]
                dve.wait_ge(s_rb, j + 1)
                for k in range(KT):
                    if place == 3:
                        dve.scalar_tensor_tensor(OUT[b - 1][:, k, :], tokens(xs, b)(k), FG[:, k:k + 1],
                                                 RB_BANK[:, 0:n], ALU.mult, ALU.mult).then_inc(s_hf, 1)
                        continue
                    if 8 * j + k >= 2:
                        dve.wait_ge(s_hl, 8 * j + k - 1)
                    link(dve.tensor_tensor(HF[:, k % 2, 0:n], tokens(xs, b)(k), RB_BANK[:, 0:n], ALU.mult))
                    dve.tensor_scalar(HF[:, k % 2, 0:n], HF[:, k % 2, 0:n], GAIN[:, place, k, s:s + 1],
                                      MODS[:, 3 * place * KT + k, s:s + 1], ALU.mult, ALU.add).then_inc(s_hf, 1)

            def norm(place, b):
                add_squares(place, b)
                norm_mean(place, b)
                norm_diagonal(place, b)
                norm_apply(place, b)

            def ada_rows(a, slot, bank):
                dve.wait_ge(s_ada, a + 1)
                dve.tensor_copy(A4[:, slot, :], PS[bank][0:4, 0:UC]).then_inc(s_a4, 1)

            def ada_mods(a, bank):
                dve.wait_ge(s_col, a + 1)
                dst, b = ada_tiles(MODS, a), ada_tiles(BA, a)
                dve.tensor_tensor(dst, PS[bank][:, UC:UC + 4].rearrange("p (t s) -> p t s", t=2), b,
                                  ALU.add).then_inc(s_mods, 1)

            def ada_tiles(t, a):
                return t[:, bass.ts(a, 2), :]

            def low(u):
                dve.wait_ge(s_hi, u + 1)
                dve.tensor_tensor(WL[:, 1], WR[:, 1], WH[:, 1].bitcast(F32), ALU.subtract).then_inc(s_lo[1], 1)

            def ada_pair_start(u):
                low(u + 1)
                for a in (u, u + 1):
                    ada_rows(a, a % 2, a % 4)
                for a in (u, u + 1):
                    ada_mods(a, a % 4)

            def gain(place):
                dve.wait_ge(s_mods, 4 * (3 * place + 2))
                c = (3 * place + 1) * KT
                dve.scalar_tensor_tensor(GAIN[:, place], MODS[:, c:c + KT, :], 1.0,
                                         NG[:, place, :].unsqueeze(2).to_broadcast([P, KT, 2]),
                                         ALU.add, ALU.mult).then_inc(s_coef, 1)

            def gate(place):
                dve.wait_ge(s_mods, 4 * (3 * place + 3))
                c = (3 * place + 2) * KT
                dve.tensor_scalar(GATE[:, place], MODS[:, c:c + KT, :], 1.0 if place == 1 else 0.5, None,
                                  ALU.mult).then_inc(s_coef, 1)

            add_squares(0, 0)
            norm_mean(0, 0)
            norm_diagonal(0, 0)
            ada_pair_start(0)
            add_squares(0, 1)
            norm_mean(0, 1)
            ada_pair_start(2)
            norm_diagonal(0, 1)
            add_squares(0, 2)
            ada_pair_start(4)
            ada_pair_start(6)
            gain(0)
            dve.wait_ge(s_coef, 1)
            norm_apply(0, 0)
            norm_mean(0, 2)
            norm_diagonal(0, 2)
            ada_pair_start(8)
            norm_apply(0, 1)
            ada_pair_start(10)
            gate(0)
            norm_apply(0, 2)
            ada_pair_start(12)

            def ffn(f, it, ph, pl):
                nsteps = 2 * f["T"]
                for i in range(nsteps):
                    n = f["step"] + nsteps * it + i
                    s, t0, nt = f["blocks"][i % f["T"]]
                    o = SEQ if s else t0
                    ft = i // f["T"]
                    dve.wait_ge(s_silu, n + 1)
                    dve.wait_ge(s_pl, n + 2)
                    dve.tensor_tensor(PR[:, i % 2, 0:nt], SG[:, i % 2, 0:nt], PS[2 * (i % 2) + 1][:, 0:nt],
                                      ALU.mult).then_inc(s_prod, 1)
                    dve.wait_ge(s_ph, n + 1)
                    dve.tensor_tensor(pl[:, ft, o:o + nt], PR[:, i % 2, 0:nt], ph[:, ft, o:o + nt].bitcast(F32),
                                      ALU.subtract).then_inc(s_pl, 1)
                first = f["per"] == 4
                if first:
                    for j in range(2):
                        ada_rows(ADA_FIRST + 2 * it + j, j, 6 + j)
                place = 0 if first else 2
                for t in range(f["T"]):
                    s, t0, nt = f["blocks"][t]
                    xs = XC if s else X
                    for k in range(KT):
                        dve.wait_ge(s_y, f["y"] + 8 * f["T"] * it + 8 * t + k + 1)
                        xv = xs[:, k, t0:t0 + nt]
                        dve.scalar_tensor_tensor(xv, PS[4 + k % 2][:, 0:nt], GATE[:, place, k, s:s + 1], xv,
                                                 ALU.mult, ALU.add).then_inc(s_yd, 1)
                    if first and t == 0:
                        for j in range(2):
                            ada_mods(ADA_FIRST + 2 * it + j, 6 + j)

            with dve.Fori(0, NIT) as it:
                ffn(FFN[0], it, PH1, PL1)

            gain(1)
            gate(1)
            gain(2)
            gate(2)
            dve.wait_ge(s_coef, 6)
            dve.wait_ge(s_yd, y_all[0])
            for b in range(3):
                norm(1, b)

            dve.wait_ge(s_exp, 1)
            dve.tensor_scalar(LG[:, :], LG[:, :], -1.0, None, ALU.mult).then_inc(s_lg, 1)
            for h in range(HEADS):
                dve.wait_ge(s_exp, 9 + 2 * h + 2)
                link(dve.tensor_tensor(DM[:, h, :], DT[:, 0, :], CST[:, C_LOW:C_LOW + P], ALU.mult))
                link(dve.tensor_tensor(DT[:, 0, :], DT[:, 1, :], CST[:, C_UP:C_UP + P], ALU.mult))
                dve.tensor_tensor(DM[:, h, :], DM[:, h, :], DT[:, 0, :], ALU.add).then_inc(s_dec, 1)

            def evac(key):
                n = FILL[key]
                dve.wait_ge(s_fill, n + 1)
                return PS[n % NRING], s_free[n % NRING]

            def read(key):
                dve.wait_ge(*release(FILL[key]))

            n_rope = 0
            dve.wait_ge(s_rope, 32)
            for i, (kind, a, p) in enumerate(MIX_UNITS):
                if kind == "ctx" and a == "k":
                    ps, free = evac(("ck", p, 0))
                    for tb in range(2):
                        for hh in range(2):
                            for d in range(2):
                                h = 2 * p + hh
                                ins = dve.tensor_scalar(KC[:, d, tb, h, :], ps[:, tb * UC + hh * P:tb * UC + hh * P + P],
                                                        ZC[:, tb, 4 * d + h:4 * d + h + 1], K_SCALE, ALU.mult, ALU.mult)
                    ins.then_inc(free, 1)
                if kind == "lat" and a in ("k", "q"):
                    dst = KF if a == "k" else QF
                    for t in range(2):
                        for tb in range(2):
                            ps, free = evac((a, 2 * p + t, tb))
                            d = dst[:, t, tb * TB:(tb + 1) * TB]
                            tmp = TMP[:, 0, :]
                            cols = slice(tb * TB, (tb + 1) * TB)
                            scale = K_SCALE if a == "k" else 1.0
                            if n_rope:
                                dve.wait_ge(s_rope_done, n_rope)
                            dve.scalar_tensor_tensor(tmp[0:64], ps[64:P, :], scale, SIN[64:P, cols], ALU.mult, ALU.mult)
                            dve.scalar_tensor_tensor(tmp[64:P], ps[0:64, :], scale, SIN[0:64, cols], ALU.mult, ALU.mult)
                            dve.scalar_tensor_tensor(d, ps[:, :], scale, COS[:, cols], ALU.mult, ALU.mult).then_inc(free, 1)
                            dve.wait_ge(*release(FILL[a, 2 * p + t, tb]))
                            dve.tensor_tensor(d, d, tmp, ALU.add).then_inc(s_rope_done, 1)
                            n_rope += 1
                if kind == "lat" and a == "v":
                    for hh in range(2):
                        h = 2 * p + hh
                        for j in range(2):
                            ps, free = evac(("score", h, j))
                            dve.tensor_tensor(PM[:, 4 * j:4 * j + 4, :], ps[:, :].rearrange("p (c t) -> p c t", c=4),
                                              DM[:, h, :].unsqueeze(1).to_broadcast([P, 4, P]), ALU.mult).then_inc(free, 1)
                        dve.wait_ge(s_fill, FILL["ub", h, 1] + 1)
                        dve.wait_ge(s_free[FILL["state0", 1, 0] % NRING], release(FILL["state0", 1, 0])[1])
                        for step in range(NCH - 1):
                            for d in range(2):
                                c = step if d == 0 else NCH - 1 - step
                                n = FILL["uf" if d == 0 else "ub", h, c // 4]
                                before = KZ[d][:, c, :]
                                if step == 0:
                                    before = S0[:, d, h, :]
                                else:
                                    dve.wait_ge(s_state, 14 * h + 2 * (step - 1) + d + 1)
                                dve.scalar_tensor_tensor(KZ[d][:, c + 1 - 2 * d, :], before, DEC[:, 4 * d + h:4 * d + h + 1],
                                                         PS[n % NRING][:, (c % 4) * P:(c % 4 + 1) * P],
                                                         ALU.mult, ALU.add).then_inc(s_state, 1)
                        ps, free = evac(("ysum", h, 0))
                        dve.tensor_scalar(MS[:, 8:16], ps[:, 0:8], 1.0 / P, EPS, ALU.mult, ALU.add).then_inc(s_ym, 1)
                        dve.wait_ge(s_yr, h + 1)
                        for j in range(2):
                            if h or j:
                                prev = FILL["yscale", h, 0] if j else FILL["yscale", h - 1, 1]
                                dve.wait_ge(s_fill, prev + 1)
                            diagonal(4, RS[:, 8 + 4 * j:12 + 4 * j], TMP[:, 1, :].rearrange("p (b t) -> p b t", b=4)).then_inc(s_yg, 1)
                            ps, free = evac(("yscale", h, j))
                            dve.wait_ge(s_oc, 2 * h + j + 1)
                            r = RET[:, h, j * TB:(j + 1) * TB]
                            dve.tensor_tensor(r, r, ps[:, :], ALU.mult).then_inc(free, 1)
                if kind == "lat" and a == "g":
                    for t in range(2):
                        for tb in range(2):
                            read(("g", 2 * p + t, tb))
                            r = RET[:, 2 * p + t, tb * TB:(tb + 1) * TB]
                            dve.tensor_tensor(r, r, GU[:, tb, :], ALU.mult).then_inc(s_cat, 1)
                if kind == "lat" and a == "vg":
                    for j in range(4):
                        read(("vg", p, j))
                        for c in (2 * j, 2 * j + 1):
                            for g in range(2):
                                link(dve.bn_stats(BST[:, 2 * c + g, :], V[:, c, g * P:(g + 1) * P]))
                                link(dve.bn_aggr(MV[:, 2 * c + g, :], BST[:, 2 * c + g, :]))
                    dve.tensor_scalar(MS[:, 16:32], MV[:, :, 1], EPS, None, ALU.add).then_inc(s_lv, 1)
                    dve.wait_ge(s_lr, p + 1)
                    for c in range(NCH):
                        for g in range(2):
                            m = 2 * c + g
                            v = V[:, c, g * P:(g + 1) * P]
                            ins = dve.tensor_scalar(v, v, MV[:, m, 0:1], RS[:, 16 + m:17 + m], ALU.subtract, ALU.mult)
                    ins.then_inc(s_vn, 1)
                if kind == "lat" and a == "u":
                    for t in range(2):
                        for tb in range(2):
                            g = 2 * p + t
                            ps, free = evac(("mixed", g, tb))
                            dve.wait_ge(s_gw, 32)
                            dve.tensor_tensor(MIXD[:, tb, :].rearrange("p (c t) -> p c t", c=4),
                                              ps[:, :].rearrange("p (c t) -> p c t", c=4),
                                              BB[:, g, :].unsqueeze(1).to_broadcast([P, 4, P]), ALU.add).then_inc(s_mx, 1)
                            dve.wait_ge(s_mx, 2 * g + tb + 1)
                            read(("u", g, tb))
                            dve.tensor_tensor(GM[:, g, tb * TB:(tb + 1) * TB], MIXD[:, tb, :], GU[:, tb, :],
                                              ALU.mult).then_inc(s_cat, 1)
                if kind == "out":
                    for t in range(2):
                        ps, free = evac(("out", a, 2 * p + t))
                        xv = X[:, 2 * p + t, a * TB:(a + 1) * TB]
                        dve.scalar_tensor_tensor(xv, ps[:, :], GATE[:, 1, 2 * p + t, 0:1], xv,
                                                 ALU.mult, ALU.add).then_inc(free, 1)
                    if a == 1 and p == 0:
                        add_squares(2, 1)
                        norm_mean(2, 1)
                        norm_diagonal(2, 1)
                    if a == 1 and p == 1:
                        norm_apply(2, 1)
            norm(2, 2)
            with dve.Fori(0, NIT) as it:
                ffn(FFN[1], it, PH2, PL2)
            dve.wait_ge(s_yd, y_all[1])
            for b in (1, 2):
                norm(3, b)

        @block.tensor
        def _(pe):
            def mm3(dst, wh, wl, xh, xl, first, last):
                pe.matmul(dst, wh, xh, start=first, stop=False)
                pe.matmul(dst, wh, xl, start=False, stop=False)
                return pe.matmul(dst, wl, xh, start=False, stop=last)

            def norm_sum(j, n):
                pe.wait_ge(s_acc, 8 * (j + 1))
                if j:
                    pe.wait_ge(s_ms, j)
                for b in range(n // P):
                    ins = pe.matmul(ST_BANK[:, b:b + 1], ACC[:, b * P:(b + 1) * P], ONES[:, 0:1], start=True, stop=True)
                ins.then_inc(s_st, 1)

            def norm_scale(j, n):
                pe.wait_ge(s_dg, j + 1)
                if j:
                    pe.wait_ge(s_hf, 8 * j)
                pe.matmul(RB_BANK[:, 0:n], ONES[:, :], DG[:, 0:n // P, :], start=True, stop=True).then_inc(s_rb, 1)

            def ada_product(a, slot, bank, count):
                pe.wait_ge(s_lo[slot], count)
                for k in range(KT):
                    for w in (WH, WL):
                        ins = pe.matmul(PS[bank][:, 0:UC], CV[:, 4 * k:4 * k + P], w[:, slot, k, :],
                                        start=(k == 0 and w is WH), stop=(k == KT - 1 and w is WL))
                ins.then_inc(s_ada, 1)

            def ada_columns(a, slot, bank):
                pe.wait_ge(s_a4, a + 1)
                for t in range(2):
                    ins = pe.matmul(PS[bank][:, UC + 2 * t:UC + 2 * t + 2], A4[:, slot, t * P:(t + 1) * P], SEL[:, :],
                                    start=True, stop=True)
                ins.then_inc(s_col, 1)

            def ada_pair_start(u):
                for a in (u, u + 1):
                    if a >= 4:
                        pe.wait_ge(s_mods, a - 3)
                    ada_product(a, a % 2, a % 4, a // 2 + 1)
                for a in (u, u + 1):
                    ada_columns(a, a % 2, a % 4)

            pe.wait_ge(s_const, 16 * 7)
            pe.wait_ge(s_cv, 3)
            norm_sum(J[0, 0], CTX)
            norm_scale(J[0, 0], CTX)
            ada_pair_start(0)
            norm_sum(J[0, 1], TB)
            ada_pair_start(2)
            norm_sum(J[0, 2], TB)
            ada_pair_start(4)
            ada_pair_start(6)
            norm_scale(J[0, 1], TB)
            ada_pair_start(8)
            norm_scale(J[0, 2], TB)
            ada_pair_start(10)
            ada_pair_start(12)
            pe.wait_ge(s_mods, ADA_FIRST)

            def ffn(f, it, ph, pl, w2h, w2l):
                T, first = f["T"], f["per"] == 4
                for i in range(2 * T):
                    n = f["step"] + 2 * T * it + i
                    ft, (s, t0, nt) = i // T, f["blocks"][i % T]
                    xh, xl = (HCH, HCL) if s else (HH, HL)
                    if i % T == 0:
                        pe.wait_ge(s_lo[ft], f["unit"] // 2 + (f["per"] // 2) * it + 1)
                    pe.wait_ge(s_hl, 8 * (J[0 if first else 2, BLOCKS.index(f["blocks"][i % T])] + 1))
                    pe.wait_ge(s_prod, n + 1)
                    for half in range(2):
                        for k in range(KT):
                            cols = slice(half * P, (half + 1) * P)
                            ins = mm3(PS[2 * (i % 2) + half][:, 0:nt], WH[:, ft, k, cols], WL[:, ft, k, cols],
                                      xh[:, k, t0:t0 + nt], xl[:, k, t0:t0 + nt], k == 0, k == KT - 1)
                    ins.then_inc(s_gu, 1)
                if first:
                    for j in range(2):
                        a = ADA_FIRST + 2 * it + j
                        pe.wait_ge(s_mods, ADA_FIRST + 2 * it)
                        ada_product(a, j, 6 + j, f["unit"] // 2 + 2 * it + 2)
                for t in range(T):
                    s, t0, nt = f["blocks"][t]
                    o = SEQ if s else t0
                    pe.wait_ge(s_pl, f["step"] + 2 * T * it + T + t + 3)
                    pe.wait_ge(s_w2lo, f["v"] + 2 * it + 3)
                    for d in range(KT):
                        pe.wait_ge(s_yd, f["y"] + 8 * T * it + 8 * t + d + 1)
                        for ft in range(2):
                            cols = slice(d * P, (d + 1) * P)
                            ins = mm3(PS[4 + d % 2][:, 0:nt], w2h[:, ft, cols], w2l[:, ft, cols],
                                      ph[:, ft, o:o + nt], pl[:, ft, o:o + nt], ft == 0, ft == 1)
                        ins.then_inc(s_y, 1)
                    if first and t == 0:
                        for j in range(2):
                            ada_columns(ADA_FIRST + 2 * it + j, j, 6 + j)

            with pe.Fori(0, NIT) as it:
                ffn(FFN[0], it, PH1, PL1, W2H1, W2L1)

            pe.wait_ge(s_mods, N_ADA)
            pe.wait_ge(s_prod, 6 * NIT + 2)
            pe.wait_ge(s_yd, y_all[0])
            norm_sum(J[1, 0], CTX)
            norm_scale(J[1, 0], CTX)

            def fill(key):
                n = FILL[key]
                if n >= NRING:
                    pe.wait_ge(*release(n - NRING))
                return PS[n % NRING]

            def retention(h, hh, p):
                pe.wait_ge(s_rope_done, 8 * (p + 1))
                for j in range(2):
                    ps = fill(("kt", h, j))
                    for c in range(4):
                        t0 = (4 * j + c) * P
                        ins = pe.transpose(ps[:, c * P:(c + 1) * P], KF[:, hh, t0:t0 + P], ID[:, :])
                    ins.then_inc(s_fill, 1)
                for j in range(2):
                    ps = fill(("score", h, j))
                    for c in range(4):
                        t0 = (4 * j + c) * P
                        ins = pe.matmul(ps[:, c * P:(c + 1) * P], KF[:, hh, t0:t0 + P], QF[:, hh, t0:t0 + P],
                                        start=True, stop=True)
                    ins.then_inc(s_fill, 1)
                for j in range(4):
                    pe.wait_ge(*release(FILL["v", p, j]))
                for j in range(2):
                    pe.wait_ge(*release(FILL["kt", h, j]))
                for d, name in enumerate(("uf", "ub")):
                    for j in range(2):
                        ps = fill((name, h, j))
                        for c in range(4):
                            n = 4 * j + c
                            ins = pe.matmul(ps[:, c * P:(c + 1) * P], KZ[d][:, n, :], V[:, n, hh * P:(hh + 1) * P],
                                            start=True, stop=True)
                        ins.then_inc(s_fill, 1)
                pe.wait_ge(s_q, 2 * h + 2)
                for j in range(2):
                    pe.wait_ge(*release(FILL["score", h, j]))
                pe.wait_ge(s_state, 14 * (h + 1))
                for j in range(2):
                    ps = fill(("o", h, j))
                    for c in range(4):
                        n = 4 * j + c
                        dst, t0 = ps[:, c * P:(c + 1) * P], n * P
                        pe.matmul(dst, V[:, n, hh * P:(hh + 1) * P], PM[:, n, :], start=True, stop=False)
                        sf = S0[:, 0, h, :] if n == 0 else KZ[0][:, n, :]
                        sb = S0[:, 1, h, :] if n == NCH - 1 else KZ[1][:, n, :]
                        pe.matmul(dst, sf, RET[:, h, t0:t0 + P], start=False, stop=False)
                        ins = pe.matmul(dst, sb, QF[:, hh, t0:t0 + P], start=False, stop=True)
                    ins.then_inc(s_fill, 1)
                for j in range(2):
                    pe.wait_ge(*release(FILL["o", h, j]))
                ps = fill(("ysum", h, 0))
                for c in range(NCH):
                    ins = pe.matmul(ps[:, c:c + 1], PM[:, c, :], ONES[:, 0:1], start=True, stop=True)
                ins.then_inc(s_fill, 1)
                for j in range(2):
                    pe.wait_ge(s_yg, 2 * h + j + 1)
                    ps = fill(("yscale", h, j))
                    pe.matmul(ps[:, :], ONES[:, :], TMP[:, 1, :], start=True, stop=True).then_inc(s_fill, 1)

            for i, (kind, a, p) in enumerate(MIX_UNITS):
                slot = i % 2
                pe.wait_ge(s_lo[slot], (U_MIX + i) // 2 + 1)
                wh, wl = WH[:, slot], WL[:, slot]
                if kind == "ctx":
                    pe.wait_ge(s_hl, 8 * (J[1, 0] + 1))
                    ps = fill(("c" + a, p, 0))
                    for tb in range(2):
                        for k in range(KT):
                            cols = slice(tb * P, (tb + 1) * P)
                            ins = mm3(ps[:, tb * UC:(tb + 1) * UC], HCH[:, k, cols], HCL[:, k, cols],
                                      wh[:, k, :], wl[:, k, :], k == 0, k == KT - 1)
                    ins.then_inc(s_fill, 1)
                    if i % 2 == 0:
                        norm_sum(J[1, 1 + i // 2], TB)
                    else:
                        norm_scale(J[1, 1 + i // 2], TB)
                    if i == 3:
                        for key in (("ck", 0, 0), ("ck", 1, 0), ("cv", 0, 0), ("cv", 1, 0)):
                            pe.wait_ge(*release(FILL[key]))
                        for d in range(2):
                            ps = fill(("state0", d, 0))
                            for h in range(HEADS):
                                for tb in range(2):
                                    ins = pe.matmul(ps[:, h * P:(h + 1) * P], KC[:, d, tb, h, :],
                                                    VC[:, tb, h * P:(h + 1) * P], start=(tb == 0), stop=(tb == 1))
                            ins.then_inc(s_fill, 1)
                elif kind == "out":
                    pe.wait_ge(s_catl, 8 * (a + 1))
                    for t in range(2):
                        ps = fill(("out", a, 2 * p + t))
                        for k in range(KT):
                            ins = mm3(ps[:, :], wh[:, k, t * P:(t + 1) * P], wl[:, k, t * P:(t + 1) * P],
                                      HH[:, k, a * TB:(a + 1) * TB], HL[:, k, a * TB:(a + 1) * TB], k == 0, k == KT - 1)
                        ins.then_inc(s_fill, 1)
                    if a == 1 and p == 0:
                        norm_sum(J[2, 1], TB)
                    if a == 1 and p == 1:
                        norm_scale(J[2, 1], TB)
                elif a in ("k", "q", "g", "u"):
                    for t in range(2):
                        for tb in range(2):
                            pe.wait_ge(s_hl, 8 * (J[1, tb + 1] + 1))
                            if a == "u":
                                g = 2 * p + t
                                pe.wait_ge(s_vn, p + 1)
                                pe.wait_ge(s_gw, 32)
                                ps = fill(("mixed", g, tb))
                                for c in range(4):
                                    ins = pe.matmul(ps[:, c * P:(c + 1) * P], V[:, 4 * tb + c, t * P:(t + 1) * P],
                                                    WST[:, g, :], start=True, stop=True)
                                ins.then_inc(s_fill, 1)
                            ps = fill((a, 2 * p + t, tb))
                            for k in range(KT):
                                ins = mm3(ps[:, :], wh[:, k, t * P:(t + 1) * P], wl[:, k, t * P:(t + 1) * P],
                                          HH[:, k, tb * TB:(tb + 1) * TB], HL[:, k, tb * TB:(tb + 1) * TB],
                                          k == 0, k == KT - 1)
                            ins.then_inc(s_fill, 1)
                else:
                    for j in range(4):
                        ps = fill((a, p, j))
                        for c in range(2):
                            for k in range(KT):
                                cols = slice((2 * j + c) * P, (2 * j + c + 1) * P)
                                ins = mm3(ps[:, c * UC:(c + 1) * UC], HH[:, k, cols], HL[:, k, cols],
                                          wh[:, k, :], wl[:, k, :], k == 0, k == KT - 1)
                        ins.then_inc(s_fill, 1)
                    if a == "v":
                        for hh in range(2):
                            retention(2 * p + hh, hh, p)

            norm_sum(J[2, 2], TB)
            norm_scale(J[2, 2], TB)
            for b in range(NRING):
                pe.wait_ge(*release(len(FILLS) - NRING + b))
            with pe.Fori(0, NIT) as it:
                ffn(FFN[1], it, PH2, PL2, W2H2, W2L2)
            for b in (1, 2):
                norm_sum(J[3, b], TB)
                norm_scale(J[3, b], TB)


def _units(w):
    return w.reshape(KT, P, -1, UC).transpose(2, 1, 0, 3)


def _w1_units(w):
    return w.reshape(KT, P, 2, NF, P).transpose(3, 1, 0, 2, 4).reshape(NF, P, KT, UC)


def _per_feature(v):
    return np.moveaxis(v.reshape(v.shape[:-1] + (-1, P)), -1, 0)


def _tables():
    token = np.arange(SEQ)
    nf = P // 4
    freqs = (np.float32(10000.0) ** (-np.arange(nf, dtype=np.float32) / np.float32(nf))).astype(np.float32)
    row, col = (token // GRID_W).astype(np.float32), (token % GRID_W).astype(np.float32)
    ang = np.concatenate([freqs[:, None] * row, freqs[:, None] * col]).astype(np.float32)
    cosine = np.cos(ang, dtype=np.float32)
    sine = np.sin(ang, dtype=np.float32)
    i, j = np.arange(P)[None, :], np.arange(P)[:, None]
    c = np.zeros((P, C_END), np.float32)
    c[:, C_ABS:C_ABS + P] = abs(i - j)
    c[:, C_LOW:C_LOW + P] = i >= j
    c[:, C_UP:C_UP + P] = i <= j
    c[:, C_XIF:C_XIF + P] = i + 1
    c[:, C_XIB:C_XIB + P] = CHUNK - i
    p = np.arange(P)
    for n, v in enumerate((CHUNK - 1 - p, p, CTX - 1 - p, CTX - 1 - P - p, p, P + p, CHUNK + 0 * p)):
        c[:, C_IDX + n] = v
    sel = np.array([[1, 0], [0, 1], [1, 0], [0, 1]], np.float32)
    return (np.concatenate([cosine, cosine]), np.concatenate([sine, -sine]), c, np.eye(P, dtype=np.float32), sel)


def kernel(x, c, ctx, c_ctx, w_ada, b_ada, norm_g, ffn1_w1, ffn1_w2, w_in, ret_decay,
           gmlp_ws, gmlp_bs, w_out, ffn2_w1, ffn2_w2, final_g):
    import concourse.bacc as bacc
    from concourse.bass_utils import run_bass_kernel_spmd

    a = lambda v: np.asarray(v)
    ada, win, wout = _units(a(w_ada)[0]), _units(a(w_in)[0]), _units(a(w_out)[0])
    f1, f2 = _w1_units(a(ffn1_w1)[0]), _w1_units(a(ffn2_w1)[0])
    stream = [ada[:ADA_FIRST]]
    for i in range(NIT):
        n = ADA_FIRST + 2 * i
        stream += [f1[2 * i:2 * i + 2], ada[n:n + 2]]
    for kind, part, p in MIX_UNITS:
        n = p if kind == "out" else WIN[part] + p
        stream.append((wout if kind == "out" else win)[n:n + 1])
    stream.append(f2)
    cosine, sine, consts, ident, sel = _tables()
    arrays = {
        "x": a(x)[0].T, "ctx": a(ctx)[0].T,
        "c2": np.stack([_per_feature(a(c)[0]), _per_feature(a(c_ctx))], axis=-1),
        "w_units": np.concatenate(stream),
        "w2_units": np.concatenate([a(ffn1_w2)[0].reshape(NF, P, D), a(ffn2_w2)[0].reshape(NF, P, D)]),
        "b_ada": np.repeat(_per_feature(a(b_ada)[0])[..., None], 2, axis=-1),
        "norm_g": _per_feature(a(norm_g)[0]), "final_g": _per_feature(a(final_g)),
        "decay": np.broadcast_to(a(ret_decay)[0].reshape(1, 8), (P, 8)),
        "ws": a(gmlp_ws)[0].transpose(2, 0, 1),
        "bs": np.broadcast_to(a(gmlp_bs)[0][None], (P, GROUPS, CHUNK)),
        "cosine": cosine, "sine": sine, "consts": consts, "ident": ident, "sel": sel,
    }
    arrays = {k: np.ascontiguousarray(v) for k, v in arrays.items()}
    nc = bacc.Bacc("TRN2", target_bir_lowering=False, num_devices=1, dynamic_dma_scratch_size=64)
    args = [nc.dram_tensor(k, v.shape, mybir.dt.from_np(v.dtype), kind="ExternalInput").ap()
            for k, v in arrays.items()]
    out = nc.dram_tensor("out", (D, SEQ), F32, kind="ExternalOutput").ap()
    layer(nc, *args, out)
    r = run_bass_kernel_spmd(nc, [arrays], core_ids=[0])
    return np.ascontiguousarray(r.results[0]["out"].T)[None]
```

```python
from contextlib import ExitStack

import numpy as np

import concourse.bass as bass
from concourse import mybir

ALU = mybir.AluOpType
ACT = mybir.ActivationFunctionType
F32 = mybir.dt.float32
F32R = mybir.dt.float32r

P = 128
D = 1024
KT = D // P
SEQ, CTX = 1024, 256
FF = 2816
NF = FF // P
HEADS, GROUPS = 4, 4
CHUNK = 128
NCH = SEQ // CHUNK
NMOD = 9
TB = 512
EPS = 1e-6
K_SCALE = float(P) ** -0.5
GRID_W = 64

UC = 256
N_ADA = NMOD * D // UC
ADA_FIRST = 14
NIT = NF // 2
U_FFN1 = 0
U_MIX = U_FFN1 + 4 * NIT
WIN = {"q": 0, "k": 2, "v": 4, "g": 6, "u": 8, "vg": 10}
MIX_UNITS = ([("ctx", "ck", 0), ("ctx", "ck", 1), ("ctx", "cv", 0), ("ctx", "cv", 1)]
             + [("lat", a, p) for p in range(2) for a in ("k", "q", "v")]
             + [("lat", a, p) for a in ("g", "vg", "u") for p in range(2)]
             + [("out", tb, p) for tb in range(2) for p in range(4)])
U_FFN2 = U_MIX + len(MIX_UNITS)

C_ABS, C_LOW, C_UP, C_XIF, C_XIB, C_END = 0, 128, 256, 384, 512, 640
Z_LAT, Z_CTX, Z_CHUNK, Z_END = (0, 1), ((2, 3), (4, 5)), 6, 8

BLOCKS = [(1, 0, CTX), (0, 0, TB), (0, TB, TB)]
NRING = 6


def mixer_fills():
    fills, late = [], []
    for i, (kind, a, p) in enumerate(MIX_UNITS):
        if kind == "ctx":
            fills.append((i, a, p, 0))
        elif kind == "out":
            fills += [(i, "out", a, 2 * p + t) for t in range(2)]
        elif a in ("v", "vg"):
            fills += [(i, a, p, j) for j in range(4)]
            if a == "v":
                if p == 0:
                    fills += [(i, "state0", d, 0) for d in range(2)]
                h = 2 * p
                head = lambda h, *names: [(i, name, h, j) for name in names for j in range(2)]
                fills += head(h, "kt", "score", "uf", "ub", "o") + head(h + 1, "kt", "score")
                fills += [(i, "ysum", h, 0)] + head(h + 1, "uf", "ub") + head(h, "yscale") + head(h + 1, "o")
                late = [[(i + 1, "ysum", h + 1, 0)], [(i + 1, "yscale", h + 1, j) for j in range(2)]]
        else:
            for n in range(4):
                t, tb = (n % 2, n // 2) if (a, p) == ("u", 1) else (n // 2, n % 2)
                fills.append((i, a, 2 * p + t, tb))
                if a == "u":
                    fills.append((i, "mixed", 2 * p + t, tb))
                if late:
                    fills += late.pop(0)
    return fills


FILLS = mixer_fills()
FILL = {(name, a, b): n for n, (_, name, a, b) in enumerate(FILLS)}
LAST_FILL = [max(n for n, f in enumerate(FILLS) if f[0] == i and f[1] in (a, kind)) for i, (kind, a, _) in enumerate(MIX_UNITS)]
FIRST_FILL = [min(n for n, f in enumerate(FILLS) if f[0] == i) for i in range(len(MIX_UNITS))]


def layer(nc, x, ctx, c2, ada_units, w_units, w2_units, b_ada, norm_g, final_g, decay, ws, bs, cosine, sine, consts, powers, ident, sel, out):
    stack = ExitStack()
    with stack:
        def at(name, shape, dt, offset):
            return nc.alloc_sbuf_tensor_at(name, shape, dt, offset=offset)

        top = [192]

        def keep(name, shape, dt):
            n = 4 * int(np.prod(shape[1:]))
            n += -n % 32
            top[0] += n
            return at(name, shape, dt, top[0] - n)

        X = keep("X", [P, KT, SEQ], F32)
        HH = keep("HH", [P, KT, SEQ], F32R)
        HL = keep("HL", [P, KT, SEQ], F32R)
        WR = keep("WR", [P, 2, KT, UC], F32)
        WH = keep("WH", [P, 2, KT, UC], F32R)
        WL = keep("WL", [P, 2, KT, UC], F32R)
        MODS = keep("MODS", [P, NMOD * KT, 2], F32)
        BA = keep("BA", [P, NMOD * KT, 2], F32)
        GAIN = keep("GAIN", [P, 3, KT, 2], F32)
        GATE = keep("GATE", [P, 3, KT, 2], F32)
        NG = keep("NG", [P, 3, KT], F32)
        FG = keep("FG", [P, KT], F32)
        ID = keep("ID", [P, P], F32)
        ONES = keep("ONES", [P, P], F32)
        SEL = keep("SEL", [4, 2], F32)
        MS = keep("MS", [P, 32], F32)
        RS = keep("RS", [P, 32], F32)
        NEGH = keep("NEGH", [P, 32], F32)
        LG = keep("LG", [P, 8], F32)
        IDX = keep("IDX", [P, Z_END], F32)
        Z = keep("Z", [P, 8, Z_END], F32)
        R = top[0]

        XC = at("XC", [P, KT, CTX], F32, R)
        HCH = at("HCH", [P, KT, CTX], F32R, R + 8192)
        HCL = at("HCL", [P, KT, CTX], F32R, R + 16384)
        NTOK = SEQ + CTX
        PH1 = at("PH1", [P, 2, NTOK], F32R, R + 24576)
        PL1 = at("PL1", [P, 2, NTOK], F32R, R + 34816)
        W2R1 = at("W2R1", [P, D], F32, R + 45056)
        W2H1 = at("W2H1", [P, 2, D], F32R, R + 49152)
        W2L1 = at("W2L1", [P, 2, D], F32R, R + 57344)
        SG = at("SG", [P, 2, TB], F32, R + 65536)
        PR = at("PR", [P, 2, TB], F32, R + 69632)
        A4 = at("A4", [4, 2, UC], F32, R + 73728)
        CV = at("CV", [P, 160], F32R, R + 75776)
        CIN = at("CIN", [P, KT, 2], F32, R + 76416)
        CS = at("CS", [P, KT, 2], F32, R + 76480)
        WS = at("WS", [P, 3, KT, UC], F32, R + 45056)

        def norm_buffers(place, sq, acc, dg, hf):
            return (at(f"SQ{place}", [P, 2, TB], F32, R + sq), at(f"ACC{place}", [P, TB], F32, R + acc),
                    at(f"DG{place}", [P, 4, P], F32, R + dg),
                    [at(f"HF{place}_{n}", [P, TB], F32, R + o) for n, o in enumerate(hf)])

        NB = [norm_buffers(0, 24576, 34816, 36864, (29696, 31744, 39936, 41984)),
              norm_buffers(1, 45056, 65536, 67584, (69632, 71680, 73728, 75776)),
              norm_buffers(2, 24576, 28672, 30720, (32768, 34816, 36864, 38912))]
        NB.append(NB[2])
        KF = at("KF", [P, 2, SEQ], F32, R)
        QF = at("QF", [P, 2, SEQ], F32, R + 8192)
        V = at("V", [P, NCH, UC], F32, R + 16384)
        KZ = [at(f"KZ{d}", [P, NCH, P], F32, R + 24576 + 4096 * d) for d in range(2)]
        PM = at("PM", [P, NCH, P], F32, R + 32768)
        XI = at("XI", [P, 8, P], F32, R + 36864)
        RET = at("RET", [P, HEADS, SEQ], F32, R + 40960)
        KC = at("KC", [P, 2, 2, HEADS, P], F32, R + 40960)
        VC = at("VC", [P, 2, HEADS * P], F32, R + 49152)
        CST = at("CST", [P, C_END], F32, R + 53248)
        DT = at("DT", [P, 2, P], F32, R + 55872)
        COS = at("COS", [P, SEQ], F32, R + 57344)
        SIN = at("SIN", [P, SEQ], F32, R + 61440)
        V2 = at("V2", [P, NCH, UC], F32, R + 57344)
        DG2 = at("DG2", [P, 4, P], F32, R + 67584)
        DM = at("DM", [P, HEADS, P], F32, R + 65536)
        TMP = at("TMP", [P, 2, TB], F32, R + 69632)
        S0 = at("S0", [P, 2, HEADS, P], F32, R + 73728)
        GM = at("GM", [P, GROUPS, SEQ], F32, R)
        MIXD = at("MIXD", [P, 2, TB], F32, R + 24576)
        GU = at("GU", [P, 2, TB], F32, R + 28672)
        WST = at("WST", [P, GROUPS, P], F32, R + 32768)
        BB = at("BB", [P, GROUPS, P], F32, R + 34816)
        BST = at("BST", [P, 16, 6], F32, R + 67584)
        MV = at("MV", [P, 16, 2], F32, R + 67584 + 384)
        PH2 = at("PH2", [P, 2, SEQ], F32R, R)
        PL2 = at("PL2", [P, 2, SEQ], F32R, R + 8192)
        W2R2 = at("W2R2", [P, D], F32, R + 40960)
        W2H2 = at("W2H2", [P, 2, D], F32R, R + 45056)
        W2L2 = at("W2L2", [P, 2, D], F32R, R + 53248)
        OUT = [at(f"OUT{b}", [P, KT, TB], F32, o) for b, o in enumerate((R, R + 40960))]

        PS = [stack.enter_context(nc.psum_tensor(f"PS{b}", [P, 512], F32)) for b in range(8)]
        ST_BANK, RB_BANK = PS[6], PS[7]

        sem = lambda name: stack.enter_context(nc.semaphore(name))
        s_const = sem("const_loaded")
        s_cst = sem("decay_consts_loaded")
        s_rope = sem("rope_loaded")
        s_gw = sem("gmlp_weights_loaded")
        s_x = [sem(f"x_loaded{b}") for b in range(3)]
        s_first = [sem(f"first_ada_loaded{s}") for s in range(3)]
        s_raw = [sem(f"unit_loaded{s}") for s in range(2)]
        s_hi = sem("unit_high_done")
        s_lo = [sem(f"unit_low_done{s}") for s in range(2)]
        s_w2raw = sem("w2_loaded")
        s_w2hi = sem("w2_high_done")
        s_w2lo = sem("w2_low_done")
        s_set = sem("constants_set")
        s_cv = sem("silu_c_ready")
        s_ada = sem("ada_product_ready")
        s_a4 = sem("ada_rows_copied")
        s_col = sem("ada_columns_ready")
        s_mods = sem("mods_done")
        s_coef = sem("coefficients_ready")
        s_lg = sem("log_decay_ready")
        s_sq = sem("squares_done")
        s_acc = sem("squares_added")
        s_st = sem("norm_sum_ready")
        s_ms = sem("norm_mean_ready")
        s_rs = sem("norm_rsqrt_ready")
        s_dg = sem("norm_diagonal_ready")
        s_rb = sem("norm_scale_ready")
        s_xm = sem("scaled_done")
        s_hf = sem("modulated_done")
        s_hh = sem("modulated_high_done")
        s_hl = sem("modulated_low_done")
        s_gu = sem("gate_up_ready")
        s_silu = sem("silu_done")
        s_prod = sem("product_done")
        s_ph = sem("product_high_done")
        s_pl = sem("product_low_done")
        s_y = sem("down_ready")
        s_yd = sem("down_added")
        s_fill = sem("fill_ready")
        s_free = [sem(f"bank_free{b}") for b in range(NRING)]
        s_exp = sem("exp_done")
        s_dec = sem("score_masks_ready")
        s_rope_done = sem("rope_done")
        s_kz = sem("decayed_keys_ready")
        s_state = sem("states_ready")
        s_q = sem("decayed_queries_ready")
        s_oc = sem("retention_copied")
        s_ym = sem("retention_mean_ready")
        s_yr = sem("retention_rsqrt_ready")
        s_yg = sem("retention_diagonal_ready")
        s_lv = sem("gmlp_variance_ready")
        s_lr = sem("gmlp_rsqrt_ready")
        s_vn = sem("gmlp_v_normed")
        s_mx = sem("gmlp_mixed_added")
        s_cat = sem("mixer_input_ready")
        s_cath = sem("mixer_high_done")
        s_catl = [sem(f"mixer_low_done{e}") for e in range(2)]
        s_chain = sem("vector_chain")
        s_out = sem("stored")

        def release(n):
            _, name, a, b = FILLS[n]
            if name == "uf":
                return s_state, 14 * a + (7 if b == 0 else 13)
            if name == "ub":
                return s_state, 14 * a + (8 if b == 1 else 14)
            if name == "ysum":
                return s_ym, a + 1
            if name == "mixed":
                return s_mx, sum(f[1] == "mixed" for f in FILLS[:n + 1])
            return s_free[n % NRING], sum(FILLS[m][1] not in ("uf", "ub", "ysum", "mixed")
                                          for m in range(n % NRING, n + 1, NRING))

        NORMS = [(0, b) for b in range(3)] + [(1, b) for b in range(3)] + [(2, 1), (2, 2), (3, 1), (3, 2)]
        J = {key: j for j, key in enumerate(NORMS)}
        FFN = [dict(T=3, blocks=BLOCKS, step=0, y=0, v=0, unit=U_FFN1, per=4),
               dict(T=2, blocks=BLOCKS[1:], step=6 * NIT, y=24 * NIT, v=2 * NIT, unit=U_FFN2, per=2)]
        y_all = [24 * NIT + 2, 40 * NIT + 2]

        def tokens(t, b):
            _, t0, n = BLOCKS[b]
            return lambda k: t[:, k, t0:t0 + n]

        def streams(b):
            return (XC, HCH, HCL) if b == 0 else (X, HH, HL)

        block = stack.enter_context(nc.Block())

        @block.sync
        def _(sp):
            for dst, src in ((CIN[:, :, :], c2), (LG[:, :], decay), (IDX[:, :], powers), (BA[:, :, :], b_ada),
                             (NG[:, :, :], norm_g), (FG[:, :], final_g), (ID[:, :], ident), (SEL[:, :], sel)):
                sp.dma_start(dst, src).then_inc(s_const, 16)

            def unit(u, slot):
                sp.dma_start(WR[:, slot], w_units[u]).then_inc(s_raw[slot], 16)

            def first_ada(a):
                if a >= 3:
                    sp.wait_ge(s_ada, a - 2)
                sp.dma_start(WS[:, a % 3], ada_units[a]).then_inc(s_first[a % 3], 16)

            def tokens_in(b):
                _, t0, n = BLOCKS[b]
                dst, src = (XC, ctx) if b == 0 else (X, x)
                sp.dma_start(dst[:, :, t0:t0 + n],
                             src.rearrange("(k p) t -> p k t", p=P)[:, :, t0:t0 + n]).then_inc(s_x[b], 16)

            tokens_in(0)
            first_ada(0)
            first_ada(1)
            tokens_in(1)
            first_ada(2)
            tokens_in(2)
            for a in range(3, ADA_FIRST):
                first_ada(a)
                if a in (7, 9):
                    unit(U_FFN1 + (a - 7) // 2, (a - 7) // 2)

            def ffn(f, it, w2r, prefetch):
                for j in range(2):
                    sp.wait_ge(s_w2lo, f["v"] + 2 * it + j + 1)
                    sp.dma_start(w2r[:, :], w2_units[f["v"] + 2 * it + j]).then_inc(s_w2raw, 16)
                for j in range(f["per"] if prefetch else 0):
                    u = f["unit"] + f["per"] * it + 2 + j
                    sp.wait_ge(s_lo[j % 2], (f["unit"] + j - j % 2) // 2 + (f["per"] // 2) * it + 1)
                    unit(u, j % 2)

            sp.wait_ge(s_ada, ADA_FIRST)
            with sp.Fori(0, NIT) as it:
                ffn(FFN[0], it, W2R1, True)
            sp.wait_ge(s_yd, y_all[0])
            sp.dma_start(CST[:, :], consts).then_inc(s_cst, 16)
            sp.dma_start(COS[:, :], cosine).then_inc(s_rope, 16)
            sp.dma_start(SIN[:, :], sine).then_inc(s_rope, 16)
            for u in range(U_MIX + 2, U_FFN2 + 2):
                sp.wait_ge(s_lo[u % 2], u // 2)
                unit(u, u % 2)
                if u - U_MIX == 12:
                    sp.wait_ge(s_fill, FILL["yscale", HEADS - 1, 1] + 1)
                    sp.dma_start(WST[:, :, :], ws).then_inc(s_gw, 16)
                    sp.dma_start(BB[:, :, :], bs).then_inc(s_gw, 16)
            for e in range(2):
                sp.wait_ge(s_catl[e], 8)
            with sp.Fori(0, NIT - 1) as it:
                ffn(FFN[1], it, W2R2, True)
            ffn(FFN[1], NIT - 1, W2R2, False)
            for b in range(2):
                for k in range(0, KT, 2):
                    sp.wait_ge(s_hf, 8 * J[3, b + 1] + k + 2)
                    sp.dma_start(out.rearrange("(k p) t -> p k t", p=P)[:, k:k + 2, b * TB:(b + 1) * TB],
                                 OUT[b][:, k:k + 2, :]).then_inc(s_out, 16)
            sp.wait_ge(s_out, 16 * KT)

        @block.gpsimd
        def _(pool):
            pool.memset(NEGH[:, :], -0.5).then_inc(s_w2lo, 1)

            def low(u):
                unit_low(u % 2, u + 1)

            def unit_low(slot, count):
                pool.wait_ge(s_hi, count)
                pool.tensor_tensor(WL[:, slot], WR[:, slot], WH[:, slot].bitcast(F32),
                                   ALU.subtract).then_inc(s_lo[slot], 1)

            def power(dst, src, ready, count, done):
                pool.wait_ge(ready, count)
                n = src.shape[-1]
                pool.tensor_tensor(dst, src, NEGH[:, 0:n], ALU.pow).then_inc(done, 1)

            def norm_rsqrt(place, b):
                j, n = J[place, b], BLOCKS[b][2]
                power(RS[:, 0:n // P], MS[:, 0:n // P], s_ms, j + 1, s_rs)

            def norm_low(place, b):
                n, (_, hh, hl), hf = BLOCKS[b][2], streams(b), NB[place][3]
                j = J[place, b]
                for k in range(KT):
                    pool.wait_ge(s_hh, 8 * j + k + 1)
                    pool.tensor_tensor(tokens(hl, b)(k), hf[k % 4][:, 0:n], tokens(hh, b)(k).bitcast(F32),
                                       ALU.subtract).then_inc(s_hl, 1)

            pool.wait_ge(s_w2lo, 1)
            norm_rsqrt(0, 0)
            norm_rsqrt(0, 1)
            norm_rsqrt(0, 2)
            norm_low(0, 0)
            low(U_FFN1)
            norm_low(0, 1)
            low(U_FFN1 + 1)
            norm_low(0, 2)

            def ffn(f, it, w2r, w2h, w2l, prefetch, last=False):
                for j in range(2):
                    pool.wait_ge(s_w2hi, f["v"] + 2 * it + j + 1)
                    pool.tensor_tensor(w2l[:, j], w2r[:, :], w2h[:, j].bitcast(F32),
                                       ALU.subtract).then_inc(s_w2lo, 1)
                for j in range(f["per"] if prefetch else 0):
                    unit_low(j % 2, f["unit"] + f["per"] * it + 3 + j)

            with pool.Fori(0, NIT) as it:
                ffn(FFN[0], it, W2R1, W2H1, W2L1, True)
            norm_rsqrt(1, 0)
            norm_low(1, 0)
            norm_rsqrt(1, 1)
            low(U_MIX + 2)
            low(U_MIX + 3)
            norm_low(1, 1)
            norm_rsqrt(1, 2)
            low(U_MIX + 4)
            norm_low(1, 2)

            def decay_queries(h, d):
                hh = h % 2
                q = QF[:, hh, :].rearrange("p (c t) -> p c t", c=NCH)
                if d == 0:
                    pool.wait_ge(s_rope_done, 8 * (h // 2 + 1))
                    pool.wait_ge(s_fill, FILL["state0", 1, 0] + 1)
                    dst = RET[:, h, :].rearrange("p (c t) -> p c t", c=NCH)
                else:
                    pool.wait_ge(s_fill, FILL["score", h, 1] + 1)
                    pool.wait_ge(s_q, 2 * h + 1)
                    dst = q
                pool.tensor_tensor(dst, q, XI[:, 4 * d + h, :].unsqueeze(1).to_broadcast([P, NCH, P]),
                                   ALU.mult).then_inc(s_q, 1)

            def cat_low(n):
                k, t0 = n % 8, n // 8 * TB
                pool.wait_ge(s_cath, n + 1)
                src = RET[:, k, t0:t0 + TB] if k < 4 else GM[:, k - 4, t0:t0 + TB]
                pool.tensor_tensor(HL[:, k, t0:t0 + TB], src, HH[:, k, t0:t0 + TB].bitcast(F32),
                                   ALU.subtract).then_inc(s_catl[0], 1)

            pool.wait_ge(s_exp, 17)
            for n, (i, name, a, b) in enumerate(FILLS):
                if n == FIRST_FILL[i] and i >= 4:
                    low(U_MIX + i + 1)
                if (name, b) == ("kt", 0):
                    decay_queries(a, 0)
                if (name, b) == ("score", 1) and a % 2 == 0:
                    decay_queries(a, 1)
                if name == "ysum":
                    power(RS[:, 8:16], MS[:, 8:16], s_ym, a + 1, s_yr)
                    if a % 2 == 0:
                        decay_queries(a + 1, 1)
                if (name, b) == ("vg", 3):
                    power(RS[:, 16:32], MS[:, 16:32], s_lv, a + 1, s_lr)
                if (name, a, b) == ("mixed", GROUPS - 1, 0):
                    for m in range(0, 8, 2):
                        cat_low(m)
                if (name, a, b) == ("mixed", GROUPS - 1, 1):
                    for m in range(8, 16, 2):
                        cat_low(m)
                if (name, a, b) == ("out", 1, 1):
                    norm_rsqrt(2, 1)
                if (name, a, b) == ("out", 1, 3):
                    norm_low(2, 1)
            low(U_FFN2 + 1)
            norm_rsqrt(2, 2)
            norm_low(2, 2)
            with pool.Fori(0, NIT - 1) as it:
                ffn(FFN[1], it, W2R2, W2H2, W2L2, True)
            ffn(FFN[1], NIT - 1, W2R2, W2H2, W2L2, False)
            for b in (1, 2):
                norm_rsqrt(3, b)

        @block.scalar
        def _(act):
            def high(slot, raw_count):
                act.wait_ge(s_raw[slot], raw_count)
                act.activation(WH[:, slot], WR[:, slot], ACT.Copy).then_inc(s_hi, 1)

            def mix_high(i):
                if i >= 2:
                    act.wait_ge(s_fill, LAST_FILL[i - 2] + 1)
                u = U_MIX + i
                high(u % 2, 16 * (u // 2 + 1))

            def square(place, b, k):
                n, (xs, _, _) = BLOCKS[b][2], streams(b)
                j = J[place, b]
                if 8 * j + k >= 2:
                    act.wait_ge(s_acc, 8 * j + k - 1)
                act.activation(NB[place][0][:, k % 2, 0:n], tokens(xs, b)(k), ACT.Square).then_inc(s_sq, 1)

            def norm_high(place, b):
                n, (_, hh, _) = BLOCKS[b][2], streams(b)
                j = J[place, b]
                for k in range(KT):
                    act.wait_ge(s_hf, 8 * j + k + 1)
                    act.activation(tokens(hh, b)(k), NB[place][3][k % 4][:, 0:n], ACT.Copy).then_inc(s_hh, 1)

            act.wait_ge(s_const, 16 * 8)
            act.activation(LG[:, :], LG[:, :], ACT.Exp).then_inc(s_exp, 1)
            act.wait_ge(s_lg, 1)
            for dh in range(8):
                act.activation(Z[:, dh, :], IDX[:, :], ACT.Exp, scale=LG[:, dh:dh + 1]).then_inc(s_exp, 1)
            act.activation(CS[:, :, :], CIN[:, :, :], ACT.Silu).then_inc(s_cv, 1)
            act.wait_ge(s_set, 1)
            act.wait_ge(s_cv, 1)
            act.activation(CV[:, 0:4 * KT].rearrange("p (k c) -> p k c", c=4)[:, :, 0:2], CS[:, :, :],
                           ACT.Copy).then_inc(s_cv, 1)
            for b in range(3):
                act.wait_ge(s_x[b], 16)
                for k in range(KT):
                    square(0, b, k)
            for slot in range(2):
                high(slot, 16)
            for b in range(3):
                norm_high(0, b)

            def off(f, i):
                s, t0, _ = f["blocks"][i % f["T"]]
                return SEQ if s else t0

            def ffn(f, it, ph, w2r, w2h, prefetch):
                nsteps = 2 * f["T"]
                for i in range(nsteps):
                    n = f["step"] + nsteps * it + i
                    ft, (_, t0, nt) = i // f["T"], f["blocks"][i % f["T"]]
                    act.wait_ge(s_gu, n + 1)
                    act.activation(SG[:, i % 2, 0:nt], PS[2 * (i % 2)][:, 0:nt], ACT.Silu).then_inc(s_silu, 1)
                    act.wait_ge(s_prod, n + 3)
                    act.activation(ph[:, ft, off(f, i):off(f, i) + nt], PR[:, i % 2, 0:nt],
                                   ACT.Copy).then_inc(s_ph, 1)
                    if i < 2:
                        if i == 0:
                            act.wait_ge(s_yd, f["y"] + 8 * f["T"] * it + 2)
                        act.wait_ge(s_w2raw, 16 * (f["v"] + i + 1) + 32 * it)
                        act.activation(w2h[:, i], w2r[:, :], ACT.Copy).then_inc(s_w2hi, 1)
                    if i == f["T"] - 1 and prefetch:
                        high(0, 8 * (f["unit"] + 2) + 16 + 8 * f["per"] * it)
                if prefetch:
                    high(1, 8 * (f["unit"] + 2) + 16 + 8 * f["per"] * it)

            def ffn1_next(it, j):
                act.wait_ge(s_ada, ADA_FIRST + 2 * it + j + 1)
                high(j, 8 * (U_FFN1 + 4) + 16 + 32 * it)

            def down_squares(f, place, t):
                for k in range(KT):
                    act.wait_ge(s_yd, f["y"] + 8 * f["T"] * (NIT - 1) + 8 * t + k + 3)
                    square(place, t + 3 - f["T"], k)

            with act.Fori(0, NIT - 1) as it:
                ffn(FFN[0], it, PH1, W2R1, W2H1, True)
                ffn1_next(it, 0)
                ffn1_next(it, 1)
            ffn(FFN[0], NIT - 1, PH1, W2R1, W2H1, True)
            ffn1_next(NIT - 1, 0)
            down_squares(FFN[0], 1, 0)
            ffn1_next(NIT - 1, 1)
            norm_high(1, 0)
            down_squares(FFN[0], 1, 1)
            mix_high(2)
            down_squares(FFN[0], 1, 2)
            mix_high(3)
            norm_high(1, 1)
            mix_high(4)
            norm_high(1, 2)

            act.wait_ge(s_cst, 16)
            for dh in range(8):
                c0 = C_XIF if dh < 4 else C_XIB
                act.activation(XI[:, dh, :], CST[:, c0:c0 + P], ACT.Exp, scale=LG[:, dh:dh + 1]).then_inc(s_exp, 1)
            for h in range(HEADS):
                for d in range(2):
                    if h:
                        act.wait_ge(s_dec, h)
                    act.activation(DT[:, d, :], CST[:, C_ABS:C_ABS + P], ACT.Exp,
                                   scale=LG[:, 4 * d + h:4 * d + h + 1]).then_inc(s_exp, 1)

            n_gate = 0
            for n, (i, name, a, b) in enumerate(FILLS):
                ps, free = PS[n % NRING], s_free[n % NRING]
                if n == FIRST_FILL[i] and i >= 4:
                    mix_high(i + 1)
                if name in ("cv", "state0", "v", "vg", "kt", "o", "g", "u"):
                    act.wait_ge(s_fill, n + 1)
                if name == "cv":
                    act.activation(VC[:, :, a * UC:(a + 1) * UC], ps[:, :].rearrange("p (b c) -> p b c", b=2),
                                   ACT.Copy).then_inc(free, 1)
                elif name == "state0":
                    act.activation(S0[:, a, :, :], ps[:, :].rearrange("p (h v) -> p h v", h=HEADS),
                                   ACT.Copy).then_inc(free, 1)
                elif name in ("v", "vg"):
                    dst = V2 if (name, a) == ("vg", 1) else V
                    act.activation(dst[:, 2 * b:2 * b + 2, :], ps[:, :].rearrange("p (b c) -> p b c", b=2),
                                   ACT.Copy if name == "v" else ACT.Gelu_apprx_tanh).then_inc(free, 1)
                elif name == "kt":
                    for d in range(2):
                        act.activation(KZ[d][:, 4 * b:4 * b + 4, :], ps[:, :].rearrange("p (c d) -> p c d", c=4),
                                       ACT.Copy, scale=Z[:, 4 * d + a, Z_LAT[d]:Z_LAT[d] + 1]).then_inc(free if d else s_kz, 1)
                elif name == "o":
                    act.activation(RET[:, a, b * TB:(b + 1) * TB], ps[:, :], ACT.Copy).then_inc(s_oc, 1)
                    act.activation(KF[:, a % 2, b * TB:(b + 1) * TB], ps[:, :], ACT.Square).then_inc(free, 1)
                elif name in ("g", "u"):
                    if n_gate >= 2:
                        act.wait_ge(s_cat, n_gate - 1)
                    act.activation(GU[:, n_gate % 2, :], ps[:, :],
                                   ACT.Silu if name == "g" else ACT.Gelu_apprx_tanh).then_inc(free, 1)
                    n_gate += 1
                if name == "mixed" and a == GROUPS - 1:
                    act.wait_ge(s_fill, n)
                    act.wait_ge(s_cat, 14 + 2 * b)
                    t0 = b * TB
                    for k in range(KT):
                        src = RET[:, k, t0:t0 + TB] if k < 4 else GM[:, k - 4, t0:t0 + TB]
                        act.activation(HH[:, k, t0:t0 + TB], src, ACT.Copy).then_inc(s_cath, 1)
                if name == "out" and n > FILL["out", 0, 0]:
                    m = n - FILL["out", 0, 0] - 1
                    act.wait_ge(*release(n - 1))
                    square(2, 1 + m // 8, m % 8)
                if (name, a, b) == ("out", 1, 3):
                    norm_high(2, 1)
            mix_high(len(MIX_UNITS) + 1)
            act.wait_ge(*release(len(FILLS) - 1))
            square(2, 2, 7)
            norm_high(2, 2)
            with act.Fori(0, NIT - 1) as it:
                ffn(FFN[1], it, PH2, W2R2, W2H2, True)
            ffn(FFN[1], NIT - 1, PH2, W2R2, W2H2, False)
            down_squares(FFN[1], 3, 0)
            down_squares(FFN[1], 3, 1)

        @block.vector
        def _(dve):
            chain = [0]

            def link(ins):
                chain[0] += 1
                ins.then_inc(s_chain, 1)
                dve.wait_ge(s_chain, chain[0])

            link(dve.memset(ONES[:, :], 1.0))
            dve.memset(CV[:, :].bitcast(F32), 0.0).then_inc(s_set, 1)
            dve.memset(MS[:, :], 0.0).then_inc(s_prod, 2)
            dve.memset(RS[:, :], 0.0).then_inc(s_pl, 2)
            dve.memset(A4[:, :, :], 0.0).then_inc(s_yd, 2)
            dve.wait_ge(s_exp, 1)
            dve.tensor_scalar(LG[:, :], LG[:, :], -1.0, None, ALU.mult).then_inc(s_lg, 1)
            dve.wait_ge(s_cv, 2)
            dve.tensor_tensor(CV[:, 0:4 * KT].rearrange("p (k c) -> p k c", c=4)[:, :, 2:4], CS[:, :, :],
                              CV[:, 0:4 * KT].rearrange("p (k c) -> p k c", c=4)[:, :, 0:2].bitcast(F32),
                              ALU.subtract).then_inc(s_cv, 1)

            def add_square(place, b, k):
                n, j = BLOCKS[b][2], J[place, b]
                sq, acc = NB[place][0], NB[place][1]
                dve.wait_ge(s_sq, 8 * j + k + 1)
                if k == 0:
                    if j:
                        dve.wait_ge(s_st, j)
                    ins = dve.tensor_copy(acc[:, 0:n], sq[:, 0, 0:n])
                else:
                    dve.wait_ge(s_acc, 8 * j + k)
                    ins = dve.tensor_tensor(acc[:, 0:n], acc[:, 0:n], sq[:, k % 2, 0:n], ALU.add)
                ins.then_inc(s_acc, 1)

            def add_squares(place, b):
                for k in range(KT):
                    add_square(place, b, k)

            def norm_mean(place, b):
                nb, j = BLOCKS[b][2] // P, J[place, b]
                dve.wait_ge(s_st, j + 1)
                dve.tensor_scalar(MS[:, 0:nb], ST_BANK[:, 0:nb], 1.0 / D, EPS, ALU.mult, ALU.add).then_inc(s_ms, 1)

            def diagonal(nb, rs, dst):
                return dve.tensor_tensor(dst, ID[:, :].unsqueeze(1).to_broadcast([P, nb, P]),
                                         rs.unsqueeze(2).to_broadcast([P, nb, P]), ALU.mult)

            def norm_diagonal(place, b):
                nb, j = BLOCKS[b][2] // P, J[place, b]
                dve.wait_ge(s_rs, j + 1)
                if j:
                    dve.wait_ge(s_rb, j)
                diagonal(nb, RS[:, 0:nb], NB[place][2][:, 0:nb, :]).then_inc(s_dg, 1)

            def scaled(place, b, k):
                n, j = BLOCKS[b][2], J[place, b]
                if 8 * j + k >= 4:
                    dve.wait_ge(s_hl, 8 * j + k - 3)
                dve.tensor_tensor(NB[place][3][k % 4][:, 0:n], tokens(streams(b)[0], b)(k), RB_BANK[:, 0:n],
                                  ALU.mult).then_inc(s_xm, 1)

            def modulated(place, b, k):
                s, _, n = BLOCKS[b]
                j, hf = J[place, b], NB[place][3][k % 4]
                dve.wait_ge(s_xm, 8 * j + k + 1)
                dve.tensor_scalar(hf[:, 0:n], hf[:, 0:n], GAIN[:, place, k, s:s + 1],
                                  MODS[:, 3 * place * KT + k, s:s + 1], ALU.mult, ALU.add).then_inc(s_hf, 1)

            def norm_apply(place, b):
                j = J[place, b]
                dve.wait_ge(s_rb, j + 1)
                for k in range(KT + 1):
                    if k < KT:
                        scaled(place, b, k)
                    if k:
                        modulated(place, b, k - 1)

            def norm_out(b):
                dve.wait_ge(s_rb, J[3, b] + 1)
                for k in range(KT):
                    dve.scalar_tensor_tensor(OUT[b - 1][:, k, :], tokens(X, b)(k), FG[:, k:k + 1],
                                             RB_BANK[:, :], ALU.mult, ALU.mult).then_inc(s_hf, 1)

            def ada_rows(a, slot, bank, rows=4):
                dve.wait_ge(s_ada, a + 1)
                dve.tensor_copy(A4[0:rows, slot, :], PS[bank][0:rows, 0:UC]).then_inc(s_a4, 1)

            def ada_mods(a, bank):
                dve.wait_ge(s_col, a + 1)
                dst, b = MODS[:, bass.ts(a, 2), :], BA[:, bass.ts(a, 2), :]
                dve.tensor_tensor(dst, PS[bank][:, UC:UC + 4].rearrange("p (t s) -> p t s", t=2), b,
                                  ALU.add).then_inc(s_mods, 1)

            def gain(place):
                dve.wait_ge(s_mods, 4 * (3 * place + 2))
                c = (3 * place + 1) * KT
                dve.scalar_tensor_tensor(GAIN[:, place], MODS[:, c:c + KT, :], 1.0,
                                         NG[:, place, :].unsqueeze(2).to_broadcast([P, KT, 2]),
                                         ALU.add, ALU.mult).then_inc(s_coef, 1)

            def gate(place):
                dve.wait_ge(s_mods, 4 * (3 * place + 3))
                c = (3 * place + 2) * KT
                dve.tensor_scalar(GATE[:, place], MODS[:, c:c + KT, :], 1.0 if place == 1 else 0.5, None,
                                  ALU.mult).then_inc(s_coef, 1)

            def first_rows(*units):
                for a in units:
                    ada_rows(a, a % 2, a % 4, 2)

            def first_mods(*units):
                for a in units:
                    ada_mods(a, a % 4)

            add_squares(0, 0)
            first_rows(0, 1)
            first_mods(0)
            norm_mean(0, 0)
            norm_diagonal(0, 0)
            add_squares(0, 1)
            for a in (2, 3, 4):
                first_rows(a)
                first_mods(a - 1)
            norm_mean(0, 1)
            norm_diagonal(0, 1)
            add_squares(0, 2)
            for a in (5, 6, 7):
                first_rows(a)
                first_mods(a - 1)
            first_mods(7)
            norm_mean(0, 2)
            gain(0)
            dve.wait_ge(s_coef, 1)
            norm_apply(0, 0)
            first_rows(8)
            first_mods(8)
            first_rows(9)
            first_mods(9)
            norm_apply(0, 1)
            norm_diagonal(0, 2)
            first_rows(10, 11)
            first_mods(10, 11)
            gate(0)
            first_rows(12, 13)
            first_mods(12, 13)
            norm_apply(0, 2)

            def ffn(f, it, ph, pl, last=False):
                nsteps = 2 * f["T"]
                for i in range(nsteps):
                    n = f["step"] + nsteps * it + i
                    s, t0, nt = f["blocks"][i % f["T"]]
                    o = SEQ if s else t0
                    ft = i // f["T"]
                    dve.wait_ge(s_silu, n + 1)
                    dve.wait_ge(s_pl, n + 2)
                    dve.tensor_tensor(PR[:, i % 2, 0:nt], SG[:, i % 2, 0:nt], PS[2 * (i % 2) + 1][:, 0:nt],
                                      ALU.mult).then_inc(s_prod, 1)
                    dve.wait_ge(s_ph, n + 1)
                    dve.tensor_tensor(pl[:, ft, o:o + nt], PR[:, i % 2, 0:nt], ph[:, ft, o:o + nt].bitcast(F32),
                                      ALU.subtract).then_inc(s_pl, 1)
                first = f["per"] == 4
                a = ADA_FIRST + 2 * it
                if first:
                    ada_rows(a, 0, 6)
                place = 0 if first else 2
                at_next = place + 1
                for t in range(f["T"]):
                    s, t0, nt = f["blocks"][t]
                    xs = XC if s else X
                    b = t + 3 - f["T"]
                    for k in range(KT):
                        dve.wait_ge(s_y, f["y"] + 8 * f["T"] * it + 8 * t + k + 1)
                        xv = xs[:, k, t0:t0 + nt]
                        dve.scalar_tensor_tensor(xv, PS[4 + k % 2][:, 0:nt], GATE[:, place, k, s:s + 1], xv,
                                                 ALU.mult, ALU.add).then_inc(s_yd, 1)
                        if not last:
                            continue
                        if t == 0 and k >= 2:
                            add_square(at_next, b, k - 2)
                        if t == 1:
                            if k < 2:
                                add_square(at_next, b - 1, KT - 2 + k)
                            if k == 3:
                                norm_mean(at_next, b - 1)
                            if k == 5:
                                norm_diagonal(at_next, b - 1)
                            if k >= 3 and not first:
                                add_square(at_next, b, k - 3)
                        if t == 2:
                            if k == 0:
                                dve.wait_ge(s_rb, J[1, 0] + 1)
                            else:
                                modulated(1, 0, k - 1)
                            scaled(1, 0, k)
                    if first and t == 0:
                        ada_mods(a, 6)
                    if first and t == (0 if last else 1):
                        ada_rows(a + 1, 1, 7)
                    if first and t == (1 if last else 2):
                        ada_mods(a + 1, 7)

            with dve.Fori(0, NIT - 1) as it:
                ffn(FFN[0], it, PH1, PL1)
            gain(1)
            gain(2)
            dve.wait_ge(s_coef, 4)
            ffn(FFN[0], NIT - 1, PH1, PL1, last=True)
            modulated(1, 0, KT - 1)
            add_squares(1, 1)
            norm_mean(1, 1)
            norm_diagonal(1, 1)
            add_squares(1, 2)
            norm_apply(1, 1)
            norm_mean(1, 2)
            norm_diagonal(1, 2)
            norm_apply(1, 2)
            gate(1)
            gate(2)
            dve.wait_ge(s_coef, 6)

            def masks():
                for h in range(HEADS):
                    dve.wait_ge(s_exp, 17 + 2 * h + 2)
                    link(dve.tensor_tensor(DM[:, h, :], DT[:, 0, :], CST[:, C_LOW:C_LOW + P], ALU.mult))
                    link(dve.tensor_tensor(DT[:, 0, :], DT[:, 1, :], CST[:, C_UP:C_UP + P], ALU.mult))
                    dve.tensor_tensor(DM[:, h, :], DM[:, h, :], DT[:, 0, :], ALU.add).then_inc(s_dec, 1)

            def read(*key):
                dve.wait_ge(*release(FILL[key]))

            n_rope = n_gate = 0
            for n, (i, name, a, b) in enumerate(FILLS):
                ps, free = PS[n % NRING], s_free[n % NRING]
                four = ps[:, :].rearrange("p (c t) -> p c t", c=4)
                cols = slice(b * TB, (b + 1) * TB)
                if name in ("ck", "k", "q", "score", "ub", "ysum", "yscale", "mixed", "out"):
                    dve.wait_ge(s_fill, n + 1)
                if name == "ck":
                    for tb in range(2):
                        for hh in range(2):
                            for d in range(2):
                                h = 2 * a + hh
                                z = Z_CTX[d][tb]
                                ins = dve.tensor_scalar(KC[:, d, tb, h, :], ps[:, tb * UC + hh * P:tb * UC + hh * P + P],
                                                        Z[:, 4 * d + h, z:z + 1], K_SCALE, ALU.mult, ALU.mult)
                    ins.then_inc(free, 1)
                    if a == 1:
                        masks()
                        dve.wait_ge(s_rope, 32)
                        dve.wait_ge(s_hl, 8 * (J[1, 2] + 1))
                elif name in ("k", "q"):
                    dst = (KF if name == "k" else QF)[:, a % 2, cols]
                    tmp = TMP[:, 0, :]
                    scale = K_SCALE if name == "k" else 1.0
                    if n_rope:
                        dve.wait_ge(s_rope_done, n_rope)
                    dve.scalar_tensor_tensor(tmp[0:64], ps[64:P, :], scale, SIN[64:P, cols], ALU.mult, ALU.mult)
                    dve.scalar_tensor_tensor(tmp[64:P], ps[0:64, :], scale, SIN[0:64, cols], ALU.mult, ALU.mult)
                    dve.scalar_tensor_tensor(dst, ps[:, :], scale, COS[:, cols], ALU.mult, ALU.mult).then_inc(free, 1)
                    dve.wait_ge(*release(n))
                    dve.tensor_tensor(dst, dst, tmp, ALU.add).then_inc(s_rope_done, 1)
                    n_rope += 1
                elif name == "score":
                    dve.tensor_tensor(PM[:, 4 * b:4 * b + 4, :], four, DM[:, a, :].unsqueeze(1).to_broadcast([P, 4, P]),
                                      ALU.mult).then_inc(free, 1)
                elif (name, b) == ("ub", 1):
                    read("state0", 0, 0)
                    read("state0", 1, 0)
                    for step in range(NCH - 1):
                        for d in range(2):
                            c = step if d == 0 else NCH - 1 - step
                            bank = PS[FILL["uf" if d == 0 else "ub", a, c // 4] % NRING]
                            before = KZ[d][:, c, :]
                            if step == 0:
                                before = S0[:, d, a, :]
                            else:
                                dve.wait_ge(s_state, 14 * a + 2 * (step - 1) + d + 1)
                            z = Z[:, 4 * d + a, Z_CHUNK:Z_CHUNK + 1]
                            dve.scalar_tensor_tensor(KZ[d][:, c + 1 - 2 * d, :], before, z,
                                                     bank[:, (c % 4) * P:(c % 4 + 1) * P],
                                                     ALU.mult, ALU.add).then_inc(s_state, 1)
                elif name == "ysum":
                    dve.tensor_scalar(MS[:, 8:16], ps[:, 0:8], 1.0 / P, EPS, ALU.mult, ALU.add).then_inc(s_ym, 1)
                    dve.wait_ge(s_yr, a + 1)
                    for j, dg in enumerate((TMP[:, 1, :].rearrange("p (b t) -> p b t", b=4), DG2[:, :, :])):
                        if a:
                            dve.wait_ge(s_fill, FILL["yscale", a - 1, j] + 1)
                        diagonal(4, RS[:, 8 + 4 * j:12 + 4 * j], dg).then_inc(s_yg, 1)
                elif name == "yscale":
                    dve.wait_ge(s_oc, 2 * a + b + 1)
                    r = RET[:, a, cols]
                    dve.tensor_tensor(r, r, ps[:, :], ALU.mult).then_inc(free, 1)
                elif name == "g":
                    read("g", a, b)
                    r = RET[:, a, cols]
                    dve.tensor_tensor(r, r, GU[:, n_gate % 2, :], ALU.mult).then_inc(s_cat, 1)
                    n_gate += 1
                elif name == "vg":
                    read("vg", a, b)
                    v = V2 if a else V
                    tiles = [(c, g) for c in (2 * b, 2 * b + 1) for g in range(2)]
                    for c, g in tiles:
                        ins = dve.bn_stats(BST[:, 2 * c + g, :], v[:, c, g * P:(g + 1) * P])
                    link(ins)
                    for c, g in tiles:
                        ins = dve.bn_aggr(MV[:, 2 * c + g, :], BST[:, 2 * c + g, :])
                    link(ins)
                    if b == 3:
                        dve.tensor_scalar(MS[:, 16:32], MV[:, :, 1], EPS, None, ALU.add).then_inc(s_lv, 1)
                        dve.wait_ge(s_lr, a + 1)
                        for c in range(NCH):
                            for g in range(2):
                                m = 2 * c + g
                                tile = v[:, c, g * P:(g + 1) * P]
                                ins = dve.tensor_scalar(tile, tile, MV[:, m, 0:1], RS[:, 16 + m:17 + m],
                                                        ALU.subtract, ALU.mult)
                        ins.then_inc(s_vn, 1)
                elif name == "mixed":
                    dve.wait_ge(s_gw, 32)
                    m = n_gate % 2
                    dve.tensor_tensor(MIXD[:, m, :].rearrange("p (c t) -> p c t", c=4), four,
                                      BB[:, a, :].unsqueeze(1).to_broadcast([P, 4, P]), ALU.add).then_inc(s_mx, 1)
                    dve.wait_ge(*release(n))
                    read("u", a, b)
                    dve.tensor_tensor(GM[:, a, cols], MIXD[:, m, :], GU[:, m, :], ALU.mult).then_inc(s_cat, 1)
                    n_gate += 1
                    if a == GROUPS - 1:
                        for k in range(1, KT, 2):
                            dve.wait_ge(s_cath, 8 * b + k + 1)
                            src = RET[:, k, cols] if k < 4 else GM[:, k - 4, cols]
                            dve.tensor_tensor(HL[:, k, cols], src, HH[:, k, cols].bitcast(F32),
                                              ALU.subtract).then_inc(s_catl[1], 1)
                elif name == "out":
                    xv = X[:, b, a * TB:(a + 1) * TB]
                    dve.scalar_tensor_tensor(xv, ps[:, :], GATE[:, 1, b, 0:1], xv, ALU.mult, ALU.add).then_inc(free, 1)
                    m = n - FILL["out", 0, 0] - 1
                    if m >= 0:
                        add_square(2, 1 + m // 8, m % 8)
                    if (a, b) == (1, 1):
                        norm_mean(2, 1)
                        norm_diagonal(2, 1)
                    if (a, b) == (1, 3):
                        norm_apply(2, 1)
            add_square(2, 2, KT - 1)
            norm_mean(2, 2)
            norm_diagonal(2, 2)
            norm_apply(2, 2)
            with dve.Fori(0, NIT - 1) as it:
                ffn(FFN[1], it, PH2, PL2)
            ffn(FFN[1], NIT - 1, PH2, PL2, last=True)
            for k in range(KT - 3, KT):
                add_square(3, 2, k)
            norm_out(1)
            norm_mean(3, 2)
            norm_diagonal(3, 2)
            norm_out(2)

        @block.tensor
        def _(pe):
            def mm3(dst, wh, wl, xh, xl, first, last):
                pe.matmul(dst, wh, xh, start=first, stop=False)
                pe.matmul(dst, wh, xl, start=False, stop=False)
                return pe.matmul(dst, wl, xh, start=False, stop=last)

            def norm_sum(place, b):
                j, n, acc = J[place, b], BLOCKS[b][2], NB[place][1]
                pe.wait_ge(s_acc, 8 * (j + 1))
                if j:
                    pe.wait_ge(s_ms, j)
                for c in range(n // P):
                    ins = pe.matmul(ST_BANK[:, c:c + 1], acc[:, c * P:(c + 1) * P], ONES[:, 0:1], start=True, stop=True)
                ins.then_inc(s_st, 1)

            def norm_scale(place, b):
                j, n = J[place, b], BLOCKS[b][2]
                pe.wait_ge(s_dg, j + 1)
                if j:
                    pe.wait_ge(s_hf, 8 * j)
                pe.matmul(RB_BANK[:, 0:n], ONES[:, :], NB[place][2][:, 0:n // P, :], start=True, stop=True).then_inc(s_rb, 1)

            def ada_product(a, slot, bank, count):
                pe.wait_ge(s_lo[slot], count)
                for k in range(KT):
                    for w in (WH, WL):
                        ins = pe.matmul(PS[bank][:, 0:UC], CV[:, 4 * k:4 * k + P], w[:, slot, k, :],
                                        start=(k == 0 and w is WH), stop=(k == KT - 1 and w is WL))
                ins.then_inc(s_ada, 1)

            def ada_columns(a, slot, bank, rows=4):
                pe.wait_ge(s_a4, a + 1)
                add = SEL[:, :] if rows == 4 else ID[0:2, 0:2]
                for t in range(2):
                    ins = pe.matmul(PS[bank][:, UC + 2 * t:UC + 2 * t + 2], A4[0:rows, slot, t * P:(t + 1) * P], add,
                                    start=True, stop=True)
                ins.then_inc(s_col, 1)

            def first_product(a):
                pe.wait_ge(s_first[a % 3], 16 * (a // 3 + 1))
                if a >= 4:
                    pe.wait_ge(s_mods, a - 3)
                for k in range(KT):
                    ins = pe.matmul(PS[a % 4][0:2, 0:UC], CS[:, k, :], WS[:, a % 3, k, :], start=(k == 0), stop=(k == KT - 1))
                ins.then_inc(s_ada, 1)

            def first_columns(a):
                ada_columns(a, a % 2, a % 4, 2)

            pe.wait_ge(s_const, 16 * 8)
            pe.wait_ge(s_cv, 3)
            first_product(0)
            first_product(1)
            first_columns(0)
            norm_sum(0, 0)
            for a in (2, 3, 4):
                first_product(a)
                first_columns(a - 1)
                if a == 2:
                    norm_scale(0, 0)
            norm_sum(0, 1)
            for a in (5, 6, 7):
                first_product(a)
                first_columns(a - 1)
            first_columns(7)
            norm_sum(0, 2)
            first_product(8)
            first_columns(8)
            first_product(9)
            first_columns(9)
            norm_scale(0, 1)
            first_product(10)
            first_product(11)
            norm_scale(0, 2)
            first_columns(10)
            first_columns(11)
            first_product(12)
            first_product(13)
            first_columns(12)
            first_columns(13)
            pe.wait_ge(s_mods, ADA_FIRST)

            def ffn(f, it, ph, pl, w2h, w2l, last=False):
                T, first = f["T"], f["per"] == 4
                for i in range(2 * T):
                    n = f["step"] + 2 * T * it + i
                    ft, (s, t0, nt) = i // T, f["blocks"][i % T]
                    xh, xl = (HCH, HCL) if s else (HH, HL)
                    if i % T == 0:
                        pe.wait_ge(s_lo[ft], f["unit"] // 2 + (f["per"] // 2) * it + 1)
                    pe.wait_ge(s_hl, 8 * (J[0 if first else 2, i % T + 3 - T] + 1))
                    pe.wait_ge(s_prod, n + 1)
                    for half in range(2):
                        for k in range(KT):
                            cols = slice(half * P, (half + 1) * P)
                            ins = mm3(PS[2 * (i % 2) + half][:, 0:nt], WH[:, ft, k, cols], WL[:, ft, k, cols],
                                      xh[:, k, t0:t0 + nt], xl[:, k, t0:t0 + nt], k == 0, k == KT - 1)
                    ins.then_inc(s_gu, 1)
                a = ADA_FIRST + 2 * it
                if first:
                    pe.wait_ge(s_mods, ADA_FIRST + 2 * it)
                    ada_product(a, 0, 6, f["unit"] // 2 + 2 * it + 2)
                for t in range(T):
                    s, t0, nt = f["blocks"][t]
                    b = t + 3 - T
                    o = SEQ if s else t0
                    pe.wait_ge(s_pl, f["step"] + 2 * T * it + T + t + 3)
                    pe.wait_ge(s_w2lo, f["v"] + 2 * it + 3)
                    for d in range(KT):
                        pe.wait_ge(s_yd, f["y"] + 8 * T * it + 8 * t + d + 1)
                        for ft in range(2):
                            cols = slice(d * P, (d + 1) * P)
                            ins = mm3(PS[4 + d % 2][:, 0:nt], w2h[:, ft, cols], w2l[:, ft, cols],
                                      ph[:, ft, o:o + nt], pl[:, ft, o:o + nt], ft == 0, ft == 1)
                        ins.then_inc(s_y, 1)
                        if last and (t, d) == (1, 2):
                            norm_sum(1 if first else 3, b - 1)
                        if last and (t, d) == (1, 6):
                            norm_scale(1 if first else 3, b - 1)
                    if first and t == 0:
                        ada_columns(a, 0, 6)
                    if first and t == (0 if last else 1):
                        ada_product(a + 1, 1, 7, f["unit"] // 2 + 2 * it + 2)
                    if first and t == (1 if last else 2):
                        ada_columns(a + 1, 1, 7)

            with pe.Fori(0, NIT - 1) as it:
                ffn(FFN[0], it, PH1, PL1, W2H1, W2L1)
            ffn(FFN[0], NIT - 1, PH1, PL1, W2H1, W2L1, last=True)

            pe.wait_ge(s_prod, 6 * NIT + 2)
            pe.wait_ge(s_yd, y_all[0])

            for n, (i, name, a, b) in enumerate(FILLS):
                ps = PS[n % NRING]
                slot = i % 2
                wh, wl = WH[:, slot], WL[:, slot]
                if n == FIRST_FILL[i]:
                    pe.wait_ge(s_lo[slot], (U_MIX + i) // 2 + 1)
                if n >= NRING:
                    pe.wait_ge(*release(n - NRING))
                cols = slice(b * TB, (b + 1) * TB)
                hh = a % 2
                if name in ("ck", "cv"):
                    pe.wait_ge(s_hl, 8 * (J[1, 0] + 1))
                    for tb in range(2):
                        for k in range(KT):
                            t = slice(tb * P, (tb + 1) * P)
                            ins = mm3(ps[:, tb * UC:(tb + 1) * UC], HCH[:, k, t], HCL[:, k, t],
                                      wh[:, k, :], wl[:, k, :], k == 0, k == KT - 1)
                elif name == "state0":
                    for key in (("ck", 0, 0), ("ck", 1, 0), ("cv", 0, 0), ("cv", 1, 0)):
                        pe.wait_ge(*release(FILL[key]))
                    for h in range(HEADS):
                        for tb in range(2):
                            ins = pe.matmul(ps[:, h * P:(h + 1) * P], KC[:, a, tb, h, :],
                                            VC[:, tb, h * P:(h + 1) * P], start=(tb == 0), stop=(tb == 1))
                elif name in ("v", "vg"):
                    for c in range(2):
                        for k in range(KT):
                            t = slice((2 * b + c) * P, (2 * b + c + 1) * P)
                            ins = mm3(ps[:, c * UC:(c + 1) * UC], HH[:, k, t], HL[:, k, t],
                                      wh[:, k, :], wl[:, k, :], k == 0, k == KT - 1)
                elif name in ("k", "q", "g", "u"):
                    pe.wait_ge(s_hl, 8 * (J[1, b + 1] + 1))
                    for k in range(KT):
                        w = slice((a % 2) * P, (a % 2 + 1) * P)
                        ins = mm3(ps[:, :], wh[:, k, w], wl[:, k, w], HH[:, k, cols], HL[:, k, cols],
                                  k == 0, k == KT - 1)
                elif name == "mixed":
                    pe.wait_ge(s_vn, a // 2 + 1)
                    pe.wait_ge(s_gw, 32)
                    v = V2 if a // 2 else V
                    for c in range(4):
                        ins = pe.matmul(ps[:, c * P:(c + 1) * P], v[:, 4 * b + c, hh * P:(hh + 1) * P], WST[:, a, :],
                                        start=True, stop=True)
                elif name == "kt":
                    pe.wait_ge(s_rope_done, 8 * (a // 2 + 1))
                    for c in range(4):
                        t0 = (4 * b + c) * P
                        ins = pe.transpose(ps[:, c * P:(c + 1) * P], KF[:, hh, t0:t0 + P], ID[:, :])
                elif name == "score":
                    for c in range(4):
                        t0 = (4 * b + c) * P
                        ins = pe.matmul(ps[:, c * P:(c + 1) * P], KF[:, hh, t0:t0 + P], QF[:, hh, t0:t0 + P],
                                        start=True, stop=True)
                elif name in ("uf", "ub"):
                    for j in range(4):
                        pe.wait_ge(*release(FILL["v", a // 2, j]))
                    for j in range(2):
                        pe.wait_ge(*release(FILL["kt", a, j]))
                    for c in range(4):
                        m = 4 * b + c
                        ins = pe.matmul(ps[:, c * P:(c + 1) * P], KZ[name == "ub"][:, m, :], V[:, m, hh * P:(hh + 1) * P],
                                        start=True, stop=True)
                elif name == "o":
                    pe.wait_ge(*release(FILL["score", a, b]))
                    chunks = [(c, 4 * b + c, ps[:, c * P:(c + 1) * P]) for c in range(4)]
                    for c, m, dst in chunks:
                        pe.matmul(dst, V[:, m, hh * P:(hh + 1) * P], PM[:, m, :], start=(c == 0), stop=False,
                                  skip_group_check=True)
                    pe.wait_ge(s_q, 2 * a + 1)
                    for c, m, dst in chunks:
                        if m:
                            pe.wait_ge(s_state, 14 * a + 2 * (m - 1) + 1)
                        pe.matmul(dst, KZ[0][:, m, :] if m else S0[:, 0, a, :], RET[:, a, m * P:(m + 1) * P],
                                  start=False, stop=False, skip_group_check=True)
                    pe.wait_ge(s_q, 2 * a + 2)
                    for c, m, dst in reversed(chunks):
                        last = m == NCH - 1
                        if not last:
                            pe.wait_ge(s_state, 14 * a + 2 * (NCH - 2 - m) + 2)
                        ins = pe.matmul(dst, S0[:, 1, a, :] if last else KZ[1][:, m, :], QF[:, hh, m * P:(m + 1) * P],
                                        start=False, stop=True, skip_group_check=True)
                elif name == "ysum":
                    for j in range(2):
                        pe.wait_ge(*release(FILL["o", a, j]))
                    for c in range(NCH):
                        ins = pe.matmul(ps[:, c:c + 1], KF[:, hh, c * P:(c + 1) * P], ONES[:, 0:1], start=True, stop=True)
                elif name == "yscale":
                    pe.wait_ge(s_yg, 2 * a + b + 1)
                    ins = pe.matmul(ps[:, :], ONES[:, :], DG2[:, :, :] if b else TMP[:, 1, :], start=True, stop=True)
                elif name == "out":
                    for k in range(KT):
                        pe.wait_ge(s_catl[k % 2], 4 * a + k // 2 + 1)
                        w = slice(b % 2 * P, (b % 2 + 1) * P)
                        ins = mm3(ps[:, :], wh[:, k, w], wl[:, k, w], HH[:, k, a * TB:(a + 1) * TB],
                                  HL[:, k, a * TB:(a + 1) * TB], k == 0, k == KT - 1)
                ins.then_inc(s_fill, 1)
                if i < 4 and n == FIRST_FILL[i]:
                    (norm_scale if i % 2 else norm_sum)(1, 1 + i // 2)
                if (name, a, b) == ("out", 1, 0):
                    norm_sum(2, 1)
                if (name, a, b) == ("out", 1, 2):
                    norm_scale(2, 1)

            norm_sum(2, 2)
            norm_scale(2, 2)
            for b in range(NRING):
                pe.wait_ge(*release(len(FILLS) - NRING + b))
            with pe.Fori(0, NIT - 1) as it:
                ffn(FFN[1], it, PH2, PL2, W2H2, W2L2)
            ffn(FFN[1], NIT - 1, PH2, PL2, W2H2, W2L2, last=True)
            norm_sum(3, 2)
            norm_scale(3, 2)


def _units(w):
    return w.reshape(KT, P, -1, UC).transpose(2, 1, 0, 3)


def _w1_units(w):
    return w.reshape(KT, P, 2, NF, P).transpose(3, 1, 0, 2, 4).reshape(NF, P, KT, UC)


def _per_feature(v):
    return np.moveaxis(v.reshape(v.shape[:-1] + (-1, P)), -1, 0)


def _tables():
    token = np.arange(SEQ)
    nf = P // 4
    freqs = (np.float32(10000.0) ** (-np.arange(nf, dtype=np.float32) / np.float32(nf))).astype(np.float32)
    row, col = (token // GRID_W).astype(np.float32), (token % GRID_W).astype(np.float32)
    ang = np.concatenate([freqs[:, None] * row, freqs[:, None] * col]).astype(np.float32)
    cosine = np.cos(ang, dtype=np.float32)
    sine = np.sin(ang, dtype=np.float32)
    i, j = np.arange(P)[None, :], np.arange(P)[:, None]
    c = np.zeros((P, C_END), np.float32)
    powers = np.zeros((P, Z_END), np.float32)
    c[:, C_ABS:C_ABS + P] = abs(i - j)
    c[:, C_LOW:C_LOW + P] = i >= j
    c[:, C_UP:C_UP + P] = i <= j
    c[:, C_XIF:C_XIF + P] = i + 1
    c[:, C_XIB:C_XIB + P] = CHUNK - i
    p = np.arange(P)
    for n, v in enumerate((CHUNK - 1 - p, p, CTX - 1 - p, CTX - 1 - P - p, p, P + p, CHUNK + 0 * p)):
        powers[:, n] = v
    sel = np.array([[1, 0], [0, 1], [1, 0], [0, 1]], np.float32)
    return (np.concatenate([cosine, cosine]), np.concatenate([sine, -sine]), c, powers, np.eye(P, dtype=np.float32), sel)


def kernel(x, c, ctx, c_ctx, w_ada, b_ada, norm_g, ffn1_w1, ffn1_w2, w_in, ret_decay,
           gmlp_ws, gmlp_bs, w_out, ffn2_w1, ffn2_w2, final_g):
    import concourse.bacc as bacc
    from concourse.bass_utils import run_bass_kernel_spmd

    a = lambda v: np.asarray(v)
    ada, win, wout = _units(a(w_ada)[0]), _units(a(w_in)[0]), _units(a(w_out)[0])
    f1, f2 = _w1_units(a(ffn1_w1)[0]), _w1_units(a(ffn2_w1)[0])
    stream = []
    for i in range(NIT):
        n = ADA_FIRST + 2 * i
        stream += [f1[2 * i:2 * i + 2], ada[n:n + 2]]
    for kind, part, p in MIX_UNITS:
        n = p if kind == "out" else WIN[part[1:] if kind == "ctx" else part] + p
        stream.append((wout if kind == "out" else win)[n:n + 1])
    stream.append(f2)
    cosine, sine, consts, powers, ident, sel = _tables()
    arrays = {
        "x": a(x)[0].T, "ctx": a(ctx)[0].T,
        "c2": np.stack([_per_feature(a(c)[0]), _per_feature(a(c_ctx))], axis=-1),
        "ada_units": ada[:ADA_FIRST],
        "w_units": np.concatenate(stream),
        "w2_units": np.concatenate([a(ffn1_w2)[0].reshape(NF, P, D), a(ffn2_w2)[0].reshape(NF, P, D)]),
        "b_ada": np.repeat(_per_feature(a(b_ada)[0])[..., None], 2, axis=-1),
        "norm_g": _per_feature(a(norm_g)[0]), "final_g": _per_feature(a(final_g)),
        "decay": np.broadcast_to(a(ret_decay)[0].reshape(1, 8), (P, 8)),
        "ws": a(gmlp_ws)[0].transpose(2, 0, 1),
        "bs": np.broadcast_to(a(gmlp_bs)[0][None], (P, GROUPS, CHUNK)),
        "cosine": cosine, "sine": sine, "consts": consts, "powers": powers, "ident": ident, "sel": sel,
    }
    arrays = {k: np.ascontiguousarray(v) for k, v in arrays.items()}
    nc = bacc.Bacc("TRN2", target_bir_lowering=False, num_devices=1, dynamic_dma_scratch_size=64)
    args = [nc.dram_tensor(k, v.shape, mybir.dt.from_np(v.dtype), kind="ExternalInput").ap()
            for k, v in arrays.items()]
    out = nc.dram_tensor("out", (D, SEQ), F32, kind="ExternalOutput").ap()
    layer(nc, *args, out)
    r = run_bass_kernel_spmd(nc, [arrays], core_ids=[0])
    return np.ascontiguousarray(r.results[0]["out"].T)[None]
```

```python
from contextlib import ExitStack

import numpy as np

import concourse.bass as bass
from concourse import mybir

ALU = mybir.AluOpType
ACT = mybir.ActivationFunctionType
F32 = mybir.dt.float32
F32R = mybir.dt.float32r

P = 128
D = 1024
KT = D // P
SEQ, CTX = 1024, 256
FF = 2816
NF = FF // P
HEADS, GROUPS = 4, 4
CHUNK = 128
NCH = SEQ // CHUNK
NMOD = 9
TB = 512
EPS = 1e-6
K_SCALE = float(P) ** -0.5
GRID_W = 64

UC = 256
N_ADA = NMOD * D // UC
ADA_FIRST = 12
NIT = NF // 2
U_FFN1 = 0
U_MIX = U_FFN1 + 4 * NIT
WIN = {"q": 0, "k": 2, "v": 4, "g": 6, "u": 8, "vg": 10}
MIX_UNITS = ([("ctx", "ck", 0), ("ctx", "ck", 1), ("ctx", "cv", 0), ("ctx", "cv", 1)]
             + [("lat", a, p) for p in range(2) for a in ("k", "q", "v")]
             + [("lat", a, p) for a in ("g", "vg", "u") for p in range(2)]
             + [("out", tb, p) for tb in range(2) for p in range(4)])
MIX_ADA = 12
U_FFN2 = U_MIX + len(MIX_UNITS) + 2

C_ABS, C_LOW, C_UP, C_XIF, C_XIB, C_END = 0, 128, 256, 384, 512, 640
Z_LAT, Z_CTX, Z_CHUNK, Z_END = (0, 1), ((2, 3), (4, 5)), 6, 8

BLOCKS = [(1, 0, CTX), (0, 0, TB), (0, TB, TB)]
DVE_SQUARES = 4
DVE_UNIT = 23
NRING = 6


def mixer_fills():
    fills, late = [], []
    for i, (kind, a, p) in enumerate(MIX_UNITS):
        if kind == "ctx":
            fills.append((i, a, p, 0))
        elif kind == "out":
            fills += [(i, "out", a, 2 * p + t) for t in range(2)]
        elif a in ("v", "vg"):
            fills += [(i, a, p, j) for j in range(4)]
            if a == "v":
                if p == 0:
                    fills += [(i, "state0", d, 0) for d in range(2)]
                h = 2 * p
                head = lambda h, *names: [(i, name, h, j) for name in names for j in range(2)]
                fills += head(h, "kt", "score", "uf", "ub", "o") + head(h + 1, "kt", "score")
                fills += [(i, "ysum", h, 0)] + head(h + 1, "uf", "ub") + head(h, "yscale") + head(h + 1, "o")
                late = [[(i + 1, "ysum", h + 1, 0)], [(i + 1, "yscale", h + 1, j) for j in range(2)]]
        else:
            for n in range(4):
                t, tb = (n % 2, n // 2) if (a, p) in (("k", 0), ("u", 1)) else (n // 2, n % 2)
                fills.append((i, a, 2 * p + t, tb))
                if a == "u":
                    fills.append((i, "mixed", 2 * p + t, tb))
                if late:
                    fills += late.pop(0)
    return fills


FILLS = mixer_fills()
FILL = {(name, a, b): n for n, (_, name, a, b) in enumerate(FILLS)}
LAST_FILL = [max(n for n, f in enumerate(FILLS) if f[0] == i and f[1] in (a, kind)) for i, (kind, a, _) in enumerate(MIX_UNITS)]
FIRST_FILL = [min(n for n, f in enumerate(FILLS) if f[0] == i) for i in range(len(MIX_UNITS))]


def layer(nc, x, ctx, c2, ada_units, w_units, w2_units, b_ada, norm_g, final_g, decay, ws, bs, cosine, sine, consts, powers, ident, out):
    stack = ExitStack()
    with stack:
        def at(name, shape, dt, offset):
            return nc.alloc_sbuf_tensor_at(name, shape, dt, offset=offset)

        top = [192]

        def keep(name, shape, dt):
            n = 4 * int(np.prod(shape[1:]))
            n += -n % 32
            top[0] += n
            return at(name, shape, dt, top[0] - n)

        X = keep("X", [P, KT, SEQ], F32)
        HH = keep("HH", [P, KT, SEQ], F32R)
        HL = keep("HL", [P, KT, SEQ], F32R)
        WR = keep("WR", [P, 2, KT, UC], F32)
        WH = keep("WH", [P, 2, KT, UC], F32R)
        WL = keep("WL", [P, 2, KT, UC], F32R)
        MODS = keep("MODS", [P, NMOD * KT, 2], F32)
        BA = keep("BA", [P, NMOD * KT, 2], F32)
        GAIN = keep("GAIN", [P, 3, KT, 2], F32)
        GATE = keep("GATE", [P, 3, KT, 2], F32)
        NG = keep("NG", [P, 3, KT], F32)
        FG = keep("FG", [P, KT], F32)
        ID = keep("ID", [P, P], F32)
        ONES = keep("ONES", [P, P], F32)
        CIN = keep("CIN", [P, KT, 2], F32)
        CS = keep("CS", [P, KT, 2], F32)
        MS = keep("MS", [P, 32], F32)
        RS = keep("RS", [P, 32], F32)
        NEGH = keep("NEGH", [P, 32], F32)
        LG = keep("LG", [P, 8], F32)
        IDX = keep("IDX", [P, Z_END], F32)
        Z = keep("Z", [P, 8, Z_END], F32)
        R = top[0]

        XC = at("XC", [P, KT, CTX], F32, R)
        HCH = at("HCH", [P, KT, CTX], F32R, R + 8192)
        HCL = at("HCL", [P, KT, CTX], F32R, R + 16384)
        NTOK = SEQ + CTX
        PH1 = at("PH1", [P, 2, NTOK], F32R, R + 24576)
        PL1 = at("PL1", [P, 2, NTOK], F32R, R + 34816)
        W2R1 = at("W2R1", [P, D], F32, R + 45056)
        W2H1 = at("W2H1", [P, 2, D], F32R, R + 49152)
        W2L1 = at("W2L1", [P, 2, D], F32R, R + 57344)
        SG = at("SG", [P, 2, TB], F32, R + 65536)
        PR = at("PR", [P, 2, TB], F32, R + 69632)
        ROWS = at("ROWS", [2, 2, UC], F32, R + 73728)
        AS = at("AS", [P, 2, 2, UC], F32, R + 73728)
        WS = at("WS", [P, 3, KT, UC], F32, R + 45056)

        def norm_buffers(place, sq, acc, dg, hf):
            return (at(f"SQ{place}", [P, 2, TB], F32, R + sq), at(f"ACC{place}", [P, TB], F32, R + acc),
                    at(f"DG{place}", [P, 4, P], F32, R + dg),
                    [at(f"HF{place}_{n}", [P, TB], F32, R + o) for n, o in enumerate(hf)])

        NB = [norm_buffers(0, 24576, 34816, 36864, (29696, 31744, 39936, 41984)),
              norm_buffers(1, 45056, 65536, 67584, (69632, 71680, 73728, 75776)),
              norm_buffers(2, 24576, 28672, 30720, (32768, 34816, 36864, 38912))]
        NB.append(NB[2])
        KF = at("KF", [P, 2, SEQ], F32, R)
        QF = at("QF", [P, 2, SEQ], F32, R + 8192)
        V = at("V", [P, NCH, UC], F32, R + 16384)
        KZ = [at(f"KZ{d}", [P, NCH, P], F32, R + 24576 + 4096 * d) for d in range(2)]
        PM = at("PM", [P, NCH, P], F32, R + 32768)
        XI = at("XI", [P, 8, P], F32, R + 36864)
        RET = at("RET", [P, HEADS, SEQ], F32, R + 40960)
        KC = at("KC", [P, 2, 2, HEADS, P], F32, R + 40960)
        VC = at("VC", [P, 2, HEADS * P], F32, R + 49152)
        CST = at("CST", [P, C_END], F32, R + 53248)
        DT = at("DT", [P, 2, P], F32, R + 55872)
        COS = at("COS", [P, SEQ], F32, R + 57344)
        SIN = at("SIN", [P, SEQ], F32, R + 61440)
        V2 = at("V2", [P, NCH, UC], F32, R + 57344)
        DG2 = at("DG2", [P, 4, P], F32, R + 67584)
        DM = at("DM", [P, HEADS, P], F32, R + 65536)
        TMP = at("TMP", [P, 2, TB], F32, R + 69632)
        S0 = at("S0", [P, 2, HEADS, P], F32, R + 73728)
        GM = at("GM", [P, GROUPS, SEQ], F32, R)
        MIXD = at("MIXD", [P, 2, TB], F32, R + 24576)
        GU = at("GU", [P, 2, TB], F32, R + 28672)
        WST = at("WST", [P, GROUPS, P], F32, R + 32768)
        BB = at("BB", [P, GROUPS, P], F32, R + 34816)
        BST = at("BST", [P, 16, 6], F32, R + 67584)
        MV = at("MV", [P, 16, 2], F32, R + 67584 + 384)
        PH2 = at("PH2", [P, 2, SEQ], F32R, R)
        PL2 = at("PL2", [P, 2, SEQ], F32R, R + 8192)
        W2R2 = at("W2R2", [P, D], F32, R + 40960)
        W2H2 = at("W2H2", [P, 2, D], F32R, R + 45056)
        W2L2 = at("W2L2", [P, 2, D], F32R, R + 53248)
        OUT = [at(f"OUT{b}", [P, KT, TB], F32, o) for b, o in enumerate((R, R + 40960))]

        PS = [stack.enter_context(nc.psum_tensor(f"PS{b}", [P, 512], F32)) for b in range(8)]
        ST_BANK, RB_BANK = PS[6], PS[7]

        sem = lambda name: stack.enter_context(nc.semaphore(name))
        s_c = sem("c_loaded")
        s_const = sem("const_loaded")
        s_cst = sem("decay_consts_loaded")
        s_rope = sem("rope_loaded")
        s_gw = sem("gmlp_weights_loaded")
        s_x = [sem(f"x_loaded{b}") for b in range(3)]
        s_first = [sem(f"first_ada_loaded{s}") for s in range(3)]
        s_raw = [sem(f"unit_loaded{s}") for s in range(2)]
        s_hi = sem("unit_high_done")
        s_lo = [sem(f"unit_low_done{s}") for s in range(2)]
        s_w2raw = sem("w2_loaded")
        s_w2hi = sem("w2_high_done")
        s_w2lo = sem("w2_low_done")
        s_cs = sem("silu_c_ready")
        s_ada = sem("ada_product_ready")
        s_rows = sem("ada_rows_copied")
        s_asum = sem("ada_sum_chain")
        s_col = sem("ada_columns_ready")
        s_mods = sem("mods_done")
        s_coef = sem("coefficients_ready")
        s_lg = sem("log_decay_ready")
        s_sq = sem("squares_done")
        s_acc = sem("squares_added")
        s_st = sem("norm_sum_ready")
        s_ms = sem("norm_mean_ready")
        s_rs = sem("norm_rsqrt_ready")
        s_dg = sem("norm_diagonal_ready")
        s_rb = sem("norm_scale_ready")
        s_xm = sem("scaled_done")
        s_hf = sem("modulated_done")
        s_hh = sem("modulated_high_done")
        s_hl = sem("modulated_low_done")
        s_gu = sem("gate_up_ready")
        s_silu = sem("silu_done")
        s_prod = sem("product_done")
        s_ph = sem("product_high_done")
        s_pl = sem("product_low_done")
        s_y = sem("down_ready")
        s_yd = sem("down_added")
        s_fill = sem("fill_ready")
        s_free = [sem(f"bank_free{b}") for b in range(NRING)]
        s_exp = sem("exp_done")
        s_dec = sem("score_masks_ready")
        s_rope_done = sem("rope_done")
        s_kz = sem("decayed_keys_ready")
        s_state = sem("states_ready")
        s_q = sem("decayed_queries_ready")
        s_oc = sem("retention_copied")
        s_ym = sem("retention_mean_ready")
        s_yr = sem("retention_rsqrt_ready")
        s_yg = sem("retention_diagonal_ready")
        s_lv = sem("gmlp_variance_ready")
        s_lr = sem("gmlp_rsqrt_ready")
        s_vn = sem("gmlp_v_normed")
        s_mx = sem("gmlp_mixed_added")
        s_cat = sem("mixer_input_ready")
        s_cath = sem("mixer_high_done")
        s_catl = [sem(f"mixer_low_done{e}") for e in range(2)]
        s_chain = sem("vector_chain")
        s_out = sem("stored")

        def release(n):
            _, name, a, b = FILLS[n]
            if name == "uf":
                return s_state, 14 * a + (7 if b == 0 else 13)
            if name == "ub":
                return s_state, 14 * a + (8 if b == 1 else 14)
            if name == "ysum":
                return s_ym, a + 1
            if name == "mixed":
                return s_mx, sum(f[1] == "mixed" for f in FILLS[:n + 1])
            return s_free[n % NRING], sum(FILLS[m][1] not in ("uf", "ub", "ysum", "mixed")
                                          for m in range(n % NRING, n + 1, NRING))

        def scale_bank(place, b):
            return {(0, 2): ST_BANK, (1, 0): PS[2], (1, 2): ST_BANK, (3, 2): PS[0]}.get((place, b), RB_BANK)

        def last_release(bank):
            return release(max(n for n in range(len(FILLS)) if n % NRING == bank))

        NORMS = [(0, b) for b in range(3)] + [(1, b) for b in range(3)] + [(2, 1), (2, 2), (3, 1), (3, 2)]
        J = {key: j for j, key in enumerate(NORMS)}
        FFN = [dict(T=3, blocks=BLOCKS, step=0, y=0, v=0, unit=U_FFN1, per=4),
               dict(T=2, blocks=BLOCKS[1:], step=6 * NIT, y=24 * NIT, v=2 * NIT, unit=U_FFN2, per=2)]
        y_all = [24 * NIT + 2, 40 * NIT + 2]

        def mods_done(a):
            return a if a <= ADA_FIRST else ADA_FIRST + (a - ADA_FIRST) // 2

        def highs(u):
            if u >= U_MIX:
                return u - 2 * NIT - (2 if u >= U_MIX + MIX_ADA else 0)
            return 2 * (u // 4) + u % 4

        def mix_unit(i):
            return U_MIX + i + (2 if i >= MIX_ADA else 0)

        def steps(f, opening=False):
            order = [(ft, t) for ft in range(2) for t in range(f["T"])]
            return [(ft, t) for t, ft in sorted((t, ft) for ft, t in order)] if opening else order

        def first_bank(a):
            return a % 4

        def down_bank(s, d):
            return (4, 5, 0, 1)[d % 4] if s else 4 + d % 2

        def tokens(t, b):
            _, t0, n = BLOCKS[b]
            return lambda k: t[:, k, t0:t0 + n]

        def streams(b):
            return (XC, HCH, HCL) if b == 0 else (X, HH, HL)

        block = stack.enter_context(nc.Block())

        @block.sync
        def _(sp):
            sp.dma_start(CIN[:, :, :], c2).then_inc(s_c, 16)

            def unit(u, slot):
                sp.dma_start(WR[:, slot], w_units[u]).then_inc(s_raw[slot], 16)

            def first_ada(a):
                if a >= 3:
                    sp.wait_ge(s_ada, a - 2)
                sp.dma_start(WS[:, a % 3], ada_units[a]).then_inc(s_first[a % 3], 16)

            def tokens_in(b):
                _, t0, n = BLOCKS[b]
                dst, src = (XC, ctx) if b == 0 else (X, x)
                sp.dma_start(dst[:, :, t0:t0 + n],
                             src.rearrange("(k p) t -> p k t", p=P)[:, :, t0:t0 + n]).then_inc(s_x[b], 16)

            first_ada(0)
            for dst, src in ((LG[:, :], decay), (IDX[:, :], powers), (BA[:, :, :], b_ada),
                             (NG[:, :, :], norm_g), (FG[:, :], final_g), (ID[:, :], ident)):
                sp.dma_start(dst, src).then_inc(s_const, 16)
            tokens_in(0)
            for a in range(1, ADA_FIRST):
                first_ada(a)
                if a in (2, 4):
                    tokens_in(a // 2)
                if a in (7, 9):
                    unit(U_FFN1 + (a - 7) // 2, (a - 7) // 2)

            def ffn(f, it, w2r, prefetch):
                for j in range(2):
                    sp.wait_ge(s_w2lo, f["v"] + 2 * it + j + 1)
                    sp.dma_start(w2r[:, :], w2_units[f["v"] + 2 * it + j]).then_inc(s_w2raw, 16)
                for j in range(f["per"] if prefetch else 0):
                    u = f["unit"] + f["per"] * it + 2 + j
                    sp.wait_ge(s_lo[j % 2], (f["unit"] + j - j % 2) // 2 + (f["per"] // 2) * it + 1)
                    unit(u, j % 2)

            sp.wait_ge(s_ada, ADA_FIRST)
            with sp.Fori(0, NIT) as it:
                ffn(FFN[0], it, W2R1, True)
            sp.wait_ge(s_yd, y_all[0])
            sp.dma_start(CST[:, :], consts).then_inc(s_cst, 16)
            sp.dma_start(COS[:, :], cosine).then_inc(s_rope, 16)
            sp.dma_start(SIN[:, :], sine).then_inc(s_rope, 16)
            for u in range(U_MIX + 2, U_FFN2 + 2):
                sp.wait_ge(s_lo[u % 2], u // 2)
                unit(u, u % 2)
                if u == mix_unit(MIX_ADA):
                    sp.wait_ge(s_fill, FILL["yscale", HEADS - 1, 1] + 1)
                    sp.dma_start(WST[:, :, :], ws).then_inc(s_gw, 16)
                    sp.dma_start(BB[:, :, :], bs).then_inc(s_gw, 16)
            for e in range(2):
                sp.wait_ge(s_catl[e], 8)
            with sp.Fori(0, NIT - 1) as it:
                ffn(FFN[1], it, W2R2, True)
            ffn(FFN[1], NIT - 1, W2R2, False)
            stores = [(0, 0, 4), (0, 4, 8), (1, 0, 2), (1, 2, 4), (1, 4, 6), (1, 6, 7), (1, 7, 8)]
            for b, k, end in stores:
                sp.wait_ge(s_hf, 8 * J[3, b + 1] + end)
                sp.dma_start(out.rearrange("(k p) t -> p k t", p=P)[:, k:end, b * TB:(b + 1) * TB],
                             OUT[b][:, k:end, :]).then_inc(s_out, 16)
            sp.wait_ge(s_out, 16 * len(stores))

        @block.gpsimd
        def _(pool):
            pool.memset(NEGH[:, :], -0.5).then_inc(s_w2lo, 1)

            def low(u):
                unit_low(u % 2, highs(u) + 1)

            def unit_low(slot, count):
                pool.wait_ge(s_hi, count)
                pool.tensor_tensor(WL[:, slot], WR[:, slot], WH[:, slot].bitcast(F32),
                                   ALU.subtract).then_inc(s_lo[slot], 1)

            def power(dst, src, ready, count, done):
                pool.wait_ge(ready, count)
                n = src.shape[-1]
                pool.tensor_tensor(dst, src, NEGH[:, 0:n], ALU.pow).then_inc(done, 1)

            def norm_rsqrt(place, b):
                j, n = J[place, b], BLOCKS[b][2]
                power(RS[:, 0:n // P], MS[:, 0:n // P], s_ms, j + 1, s_rs)

            def norm_low(place, b, first=0, last=KT):
                n, (_, hh, hl), hf = BLOCKS[b][2], streams(b), NB[place][3]
                j = J[place, b]
                for k in range(first, last):
                    pool.wait_ge(s_hh, 8 * j + k + 1)
                    pool.tensor_tensor(tokens(hl, b)(k), hf[k % 4][:, 0:n], tokens(hh, b)(k).bitcast(F32),
                                       ALU.subtract).then_inc(s_hl, 1)

            pool.wait_ge(s_w2lo, 1)
            norm_rsqrt(0, 0)
            norm_rsqrt(0, 1)
            norm_rsqrt(0, 2)
            norm_low(0, 0)
            low(U_FFN1)
            norm_low(0, 1)
            norm_low(0, 2)
            low(U_FFN1 + 1)

            def ffn(f, it, w2r, w2h, w2l, prefetch):
                for j in range(2):
                    pool.wait_ge(s_w2hi, f["v"] + 2 * it + j + 1)
                    pool.tensor_tensor(w2l[:, j], w2r[:, :], w2h[:, j].bitcast(F32),
                                       ALU.subtract).then_inc(s_w2lo, 1)
                for j in range(2 if prefetch else 0):
                    unit_low(j, highs(f["unit"]) + 2 * it + 3 + j)

            with pool.Fori(0, NIT) as it:
                ffn(FFN[0], it, W2R1, W2H1, W2L1, True)
            norm_rsqrt(1, 0)
            for k in range(DVE_SQUARES, KT):
                j = J[1, 1]
                pool.wait_ge(s_sq, 8 * j + k + 1)
                pool.wait_ge(s_acc, 8 * j + k)
                pool.tensor_tensor(NB[1][1][:, :], NB[1][1][:, :], NB[1][0][:, k % 2, :], ALU.add).then_inc(s_acc, 1)
            norm_low(1, 0, 0, 4)
            norm_rsqrt(1, 1)
            norm_low(1, 0, 4)
            norm_rsqrt(1, 2)
            norm_low(1, 1)
            norm_low(1, 2)

            def decay_queries(h, d):
                hh = h % 2
                q = QF[:, hh, :].rearrange("p (c t) -> p c t", c=NCH)
                if d == 0:
                    pool.wait_ge(s_rope_done, 8 * (h // 2 + 1))
                    pool.wait_ge(s_fill, FILL["state0", 1, 0] + 1)
                    dst = RET[:, h, :].rearrange("p (c t) -> p c t", c=NCH)
                else:
                    pool.wait_ge(s_fill, FILL["score", h, 1] + 1)
                    pool.wait_ge(s_q, 2 * h + 1)
                    dst = q
                pool.tensor_tensor(dst, q, XI[:, 4 * d + h, :].unsqueeze(1).to_broadcast([P, NCH, P]),
                                   ALU.mult).then_inc(s_q, 1)

            def cat_low(n):
                k, t0 = n % 8, n // 8 * TB
                pool.wait_ge(s_cath, n + 1)
                src = RET[:, k, t0:t0 + TB] if k < 4 else GM[:, k - 4, t0:t0 + TB]
                pool.tensor_tensor(HL[:, k, t0:t0 + TB], src, HH[:, k, t0:t0 + TB].bitcast(F32),
                                   ALU.subtract).then_inc(s_catl[0], 1)

            low(U_MIX + 5)
            pool.wait_ge(s_exp, 17)
            for n, (i, name, a, b) in enumerate(FILLS):
                if n == FIRST_FILL[i] and i >= 5 and i + 1 != DVE_UNIT:
                    low(mix_unit(i + 1))
                if (name, b) == ("kt", 0):
                    decay_queries(a, 0)
                if (name, b) == ("score", 1) and a % 2 == 0:
                    decay_queries(a, 1)
                if name == "ysum":
                    power(RS[:, 8:16], MS[:, 8:16], s_ym, a + 1, s_yr)
                    if a % 2 == 0:
                        decay_queries(a + 1, 1)
                if (name, b) == ("vg", 3):
                    power(RS[:, 16:32], MS[:, 16:32], s_lv, a + 1, s_lr)
                if (name, a, b) == ("mixed", GROUPS - 1, 0):
                    for m in range(0, 8, 2):
                        cat_low(m)
                if (name, a, b) == ("out", 0, 1):
                    for m in range(8, 16, 2):
                        cat_low(m)
                if (name, a, b) == ("out", 1, 1):
                    norm_rsqrt(2, 1)
                if (name, a, b) in (("out", 1, 2), ("out", 1, 3)):
                    norm_low(2, 1, 4 * (b - 2), 4 * (b - 1))
            norm_rsqrt(2, 2)
            low(U_FFN2 + 1)
            norm_low(2, 2)
            with pool.Fori(0, NIT - 1) as it:
                ffn(FFN[1], it, W2R2, W2H2, W2L2, True)
            ffn(FFN[1], NIT - 1, W2R2, W2H2, W2L2, False)
            for b in (1, 2):
                norm_rsqrt(3, b)

        @block.scalar
        def _(act):
            def high(slot, raw_count):
                act.wait_ge(s_raw[slot], raw_count)
                act.activation(WH[:, slot], WR[:, slot], ACT.Copy).then_inc(s_hi, 1)

            def mix_high(i):
                if i >= 2:
                    act.wait_ge(s_fill, LAST_FILL[i - 2] + 1)
                u = mix_unit(i)
                high(u % 2, 16 * (u // 2 + 1))

            def square(place, b, k):
                n, (xs, _, _) = BLOCKS[b][2], streams(b)
                j = J[place, b]
                if 8 * j + k >= 2:
                    act.wait_ge(s_acc, 8 * j + k - 1)
                act.activation(NB[place][0][:, k % 2, 0:n], tokens(xs, b)(k), ACT.Square).then_inc(s_sq, 1)

            def norm_high(place, b, first=0, last=KT):
                n, (_, hh, _) = BLOCKS[b][2], streams(b)
                j = J[place, b]
                for k in range(first, last):
                    act.wait_ge(s_hf, 8 * j + k + 1)
                    act.activation(tokens(hh, b)(k), NB[place][3][k % 4][:, 0:n], ACT.Copy).then_inc(s_hh, 1)

            act.wait_ge(s_c, 16)
            act.activation(CS[:, :, :], CIN[:, :, :], ACT.Silu).then_inc(s_cs, 1)
            for b in range(3):
                act.wait_ge(s_x[b], 16)
                for k in range(KT):
                    square(0, b, k)
            act.wait_ge(s_const, 16 * 6)
            act.activation(LG[:, :], LG[:, :], ACT.Exp).then_inc(s_exp, 1)
            act.wait_ge(s_lg, 1)
            for dh in range(8):
                act.activation(Z[:, dh, :], IDX[:, :], ACT.Exp, scale=LG[:, dh:dh + 1]).then_inc(s_exp, 1)
            for b in range(3):
                norm_high(0, b)
                if b != 1:
                    high(b // 2, 16)

            def off(f, t):
                s, t0, _ = f["blocks"][t]
                return SEQ if s else t0

            def ffn(f, it, ph, w2r, w2h, prefetch, opening=False, last=False):
                nsteps = 2 * f["T"]
                order = steps(f, opening)
                for i, (ft, t) in enumerate(order):
                    n = f["step"] + nsteps * it + i
                    nt = f["blocks"][t][2]
                    act.wait_ge(s_gu, n + 1)
                    act.activation(SG[:, i % 2, 0:nt], PS[2 * (i % 2)][:, 0:nt], ACT.Silu).then_inc(s_silu, 1)
                    act.wait_ge(s_prod, n + 3)
                    act.activation(ph[:, ft, off(f, t):off(f, t) + nt], PR[:, i % 2, 0:nt],
                                   ACT.Copy).then_inc(s_ph, 1)
                    if opening and i == 0:
                        norm_high(2, 2)
                    if i < 2:
                        if i == 0:
                            act.wait_ge(s_yd, f["y"] + 8 * f["T"] * it + 2)
                        act.wait_ge(s_w2raw, 16 * (f["v"] + i + 1) + 32 * it)
                        act.activation(w2h[:, i], w2r[:, :], ACT.Copy).then_inc(s_w2hi, 1)
                    if (ft, t) == (0, f["T"] - 1) and prefetch:
                        high(0, 8 * (f["unit"] + f["per"]) + 16 + 8 * f["per"] * it)
                if prefetch and not last:
                    high(1, 8 * (f["unit"] + f["per"]) + 16 + 8 * f["per"] * it)

            def down_squares(f, place, t):
                for k in range(KT):
                    act.wait_ge(s_yd, f["y"] + 8 * f["T"] * (NIT - 1) + 8 * t + k + 3)
                    square(place, t + 3 - f["T"], k)

            with act.Fori(0, NIT - 1) as it:
                ffn(FFN[0], it, PH1, W2R1, W2H1, True)
            ffn(FFN[0], NIT - 1, PH1, W2R1, W2H1, True, last=True)
            down_squares(FFN[0], 1, 0)
            act.wait_ge(s_prod, 6 * NIT + 2)
            high(1, 16 * ((U_MIX + 1) // 2 + 1))
            down_squares(FFN[0], 1, 1)
            norm_high(1, 0)
            down_squares(FFN[0], 1, 2)
            mix_high(2)
            norm_high(1, 1, 0, 5)
            mix_high(3)
            norm_high(1, 1, 5)
            mix_high(4)
            norm_high(1, 2)
            mix_high(5)

            act.wait_ge(s_cst, 16)
            for dh in range(8):
                c0 = C_XIF if dh < 4 else C_XIB
                act.activation(XI[:, dh, :], CST[:, c0:c0 + P], ACT.Exp, scale=LG[:, dh:dh + 1]).then_inc(s_exp, 1)
            for h in range(HEADS):
                for d in range(2):
                    if h:
                        act.wait_ge(s_dec, h)
                    act.activation(DT[:, d, :], CST[:, C_ABS:C_ABS + P], ACT.Exp,
                                   scale=LG[:, 4 * d + h:4 * d + h + 1]).then_inc(s_exp, 1)

            n_gate = 0
            for n, (i, name, a, b) in enumerate(FILLS):
                ps, free = PS[n % NRING], s_free[n % NRING]
                if n == FIRST_FILL[i] and i >= 5:
                    mix_high(i + 1)
                if name in ("cv", "state0", "v", "vg", "kt", "o", "g", "u"):
                    act.wait_ge(s_fill, n + 1)
                if name == "cv":
                    act.activation(VC[:, :, a * UC:(a + 1) * UC], ps[:, :].rearrange("p (b c) -> p b c", b=2),
                                   ACT.Copy).then_inc(free, 1)
                elif name == "state0":
                    act.activation(S0[:, a, :, :], ps[:, :].rearrange("p (h v) -> p h v", h=HEADS),
                                   ACT.Copy).then_inc(free, 1)
                elif name in ("v", "vg"):
                    dst = V2 if (name, a) == ("vg", 1) else V
                    act.activation(dst[:, 2 * b:2 * b + 2, :], ps[:, :].rearrange("p (b c) -> p b c", b=2),
                                   ACT.Copy if name == "v" else ACT.Gelu_apprx_tanh).then_inc(free, 1)
                elif name == "kt":
                    for d in range(2):
                        act.activation(KZ[d][:, 4 * b:4 * b + 4, :], ps[:, :].rearrange("p (c d) -> p c d", c=4),
                                       ACT.Copy, scale=Z[:, 4 * d + a, Z_LAT[d]:Z_LAT[d] + 1]).then_inc(free if d else s_kz, 1)
                elif name == "o":
                    act.activation(RET[:, a, b * TB:(b + 1) * TB], ps[:, :], ACT.Copy).then_inc(s_oc, 1)
                    act.activation(KF[:, a % 2, b * TB:(b + 1) * TB], ps[:, :], ACT.Square).then_inc(free, 1)
                elif name in ("g", "u"):
                    if n_gate >= 2:
                        act.wait_ge(s_cat, n_gate - 1)
                    act.activation(GU[:, n_gate % 2, :], ps[:, :],
                                   ACT.Silu if name == "g" else ACT.Gelu_apprx_tanh).then_inc(free, 1)
                    n_gate += 1
                if (name, a, b) in (("mixed", GROUPS - 1, 0), ("out", 0, 1)):
                    act.wait_ge(s_fill, FILL["mixed", GROUPS - 1, b])
                    act.wait_ge(s_cat, 14 + 2 * b)
                    t0 = b * TB
                    for k in range(KT):
                        src = RET[:, k, t0:t0 + TB] if k < 4 else GM[:, k - 4, t0:t0 + TB]
                        act.activation(HH[:, k, t0:t0 + TB], src, ACT.Copy).then_inc(s_cath, 1)
                if name == "out" and n > FILL["out", 0, 0]:
                    m = n - FILL["out", 0, 0] - 1
                    act.wait_ge(*release(n - 1))
                    square(2, 1 + m // 8, m % 8)
                if (name, a, b) in (("out", 1, 2), ("out", 1, 3)):
                    norm_high(2, 1, 4 * (b - 2), 4 * (b - 1))
            act.wait_ge(*release(len(FILLS) - 1))
            square(2, 2, 7)
            mix_high(len(MIX_UNITS) + 1)
            ffn(FFN[1], 0, PH2, W2R2, W2H2, True, opening=True)
            with act.Fori(1, NIT - 1) as it:
                ffn(FFN[1], it, PH2, W2R2, W2H2, True)
            ffn(FFN[1], NIT - 1, PH2, W2R2, W2H2, False)
            down_squares(FFN[1], 3, 0)
            down_squares(FFN[1], 3, 1)

        @block.vector
        def _(dve):
            chain = [0]

            def link(ins):
                chain[0] += 1
                ins.then_inc(s_chain, 1)
                dve.wait_ge(s_chain, chain[0])

            link(dve.memset(ONES[:, :], 1.0))
            dve.memset(MS[:, :], 0.0).then_inc(s_prod, 2)
            dve.memset(RS[:, :], 0.0).then_inc(s_pl, 2)
            dve.memset(AS[:, 0, 0, :], 0.0).then_inc(s_yd, 2)

            def add_square(place, b, k):
                n, j = BLOCKS[b][2], J[place, b]
                sq, acc = NB[place][0], NB[place][1]
                dve.wait_ge(s_sq, 8 * j + k + 1)
                if k == 0:
                    if j:
                        dve.wait_ge(s_st, j)
                    ins = dve.tensor_copy(acc[:, 0:n], sq[:, 0, 0:n])
                else:
                    dve.wait_ge(s_acc, 8 * j + k)
                    ins = dve.tensor_tensor(acc[:, 0:n], acc[:, 0:n], sq[:, k % 2, 0:n], ALU.add)
                ins.then_inc(s_acc, 1)

            def add_squares(place, b):
                for k in range(KT):
                    add_square(place, b, k)

            def norm_mean(place, b):
                nb, j = BLOCKS[b][2] // P, J[place, b]
                dve.wait_ge(s_st, j + 1)
                dve.tensor_scalar(MS[:, 0:nb], ST_BANK[:, 0:nb], 1.0 / D, EPS, ALU.mult, ALU.add).then_inc(s_ms, 1)

            def diagonal(nb, rs, dst):
                return dve.tensor_tensor(dst, ID[:, :].unsqueeze(1).to_broadcast([P, nb, P]),
                                         rs.unsqueeze(2).to_broadcast([P, nb, P]), ALU.mult)

            def norm_diagonal(place, b):
                nb, j = BLOCKS[b][2] // P, J[place, b]
                dve.wait_ge(s_rs, j + 1)
                if j:
                    dve.wait_ge(s_rb, j)
                diagonal(nb, RS[:, 0:nb], NB[place][2][:, 0:nb, :]).then_inc(s_dg, 1)

            def scaled(place, b, k):
                n, j = BLOCKS[b][2], J[place, b]
                if 8 * j + k >= 4:
                    dve.wait_ge(s_hl, 8 * j + k - 3)
                dve.tensor_tensor(NB[place][3][k % 4][:, 0:n], tokens(streams(b)[0], b)(k), scale_bank(place, b)[:, 0:n],
                                  ALU.mult).then_inc(s_xm, 1)

            def modulated(place, b, k):
                s, _, n = BLOCKS[b]
                j, hf = J[place, b], NB[place][3][k % 4]
                dve.wait_ge(s_xm, 8 * j + k + 1)
                dve.tensor_scalar(hf[:, 0:n], hf[:, 0:n], GAIN[:, place, k, s:s + 1],
                                  MODS[:, 3 * place * KT + k, s:s + 1], ALU.mult, ALU.add).then_inc(s_hf, 1)

            def norm_apply(place, b, between=lambda k: None):
                j = J[place, b]
                dve.wait_ge(s_rb, j + 1)
                for k in range(KT + 1):
                    between(k)
                    if k < KT:
                        scaled(place, b, k)
                    if k:
                        modulated(place, b, k - 1)

            def norm_out(b, first, last):
                dve.wait_ge(s_rb, J[3, b] + 1)
                for k in range(first, last):
                    dve.scalar_tensor_tensor(OUT[b - 1][:, k, :], tokens(X, b)(k), FG[:, k:k + 1],
                                             scale_bank(3, b)[:, :], ALU.mult, ALU.mult).then_inc(s_hf, 1)

            def ada_rows(a, slot, bank):
                dve.wait_ge(s_ada, a + 1)
                dve.tensor_copy(ROWS[:, slot, :], PS[bank][0:2, 0:UC]).then_inc(s_rows, 1)

            def ada_mods(a, bank):
                dve.wait_ge(s_col, a + 1)
                dst, b = MODS[:, bass.ts(a, 2), :], BA[:, bass.ts(a, 2), :]
                dve.tensor_tensor(dst, PS[bank][:, UC:UC + 4].rearrange("p (t s) -> p t s", t=2), b,
                                  ALU.add).then_inc(s_mods, 1)

            def gain(place):
                dve.wait_ge(s_mods, mods_done(4 * (3 * place + 2)))
                c = (3 * place + 1) * KT
                dve.scalar_tensor_tensor(GAIN[:, place], MODS[:, c:c + KT, :], 1.0,
                                         NG[:, place, :].unsqueeze(2).to_broadcast([P, KT, 2]),
                                         ALU.add, ALU.mult).then_inc(s_coef, 1)

            def gate(place):
                dve.wait_ge(s_mods, mods_done(4 * (3 * place + 3)))
                c = (3 * place + 2) * KT
                dve.tensor_scalar(GATE[:, place], MODS[:, c:c + KT, :], 1.0 if place == 1 else 0.5, None,
                                  ALU.mult).then_inc(s_coef, 1)

            def first_rows(*units):
                for a in units:
                    ada_rows(a, a % 2, first_bank(a))

            def first_mods(*units):
                for a in units:
                    ada_mods(a, first_bank(a))

            dve.wait_ge(s_const, 16 * 6)
            add_squares(0, 0)
            first_rows(0, 1)
            first_mods(0)
            norm_mean(0, 0)
            norm_diagonal(0, 0)
            add_squares(0, 1)
            for a in (2, 3, 4):
                first_rows(a)
                first_mods(a - 1)
            norm_mean(0, 1)
            norm_diagonal(0, 1)
            add_squares(0, 2)
            dve.wait_ge(s_exp, 1)
            dve.tensor_scalar(LG[:, :], LG[:, :], -1.0, None, ALU.mult).then_inc(s_lg, 1)
            for a in (5, 6, 7):
                first_rows(a)
                first_mods(a - 1)
            first_mods(7)
            norm_mean(0, 2)
            gain(0)
            dve.wait_ge(s_coef, 1)
            norm_apply(0, 0)
            first_rows(8)
            first_mods(8)
            first_rows(9)
            first_mods(9)
            norm_diagonal(0, 2)
            norm_apply(0, 1, lambda k: first_rows(*{5: (10,), 7: (11,)}.get(k, ())))
            first_mods(10, 11)
            gate(0)
            norm_apply(0, 2)

            def ada_sums(it, slot, raw):
                dve.wait_ge(s_raw[slot], raw)
                dve.wait_ge(s_col, ADA_FIRST + it)
                links = 30 * it + 15 * slot
                for k in range(KT):
                    for v in range(2):
                        dst, w, c = AS[:, slot, v, :], WR[:, slot, k, :], CS[:, k, v:v + 1]
                        if k == 0:
                            ins = dve.tensor_scalar(dst, w, c, None, ALU.mult)
                        else:
                            dve.wait_ge(s_asum, links + 2 * k + v - 1)
                            ins = dve.scalar_tensor_tensor(dst, w, c, dst, ALU.mult, ALU.add)
                        ins.then_inc(s_lo[slot] if (k, v) == (KT - 1, 1) else s_asum, 1)

            def ada_pair_mods(it):
                dve.wait_ge(s_col, ADA_FIRST + it + 1)
                at_a = bass.ts(ADA_FIRST // 2 + it, 4)
                dve.tensor_tensor(MODS[:, at_a, :], PS[6][:, 0:8].rearrange("p (t s) -> p t s", s=2),
                                  BA[:, at_a, :], ALU.add).then_inc(s_mods, 1)

            def ffn(f, it, ph, pl, last=False, opening=False):
                nsteps = 2 * f["T"]
                first = f["per"] == 4

                def low_part(n, i, ft, o, nt):
                    dve.wait_ge(s_ph, n + 1)
                    dve.tensor_tensor(pl[:, ft, o:o + nt], PR[:, i % 2, 0:nt], ph[:, ft, o:o + nt].bitcast(F32),
                                      ALU.subtract).then_inc(s_pl, 1)

                for i, (ft, t) in enumerate(steps(f, opening)):
                    n = f["step"] + nsteps * it + i
                    s, t0, nt = f["blocks"][t]
                    o = SEQ if s else t0
                    dve.wait_ge(s_silu, n + 1)
                    dve.wait_ge(s_pl, n + 2)
                    dve.tensor_tensor(PR[:, i % 2, 0:nt], SG[:, i % 2, 0:nt], PS[2 * (i % 2) + 1][:, 0:nt],
                                      ALU.mult).then_inc(s_prod, 1)
                    if opening and i == 0:
                        norm_apply(2, 2, lambda k: low_part(n, i, ft, o, nt) if k == 2 else None)
                    elif i < nsteps - 1:
                        low_part(n, i, ft, o, nt)
                    else:
                        final = n, i, ft, o, nt
                    if first and i in (1, 4):
                        ada_sums(it, i // 4, 32 * it + 32)
                place = 0 if first else 2
                at_next = place + 1
                for t in range(f["T"]):
                    s, t0, nt = f["blocks"][t]
                    xs = XC if s else X
                    b = t + 3 - f["T"]
                    for k in range(KT):
                        dve.wait_ge(s_y, f["y"] + 8 * f["T"] * it + 8 * t + k + 1)
                        xv = xs[:, k, t0:t0 + nt]
                        dve.scalar_tensor_tensor(xv, PS[down_bank(s, k)][:, 0:nt], GATE[:, place, k, s:s + 1], xv,
                                                 ALU.mult, ALU.add).then_inc(s_yd, 1)
                        if (t, k) == (0, 0):
                            low_part(*final)
                        if not last:
                            continue
                        lag = 3 if first else 2
                        if t == 0 and k >= lag:
                            add_square(at_next, b, k - lag)
                        if t == 1:
                            if k < lag:
                                add_square(at_next, b - 1, KT - lag + k)
                            if k == lag + 1:
                                norm_mean(at_next, b - 1)
                            if k == lag + 3:
                                norm_diagonal(at_next, b - 1)
                            if first and 4 <= k < 4 + DVE_SQUARES:
                                add_square(at_next, b, k - 4)
                            if k == 3 and not first:
                                add_square(at_next, b, 0)
                            if k >= 3 and not first:
                                add_square(at_next, b, k - 2)
                        if t == 2:
                            if k == 0:
                                dve.wait_ge(s_rb, J[1, 0] + 1)
                            else:
                                modulated(1, 0, k - 1)
                            scaled(1, 0, k)
                            if k == 5:
                                norm_mean(1, 1)
                            if k == 7:
                                norm_diagonal(1, 1)
                    if first and t == 0:
                        ada_pair_mods(it)

            with dve.Fori(0, NIT - 1) as it:
                ffn(FFN[0], it, PH1, PL1)
            gain(1)
            gain(2)
            dve.wait_ge(s_coef, 4)
            ffn(FFN[0], NIT - 1, PH1, PL1, last=True)
            modulated(1, 0, KT - 1)
            add_squares(1, 2)

            def unit_low(u):
                dve.wait_ge(s_hi, highs(u) + 1)
                dve.tensor_tensor(WL[:, u % 2], WR[:, u % 2], WH[:, u % 2].bitcast(F32),
                                  ALU.subtract).then_inc(s_lo[u % 2], 1)

            def context_keys(a):
                n = FILL["ck", a, 0]
                dve.wait_ge(s_fill, n + 1)
                for tb in range(2):
                    for hh in range(2):
                        for d in range(2):
                            h = 2 * a + hh
                            z = Z_CTX[d][tb]
                            ins = dve.tensor_scalar(KC[:, d, tb, h, :], PS[n][:, tb * UC + hh * P:tb * UC + hh * P + P],
                                                    Z[:, 4 * d + h, z:z + 1], K_SCALE, ALU.mult, ALU.mult)
                ins.then_inc(s_free[n], 1)

            def meanwhile(k):
                if k == 2:
                    norm_mean(1, 2)
                if k == 5:
                    norm_diagonal(1, 2)
                if k in (3, 7):
                    unit_low(U_MIX + 2 + k // 4)
                if k == 6:
                    context_keys(0)

            norm_apply(1, 1, meanwhile)
            norm_apply(1, 2, lambda k: unit_low(U_MIX + 4) if k == 1 else context_keys(1) if k == 4 else None)
            gate(1)
            dve.wait_ge(s_coef, 5)

            def masks():
                for h in range(HEADS):
                    dve.wait_ge(s_exp, 17 + 2 * h + 2)
                    link(dve.tensor_tensor(DM[:, h, :], DT[:, 0, :], CST[:, C_LOW:C_LOW + P], ALU.mult))
                    link(dve.tensor_tensor(DT[:, 0, :], DT[:, 1, :], CST[:, C_UP:C_UP + P], ALU.mult))
                    dve.tensor_tensor(DM[:, h, :], DM[:, h, :], DT[:, 0, :], ALU.add).then_inc(s_dec, 1)

            def read(*key):
                dve.wait_ge(*release(FILL[key]))

            def cat_low(b):
                cols = slice(b * TB, (b + 1) * TB)
                for k in range(1, KT, 2):
                    dve.wait_ge(s_cath, 8 * b + k + 1)
                    src = RET[:, k, cols] if k < 4 else GM[:, k - 4, cols]
                    dve.tensor_tensor(HL[:, k, cols], src, HH[:, k, cols].bitcast(F32),
                                      ALU.subtract).then_inc(s_catl[1], 1)

            n_rope = n_gate = 0
            for n, (i, name, a, b) in enumerate(FILLS):
                ps, free = PS[n % NRING], s_free[n % NRING]
                four = ps[:, :].rearrange("p (c t) -> p c t", c=4)
                cols = slice(b * TB, (b + 1) * TB)
                if name in ("k", "q", "score", "ub", "ysum", "yscale", "mixed", "out"):
                    dve.wait_ge(s_fill, n + 1)
                if (name, a) == ("ck", 1):
                    masks()
                    dve.wait_ge(s_rope, 32)
                    dve.wait_ge(s_hl, 8 * (J[1, 2] + 1))
                elif name in ("k", "q"):
                    dst = (KF if name == "k" else QF)[:, a % 2, cols]
                    tmp = TMP[:, 0, :]
                    scale = K_SCALE if name == "k" else 1.0
                    if n_rope:
                        dve.wait_ge(s_rope_done, n_rope)
                    dve.scalar_tensor_tensor(tmp[0:64], ps[64:P, :], scale, SIN[64:P, cols], ALU.mult, ALU.mult)
                    dve.scalar_tensor_tensor(tmp[64:P], ps[0:64, :], scale, SIN[0:64, cols], ALU.mult, ALU.mult)
                    dve.scalar_tensor_tensor(dst, ps[:, :], scale, COS[:, cols], ALU.mult, ALU.mult).then_inc(free, 1)
                    dve.wait_ge(*release(n))
                    dve.tensor_tensor(dst, dst, tmp, ALU.add).then_inc(s_rope_done, 1)
                    n_rope += 1
                elif name == "score":
                    dve.tensor_tensor(PM[:, 4 * b:4 * b + 4, :], four, DM[:, a, :].unsqueeze(1).to_broadcast([P, 4, P]),
                                      ALU.mult).then_inc(free, 1)
                elif (name, b) == ("ub", 1):
                    read("state0", 0, 0)
                    read("state0", 1, 0)
                    for step in range(NCH - 1):
                        for d in range(2):
                            c = step if d == 0 else NCH - 1 - step
                            bank = PS[FILL["uf" if d == 0 else "ub", a, c // 4] % NRING]
                            before = KZ[d][:, c, :]
                            if step == 0:
                                before = S0[:, d, a, :]
                            else:
                                dve.wait_ge(s_state, 14 * a + 2 * (step - 1) + d + 1)
                            z = Z[:, 4 * d + a, Z_CHUNK:Z_CHUNK + 1]
                            dve.scalar_tensor_tensor(KZ[d][:, c + 1 - 2 * d, :], before, z,
                                                     bank[:, (c % 4) * P:(c % 4 + 1) * P],
                                                     ALU.mult, ALU.add).then_inc(s_state, 1)
                elif name == "ysum":
                    dve.tensor_scalar(MS[:, 8:16], ps[:, 0:8], 1.0 / P, EPS, ALU.mult, ALU.add).then_inc(s_ym, 1)
                    dve.wait_ge(s_yr, a + 1)
                    for j, dg in enumerate((TMP[:, 1, :].rearrange("p (b t) -> p b t", b=4), DG2[:, :, :])):
                        if a:
                            dve.wait_ge(s_fill, FILL["yscale", a - 1, j] + 1)
                        diagonal(4, RS[:, 8 + 4 * j:12 + 4 * j], dg).then_inc(s_yg, 1)
                elif name == "yscale":
                    dve.wait_ge(s_oc, 2 * a + b + 1)
                    r = RET[:, a, cols]
                    dve.tensor_tensor(r, r, ps[:, :], ALU.mult).then_inc(free, 1)
                elif name == "g":
                    read("g", a, b)
                    r = RET[:, a, cols]
                    dve.tensor_tensor(r, r, GU[:, n_gate % 2, :], ALU.mult).then_inc(s_cat, 1)
                    n_gate += 1
                    if b == 0 and a in (1, 2):
                        u = U_MIX + MIX_ADA + a - 1
                        ada_sums(NIT, a - 1, 16 * (u // 2 + 1))
                elif name == "vg":
                    read("vg", a, b)
                    v = V2 if a else V
                    tiles = [(c, g) for c in (2 * b, 2 * b + 1) for g in range(2)]
                    for c, g in tiles:
                        ins = dve.bn_stats(BST[:, 2 * c + g, :], v[:, c, g * P:(g + 1) * P])
                    link(ins)
                    for c, g in tiles:
                        ins = dve.bn_aggr(MV[:, 2 * c + g, :], BST[:, 2 * c + g, :])
                    link(ins)
                    if b == 3:
                        dve.tensor_scalar(MS[:, 16:32], MV[:, :, 1], EPS, None, ALU.add).then_inc(s_lv, 1)
                        dve.wait_ge(s_lr, a + 1)
                        for c in range(NCH):
                            for g in range(2):
                                m = 2 * c + g
                                tile = v[:, c, g * P:(g + 1) * P]
                                ins = dve.tensor_scalar(tile, tile, MV[:, m, 0:1], RS[:, 16 + m:17 + m],
                                                        ALU.subtract, ALU.mult)
                        ins.then_inc(s_vn, 1)
                        if a == 0:
                            ada_pair_mods(NIT)
                            gate(2)
                            dve.wait_ge(s_coef, 6)
                elif name == "mixed":
                    dve.wait_ge(s_gw, 32)
                    m = n_gate % 2
                    dve.tensor_tensor(MIXD[:, m, :].rearrange("p (c t) -> p c t", c=4), four,
                                      BB[:, a, :].unsqueeze(1).to_broadcast([P, 4, P]), ALU.add).then_inc(s_mx, 1)
                    dve.wait_ge(*release(n))
                    read("u", a, b)
                    dve.tensor_tensor(GM[:, a, cols], MIXD[:, m, :], GU[:, m, :], ALU.mult).then_inc(s_cat, 1)
                    n_gate += 1
                    if (a, b) == (GROUPS - 1, 0):
                        cat_low(0)
                elif name == "out":
                    xv = X[:, b, a * TB:(a + 1) * TB]
                    dve.scalar_tensor_tensor(xv, ps[:, :], GATE[:, 1, b, 0:1], xv, ALU.mult, ALU.add).then_inc(free, 1)
                    m = n - FILL["out", 0, 0] - 1
                    if m >= 0:
                        add_square(2, 1 + m // 8, m % 8)
                    if (a, b) == (1, 1):
                        norm_mean(2, 1)
                        norm_diagonal(2, 1)
                    if (a, b) == (0, 1):
                        cat_low(1)
                    if (a, b) == (1, 2):
                        norm_apply(2, 1)
                    if n + 1 == FIRST_FILL[DVE_UNIT - 1]:
                        unit_low(mix_unit(DVE_UNIT))
            add_square(2, 2, KT - 1)
            norm_mean(2, 2)
            norm_diagonal(2, 2)
            ffn(FFN[1], 0, PH2, PL2, opening=True)
            with dve.Fori(1, NIT - 1) as it:
                ffn(FFN[1], it, PH2, PL2)
            ffn(FFN[1], NIT - 1, PH2, PL2, last=True)
            for k in range(KT - 2, KT):
                add_square(3, 2, k)
            norm_out(1, 0, 3)
            norm_mean(3, 2)
            norm_out(1, 3, 5)
            norm_diagonal(3, 2)
            norm_out(1, 5, KT)
            norm_out(2, 0, KT)

        @block.tensor
        def _(pe):
            def mm3(dst, wh, wl, xh, xl, first, last):
                pe.matmul(dst, wh, xh, start=first, stop=False)
                pe.matmul(dst, wh, xl, start=False, stop=False)
                return pe.matmul(dst, wl, xh, start=False, stop=last)

            def norm_sum(place, b):
                j, n, acc = J[place, b], BLOCKS[b][2], NB[place][1]
                pe.wait_ge(s_acc, 8 * (j + 1))
                if j:
                    pe.wait_ge(s_ms, j)
                for c in range(n // P):
                    ins = pe.matmul(ST_BANK[:, c:c + 1], acc[:, c * P:(c + 1) * P], ONES[:, 0:1], start=True, stop=True)
                ins.then_inc(s_st, 1)

            def norm_scale(place, b):
                j, n = J[place, b], BLOCKS[b][2]
                bank = scale_bank(place, b)
                pe.wait_ge(s_dg, j + 1)
                earlier = [i for i, key in enumerate(NORMS[:j]) if scale_bank(*key) is bank]
                if earlier:
                    pe.wait_ge(s_hf, 8 * (earlier[-1] + 1))
                pe.matmul(bank[:, 0:n], ONES[:, :], NB[place][2][:, 0:n // P, :], start=True, stop=True).then_inc(s_rb, 1)

            def first_columns(a):
                pe.wait_ge(s_rows, a + 1)
                for t in range(2):
                    ins = pe.matmul(PS[first_bank(a)][:, UC + 2 * t:UC + 2 * t + 2], ROWS[:, a % 2, t * P:(t + 1) * P],
                                    ID[0:2, 0:2], start=True, stop=True)
                ins.then_inc(s_col, 1)

            def ada_columns(it, used):
                for slot in range(2):
                    pe.wait_ge(s_lo[slot], used)
                pe.wait_ge(s_mods, ADA_FIRST + it)
                for c in range(8):
                    slot, t, v = c // 4, c // 2 % 2, c % 2
                    ins = pe.matmul(PS[6][:, c:c + 1], AS[:, slot, v, t * P:(t + 1) * P], ONES[:, 0:1], start=True, stop=True)
                ins.then_inc(s_col, 1)

            def first_product(a):
                pe.wait_ge(s_first[a % 3], 16 * (a // 3 + 1))
                if a >= 4:
                    pe.wait_ge(s_mods, a - 3)
                for k in range(KT):
                    ins = pe.matmul(PS[first_bank(a)][0:2, 0:UC], CS[:, k, :], WS[:, a % 3, k, :], start=(k == 0), stop=(k == KT - 1))
                ins.then_inc(s_ada, 1)

            pe.wait_ge(s_cs, 1)
            first_product(0)
            pe.wait_ge(s_const, 16 * 6)
            first_product(1)
            first_columns(0)
            norm_sum(0, 0)
            for a in (2, 3, 4):
                first_product(a)
                first_columns(a - 1)
                if a == 2:
                    norm_scale(0, 0)
            norm_sum(0, 1)
            for a in (5, 6, 7):
                first_product(a)
                first_columns(a - 1)
            first_columns(7)
            norm_sum(0, 2)
            first_product(8)
            first_product(9)
            norm_scale(0, 1)
            first_columns(8)
            first_columns(9)
            norm_scale(0, 2)
            first_product(10)
            first_product(11)
            first_columns(10)
            first_columns(11)
            pe.wait_ge(s_mods, ADA_FIRST)

            def ffn(f, it, ph, pl, w2h, w2l, last=False, opening=False):
                T, first = f["T"], f["per"] == 4
                order = steps(f, opening)
                for i, (ft, t) in enumerate(order):
                    n = f["step"] + 2 * T * it + i
                    s, t0, nt = f["blocks"][t]
                    xh, xl = (HCH, HCL) if s else (HH, HL)
                    if t == 0:
                        pe.wait_ge(s_lo[ft], f["unit"] // 2 + (f["per"] // 2) * it + 1)
                    j = J[0 if first else 2, t + 3 - T]
                    by_tile = opening and (ft, t) == (0, 1)
                    if not by_tile:
                        pe.wait_ge(s_hl, 8 * (j + 1))
                    pe.wait_ge(s_prod, n + 1)
                    if opening and i < 2:
                        for b in (2 * i, 2 * i + 1):
                            pe.wait_ge(*last_release(b))
                    for half in range(2):
                        for k in range(KT):
                            if by_tile and half == 0:
                                pe.wait_ge(s_hl, 8 * j + k + 1)
                            cols = slice(half * P, (half + 1) * P)
                            ins = mm3(PS[2 * (i % 2) + half][:, 0:nt], WH[:, ft, k, cols], WL[:, ft, k, cols],
                                      xh[:, k, t0:t0 + nt], xl[:, k, t0:t0 + nt], k == 0, k == KT - 1)
                        if half:
                            ins.then_inc(s_gu, 1)
                        if opening and i == 0:
                            (norm_scale if half else norm_sum)(2, 2)
                if opening:
                    for b in (4, 5):
                        pe.wait_ge(*last_release(b))
                for t in range(T):
                    s, t0, nt = f["blocks"][t]
                    b = t + 3 - T
                    o = SEQ if s else t0
                    pe.wait_ge(s_pl, f["step"] + 2 * T * it + order.index((1, t)) + 3)
                    pe.wait_ge(s_w2lo, f["v"] + 2 * it + 3)
                    for d in range(KT):
                        base = f["y"] + 8 * T * it + 8 * t
                        if s and d in (2, 3):
                            pe.wait_ge(s_prod, f["step"] + 2 * T * it + 2 * T + 1)
                        else:
                            pe.wait_ge(s_yd, base + d + (-1 if s and d >= 4 else 1))
                        for ft in range(2):
                            cols = slice(d * P, (d + 1) * P)
                            ins = mm3(PS[down_bank(s, d)][:, 0:nt], w2h[:, ft, cols], w2l[:, ft, cols],
                                      ph[:, ft, o:o + nt], pl[:, ft, o:o + nt], ft == 0, ft == 1)
                        ins.then_inc(s_y, 1)
                        if last and (t, d) == (1, 3 if first else 2):
                            norm_sum(1 if first else 3, b - 1)
                        if last and (t, d) == (1, 7 if first else 6):
                            pe.wait_ge(s_prod, f["step"] + 2 * T * NIT + 2)
                            norm_scale(1 if first else 3, b - 1)
                        if last and (t, d) == (2, 4):
                            norm_sum(1, 1)
                    if first and t == 0:
                        ada_columns(it, 2 * it + 2)

            with pe.Fori(0, NIT - 1) as it:
                ffn(FFN[0], it, PH1, PL1, W2H1, W2L1)
            ffn(FFN[0], NIT - 1, PH1, PL1, W2H1, W2L1, last=True)

            norm_scale(1, 1)

            for n, (i, name, a, b) in enumerate(FILLS):
                ps = PS[n % NRING]
                slot = i % 2
                wh, wl = WH[:, slot], WL[:, slot]
                if n == FIRST_FILL[i]:
                    pe.wait_ge(s_lo[slot], mix_unit(i) // 2 + 1)
                if n >= NRING:
                    pe.wait_ge(*release(n - NRING))
                elif n >= 4:
                    pe.wait_ge(s_yd, y_all[0])
                cols = slice(b * TB, (b + 1) * TB)
                hh = a % 2
                if name in ("ck", "cv"):
                    pe.wait_ge(s_hl, 8 * (J[1, 0] + 1))
                    for tb in range(2):
                        for k in range(KT):
                            t = slice(tb * P, (tb + 1) * P)
                            ins = mm3(ps[:, tb * UC:(tb + 1) * UC], HCH[:, k, t], HCL[:, k, t],
                                      wh[:, k, :], wl[:, k, :], k == 0, k == KT - 1)
                elif name == "state0":
                    for key in (("ck", 0, 0), ("ck", 1, 0), ("cv", 0, 0), ("cv", 1, 0)):
                        pe.wait_ge(*release(FILL[key]))
                    for h in range(HEADS):
                        for tb in range(2):
                            ins = pe.matmul(ps[:, h * P:(h + 1) * P], KC[:, a, tb, h, :],
                                            VC[:, tb, h * P:(h + 1) * P], start=(tb == 0), stop=(tb == 1))
                elif name in ("v", "vg"):
                    for c in range(2):
                        for k in range(KT):
                            t = slice((2 * b + c) * P, (2 * b + c + 1) * P)
                            ins = mm3(ps[:, c * UC:(c + 1) * UC], HH[:, k, t], HL[:, k, t],
                                      wh[:, k, :], wl[:, k, :], k == 0, k == KT - 1)
                elif name in ("k", "q", "g", "u"):
                    pe.wait_ge(s_hl, 8 * (J[1, b + 1] + 1))
                    for k in range(KT):
                        w = slice((a % 2) * P, (a % 2 + 1) * P)
                        ins = mm3(ps[:, :], wh[:, k, w], wl[:, k, w], HH[:, k, cols], HL[:, k, cols],
                                  k == 0, k == KT - 1)
                elif name == "mixed":
                    pe.wait_ge(s_vn, a // 2 + 1)
                    pe.wait_ge(s_gw, 32)
                    v = V2 if a // 2 else V
                    for c in range(4):
                        ins = pe.matmul(ps[:, c * P:(c + 1) * P], v[:, 4 * b + c, hh * P:(hh + 1) * P], WST[:, a, :],
                                        start=True, stop=True)
                elif name == "kt":
                    pe.wait_ge(s_rope_done, 8 * (a // 2 + 1))
                    for c in range(4):
                        t0 = (4 * b + c) * P
                        ins = pe.transpose(ps[:, c * P:(c + 1) * P], KF[:, hh, t0:t0 + P], ID[:, :])
                elif name == "score":
                    for c in range(4):
                        t0 = (4 * b + c) * P
                        ins = pe.matmul(ps[:, c * P:(c + 1) * P], KF[:, hh, t0:t0 + P], QF[:, hh, t0:t0 + P],
                                        start=True, stop=True)
                elif name in ("uf", "ub"):
                    for j in range(4):
                        pe.wait_ge(*release(FILL["v", a // 2, j]))
                    for j in range(2):
                        pe.wait_ge(*release(FILL["kt", a, j]))
                    for c in range(4):
                        m = 4 * b + c
                        ins = pe.matmul(ps[:, c * P:(c + 1) * P], KZ[name == "ub"][:, m, :], V[:, m, hh * P:(hh + 1) * P],
                                        start=True, stop=True)
                elif name == "o":
                    pe.wait_ge(*release(FILL["score", a, b]))
                    chunks = [(c, 4 * b + c, ps[:, c * P:(c + 1) * P]) for c in range(4)]
                    for c, m, dst in chunks:
                        pe.matmul(dst, V[:, m, hh * P:(hh + 1) * P], PM[:, m, :], start=(c == 0), stop=False,
                                  skip_group_check=True)
                    pe.wait_ge(s_q, 2 * a + 1)
                    for c, m, dst in chunks:
                        if m:
                            pe.wait_ge(s_state, 14 * a + 2 * (m - 1) + 1)
                        pe.matmul(dst, KZ[0][:, m, :] if m else S0[:, 0, a, :], RET[:, a, m * P:(m + 1) * P],
                                  start=False, stop=False, skip_group_check=True)
                    pe.wait_ge(s_q, 2 * a + 2)
                    for c, m, dst in reversed(chunks):
                        last = m == NCH - 1
                        if not last:
                            pe.wait_ge(s_state, 14 * a + 2 * (NCH - 2 - m) + 2)
                        ins = pe.matmul(dst, S0[:, 1, a, :] if last else KZ[1][:, m, :], QF[:, hh, m * P:(m + 1) * P],
                                        start=False, stop=True, skip_group_check=True)
                elif name == "ysum":
                    for j in range(2):
                        pe.wait_ge(*release(FILL["o", a, j]))
                    for c in range(NCH):
                        ins = pe.matmul(ps[:, c:c + 1], KF[:, hh, c * P:(c + 1) * P], ONES[:, 0:1], start=True, stop=True)
                elif name == "yscale":
                    pe.wait_ge(s_yg, 2 * a + b + 1)
                    ins = pe.matmul(ps[:, :], ONES[:, :], DG2[:, :, :] if b else TMP[:, 1, :], start=True, stop=True)
                elif name == "out":
                    for k in range(KT):
                        pe.wait_ge(s_catl[k % 2], 4 * a + k // 2 + 1)
                        w = slice(b % 2 * P, (b % 2 + 1) * P)
                        ins = mm3(ps[:, :], wh[:, k, w], wl[:, k, w], HH[:, k, a * TB:(a + 1) * TB],
                                  HL[:, k, a * TB:(a + 1) * TB], k == 0, k == KT - 1)
                ins.then_inc(s_fill, 1)
                if n in (0, 2):
                    (norm_scale if n else norm_sum)(1, 2)
                if (name, a, b) == ("g", 3, 1):
                    ada_columns(NIT, (U_MIX + MIX_ADA) // 2 + 1)
                if (name, a, b) == ("out", 1, 1):
                    norm_sum(2, 1)
                if (name, a, b) == ("out", 1, 2):
                    norm_scale(2, 1)

            ffn(FFN[1], 0, PH2, PL2, W2H2, W2L2, opening=True)
            with pe.Fori(1, NIT - 1) as it:
                ffn(FFN[1], it, PH2, PL2, W2H2, W2L2)
            ffn(FFN[1], NIT - 1, PH2, PL2, W2H2, W2L2, last=True)
            norm_sum(3, 2)
            norm_scale(3, 2)


def _units(w):
    return w.reshape(KT, P, -1, UC).transpose(2, 1, 0, 3)


def _w1_units(w):
    return w.reshape(KT, P, 2, NF, P).transpose(3, 1, 0, 2, 4).reshape(NF, P, KT, UC)


def _per_feature(v):
    return np.moveaxis(v.reshape(v.shape[:-1] + (-1, P)), -1, 0)


def _tables():
    token = np.arange(SEQ)
    nf = P // 4
    freqs = (np.float32(10000.0) ** (-np.arange(nf, dtype=np.float32) / np.float32(nf))).astype(np.float32)
    row, col = (token // GRID_W).astype(np.float32), (token % GRID_W).astype(np.float32)
    ang = np.concatenate([freqs[:, None] * row, freqs[:, None] * col]).astype(np.float32)
    cosine = np.cos(ang, dtype=np.float32)
    sine = np.sin(ang, dtype=np.float32)
    i, j = np.arange(P)[None, :], np.arange(P)[:, None]
    c = np.zeros((P, C_END), np.float32)
    powers = np.zeros((P, Z_END), np.float32)
    c[:, C_ABS:C_ABS + P] = abs(i - j)
    c[:, C_LOW:C_LOW + P] = i >= j
    c[:, C_UP:C_UP + P] = i <= j
    c[:, C_XIF:C_XIF + P] = i + 1
    c[:, C_XIB:C_XIB + P] = CHUNK - i
    p = np.arange(P)
    for n, v in enumerate((CHUNK - 1 - p, p, CTX - 1 - p, CTX - 1 - P - p, p, P + p, CHUNK + 0 * p)):
        powers[:, n] = v
    return (np.concatenate([cosine, cosine]), np.concatenate([sine, -sine]), c, powers, np.eye(P, dtype=np.float32))


def kernel(x, c, ctx, c_ctx, w_ada, b_ada, norm_g, ffn1_w1, ffn1_w2, w_in, ret_decay,
           gmlp_ws, gmlp_bs, w_out, ffn2_w1, ffn2_w2, final_g):
    import concourse.bacc as bacc
    from concourse.bass_utils import run_bass_kernel_spmd

    a = lambda v: np.asarray(v)
    ada, win, wout = _units(a(w_ada)[0]), _units(a(w_in)[0]), _units(a(w_out)[0])
    f1, f2 = _w1_units(a(ffn1_w1)[0]), _w1_units(a(ffn2_w1)[0])
    stream = []
    for i in range(NIT):
        n = ADA_FIRST + 2 * i
        stream += [f1[2 * i:2 * i + 2], ada[n:n + 2]]
    for i, (kind, part, p) in enumerate(MIX_UNITS):
        if i == MIX_ADA:
            stream.append(ada[N_ADA - 2:])
        n = p if kind == "out" else WIN[part[1:] if kind == "ctx" else part] + p
        stream.append((wout if kind == "out" else win)[n:n + 1])
    stream.append(f2)
    cosine, sine, consts, powers, ident = _tables()
    arrays = {
        "x": a(x)[0].T, "ctx": a(ctx)[0].T,
        "c2": np.stack([_per_feature(a(c)[0]), _per_feature(a(c_ctx))], axis=-1),
        "ada_units": ada[:ADA_FIRST],
        "w_units": np.concatenate(stream),
        "w2_units": np.concatenate([a(ffn1_w2)[0].reshape(NF, P, D), a(ffn2_w2)[0].reshape(NF, P, D)]),
        "b_ada": np.repeat(_per_feature(a(b_ada)[0])[..., None], 2, axis=-1),
        "norm_g": _per_feature(a(norm_g)[0]), "final_g": _per_feature(a(final_g)),
        "decay": np.broadcast_to(a(ret_decay)[0].reshape(1, 8), (P, 8)),
        "ws": a(gmlp_ws)[0].transpose(2, 0, 1),
        "bs": np.broadcast_to(a(gmlp_bs)[0][None], (P, GROUPS, CHUNK)),
        "cosine": cosine, "sine": sine, "consts": consts, "powers": powers, "ident": ident,
    }
    arrays = {k: np.ascontiguousarray(v) for k, v in arrays.items()}
    nc = bacc.Bacc("TRN2", target_bir_lowering=False, num_devices=1, dynamic_dma_scratch_size=64)
    args = [nc.dram_tensor(k, v.shape, mybir.dt.from_np(v.dtype), kind="ExternalInput").ap()
            for k, v in arrays.items()]
    out = nc.dram_tensor("out", (D, SEQ), F32, kind="ExternalOutput").ap()
    layer(nc, *args, out)
    r = run_bass_kernel_spmd(nc, [arrays], core_ids=[0])
    return np.ascontiguousarray(r.results[0]["out"].T)[None]
```
